# Optimizing a Trainium2 kernel written in Bass

```python
import jax, jax.numpy as jnp
from jax import lax
import numpy as np

D_MODEL = 1024
BATCH = 1
SEQ = 256
DEPTH = 1

M_HEADS = 4
M_DQK = 128
M_DV = 128
M_CHUNK = 64
CONV_W = 4
F_HEADS = 8
F_DH = 64
Q_BLOCK = 128
N_EXPERTS = 32
TOP_K = 4
D_FF = D_MODEL
SWIGLU_ALPHA = 1.702
SWIGLU_LIMIT = 7.0
MOE_BLOCK = 256
DN_ALPHA = (2.0 * DEPTH) ** 0.25
DN_BETA = (8.0 * DEPTH) ** -0.25
LN_EPS = 1e-5

M_W = M_HEADS * M_DV
F_W = F_HEADS * F_DH
MQK_W = 2 * M_HEADS * M_DQK
MQK_OFF = 0
MV_OFF = MQK_OFF + MQK_W
MO_OFF = MV_OFF + M_W
MI_OFF = MO_OFF + M_W
MF_OFF = MI_OFF + M_HEADS
FQ_OFF = MF_OFF + M_HEADS
FK_OFF = FQ_OFF + F_W
FV_OFF = FK_OFF + F_W
FF_OFF = FV_OFF + F_W
GM_OFF = FF_OFF + F_HEADS
GF_OFF = GM_OFF + D_MODEL
IN_COLS = GF_OFF + D_MODEL
SPLIT_IDX = (MV_OFF, MO_OFF, MI_OFF, MF_OFF, FQ_OFF, FK_OFF, FV_OFF, FF_OFF, GM_OFF, GF_OFF)

kernel_name = "hybrid_mlstm_fox_moe_deepnorm"

def layer_norm(x, g, b):
    xf = x.astype(jnp.float32)
    mu = jnp.mean(xf, -1, keepdims=True)
    var = jnp.mean(jnp.square(xf - mu), -1, keepdims=True)
    return ((xf - mu) * lax.rsqrt(var + LN_EPS)).astype(x.dtype) * g + b

def head_layer_norm(h):
    mu = jnp.mean(h, -1, keepdims=True)
    var = jnp.mean(jnp.square(h - mu), -1, keepdims=True)
    return (h - mu) * lax.rsqrt(var + LN_EPS)

def causal_depthwise_conv(u, w, b):
    c = u.shape[-1]
    y = lax.conv_general_dilated(u, w[:, None, :].astype(u.dtype), window_strides=(1,),
                                 padding=[(CONV_W - 1, 0)],
                                 dimension_numbers=("NWC", "WIO", "NWC"),
                                 feature_group_count=c)
    return y + b

def to_heads(t, n_heads):
    bsz, s, _ = t.shape
    return t.reshape(bsz, s, n_heads, -1).transpose(0, 2, 1, 3)

def mlstm_chunkwise(q, k, v, i_pre, logf):
    f32 = jnp.float32
    q, k, v = q.astype(f32), k.astype(f32), v.astype(f32)
    i_pre, logf = i_pre.astype(f32), logf.astype(f32)
    bsz, nh, s, dk = q.shape
    dv = v.shape[-1]
    L = M_CHUNK
    n = s // L
    q = q.reshape(bsz, nh, n, L, dk)
    k = k.reshape(bsz, nh, n, L, dk)
    v = v.reshape(bsz, nh, n, L, dv)
    i_pre = i_pre.reshape(bsz, nh, n, L)
    logf = logf.reshape(bsz, nh, n, L)

    b = jnp.cumsum(logf, axis=-1)
    g = b[..., -1]
    a = g[..., None] - b + i_pre
    m_loc = jnp.max(a, axis=-1)
    causal = jnp.tril(jnp.ones((L, L), dtype=bool))
    dlog = jnp.where(causal, b[..., :, None] - b[..., None, :] + i_pre[..., None, :], -jnp.inf)

    def step(carry, xs):
        c_st, n_st, m_st = carry
        k_c, v_c, a_c, g_c, ml_c = xs
        m_new = jnp.maximum(g_c + m_st, ml_c)
        decay = jnp.exp(g_c + m_st - m_new)
        w = jnp.exp(a_c - m_new[..., None])
        c_new = decay[..., None, None] * c_st + jnp.einsum('bhl,bhlk,bhlv->bhkv', w, k_c, v_c)
        n_new = decay[..., None] * n_st + jnp.einsum('bhl,bhlk->bhk', w, k_c)
        return (c_new, n_new, m_new), (c_st, n_st, m_st)

    init = (jnp.zeros((bsz, nh, dk, dv), f32), jnp.zeros((bsz, nh, dk), f32), jnp.zeros((bsz, nh), f32))
    xs = (jnp.moveaxis(k, 2, 0), jnp.moveaxis(v, 2, 0), jnp.moveaxis(a, 2, 0),
          jnp.moveaxis(g, 2, 0), jnp.moveaxis(m_loc, 2, 0))
    _, (c_prev, n_prev, m_prev) = lax.scan(step, init, xs)
    c_prev = jnp.moveaxis(c_prev, 0, 2)
    n_prev = jnp.moveaxis(n_prev, 0, 2)
    m_prev = jnp.moveaxis(m_prev, 0, 2)

    inter_log = b + m_prev[..., None]
    m_t = jnp.maximum(inter_log, jnp.max(dlog, axis=-1))
    w_inter = jnp.exp(inter_log - m_t)
    w_intra = jnp.exp(dlog - m_t[..., None])
    qk = jnp.einsum('bhntd,bhnsd->bhnts', q, k) * w_intra
    num = (w_inter[..., None] * jnp.einsum('bhntk,bhnkv->bhntv', q, c_prev)
           + jnp.einsum('bhnts,bhnsv->bhntv', qk, v))
    den = w_inter * jnp.einsum('bhntk,bhnk->bhnt', q, n_prev) + jnp.sum(qk, axis=-1)
    h = num / jnp.maximum(jnp.abs(den), jnp.exp(-m_t))[..., None]
    return h.reshape(bsz, nh, s, dv)

def forgetting_attention(q, k, v, logf):
    f32 = jnp.float32
    s_len = q.shape[2]
    scale = q.shape[-1] ** -0.5
    c = jnp.cumsum(logf.astype(f32), axis=-1)
    outs = []
    for blk in range(s_len // Q_BLOCK):
        q0 = blk * Q_BLOCK
        q1 = q0 + Q_BLOCK
        sc = jnp.einsum('bhtd,bhsd->bhts', q[:, :, q0:q1], k[:, :, :q1],
                        preferred_element_type=f32) * scale
        sc = sc + c[:, :, q0:q1, None] - c[:, :, None, :q1]
        mask = (q0 + jnp.arange(Q_BLOCK))[:, None] >= jnp.arange(q1)[None, :]
        p = jax.nn.softmax(jnp.where(mask, sc, -jnp.inf), axis=-1)
        outs.append(jnp.einsum('bhts,bhsd->bhtd', p.astype(v.dtype), v[:, :, :q1]))
    return jnp.concatenate(outs, axis=2)

def hybrid_mixer(h, w_in, b_in, m_conv_w, m_conv_b, m_norm_g, w_bm, w_bf, w_o):
    bsz, s, _ = h.shape
    proj = jnp.einsum('bsd,dc->bsc', h, w_in) + b_in
    mqk, mv, mo, mi, mf, fq, fk, fv, ff, gm, gf = jnp.split(proj, SPLIT_IDX, axis=-1)

    mqk = jax.nn.silu(causal_depthwise_conv(mqk, m_conv_w, m_conv_b))
    mq, mk = jnp.split(mqk, 2, axis=-1)
    hm = mlstm_chunkwise(to_heads(mq, M_HEADS), to_heads(mk, M_HEADS) * (M_DQK ** -0.5),
                         to_heads(mv, M_HEADS),
                         mi.astype(jnp.float32).transpose(0, 2, 1),
                         jax.nn.log_sigmoid(mf.astype(jnp.float32)).transpose(0, 2, 1))
    hm = head_layer_norm(hm).transpose(0, 2, 1, 3).reshape(bsz, s, M_W).astype(h.dtype) * m_norm_g
    hm = jax.nn.sigmoid(mo) * hm

    hf = forgetting_attention(to_heads(fq, F_HEADS), to_heads(fk, F_HEADS), to_heads(fv, F_HEADS),
                              jax.nn.log_sigmoid(ff.astype(jnp.float32)).transpose(0, 2, 1))
    hf = hf.transpose(0, 2, 1, 3).reshape(bsz, s, F_W)

    y = jax.nn.sigmoid(gm) * (hm @ w_bm) + jax.nn.sigmoid(gf) * (hf @ w_bf)
    return y @ w_o

def moe_ffn(h, w_router, b_router, w_gu, b_gu, w_dn, b_dn):
    bsz, s, d = h.shape
    t = bsz * s
    xt = h.reshape(t, d)
    logits = (xt @ w_router + b_router).astype(jnp.float32)
    top_v, top_e = lax.top_k(logits, TOP_K)
    gate = jax.nn.softmax(top_v, axis=-1)

    n_assign = t * TOP_K
    e_flat = top_e.reshape(n_assign).astype(jnp.int32)
    tok_flat = jnp.repeat(jnp.arange(t, dtype=jnp.int32), TOP_K)
    g_flat = gate.reshape(n_assign)
    order = jnp.argsort(e_flat)
    e_sorted = e_flat[order]
    counts = jnp.bincount(e_flat, length=N_EXPERTS).astype(jnp.int32)
    start = jnp.cumsum(counts) - counts
    padded = ((counts + MOE_BLOCK - 1) // MOE_BLOCK) * MOE_BLOCK
    pad_end = jnp.cumsum(padded)
    pad_start = pad_end - padded
    dest = pad_start[e_sorted] + (jnp.arange(n_assign, dtype=jnp.int32) - start[e_sorted])
    n_blocks = -(-n_assign // MOE_BLOCK) + N_EXPERTS
    n_rows = n_blocks * MOE_BLOCK
    row_tok = jnp.full((n_rows,), t, jnp.int32).at[dest].set(tok_flat[order])
    row_gate = jnp.zeros((n_rows,), jnp.float32).at[dest].set(g_flat[order])
    block_e = jnp.minimum(jnp.searchsorted(pad_end, jnp.arange(n_blocks, dtype=jnp.int32) * MOE_BLOCK,
                                           side='right'), N_EXPERTS - 1)

    def expert_block(args):
        tok_b, e = args
        xb = xt[jnp.minimum(tok_b, t - 1)]
        gu = xb @ w_gu[e] + b_gu[e]
        x_glu, x_lin = jnp.split(gu, 2, axis=-1)
        x_glu = jnp.minimum(x_glu, SWIGLU_LIMIT)
        x_lin = jnp.clip(x_lin, -SWIGLU_LIMIT, SWIGLU_LIMIT)
        act = x_glu * jax.nn.sigmoid(SWIGLU_ALPHA * x_glu) * (x_lin + 1.0)
        return act @ w_dn[e] + b_dn[e]

    y_rows = lax.map(expert_block, (row_tok.reshape(n_blocks, MOE_BLOCK), block_e)).reshape(n_rows, d)
    y = jax.ops.segment_sum(y_rows * row_gate[:, None].astype(y_rows.dtype), row_tok, num_segments=t)
    return y.reshape(bsz, s, d)

def setup_inputs(seed: int = 0) -> dict:
    key = jax.random.key(seed)
    ks = jax.random.split(key, 20)
    L, D, E, F = DEPTH, D_MODEL, N_EXPERTS, D_FF

    def nrm(k, shape, scale):
        return jax.random.normal(k, shape, jnp.float32) * scale

    col_scale = np.ones((IN_COLS,), np.float32)
    col_scale[MV_OFF:MV_OFF + M_W] = DN_BETA
    col_scale[FV_OFF:FV_OFF + F_W] = DN_BETA
    b_off = np.zeros((IN_COLS,), np.float32)
    b_off[MF_OFF:MF_OFF + M_HEADS] = np.linspace(3.0, 6.0, M_HEADS)
    b_off[FF_OFF:FF_OFF + F_HEADS] = np.linspace(1.0, 5.0, F_HEADS)

    x = nrm(ks[0], (BATCH, SEQ, D), 1.0)
    w_in = nrm(ks[1], (L, D, IN_COLS), D ** -0.5) * jnp.asarray(col_scale)
    b_in = nrm(ks[2], (L, IN_COLS), 0.02) + jnp.asarray(b_off)
    m_conv_w = nrm(ks[3], (L, CONV_W, MQK_W), CONV_W ** -0.5)
    m_conv_b = nrm(ks[4], (L, MQK_W), 0.02)
    m_norm_g = 1.0 + nrm(ks[5], (L, M_W), 0.02)
    w_bm = nrm(ks[6], (L, M_W, D), DN_BETA * M_W ** -0.5)
    w_bf = nrm(ks[7], (L, F_W, D), DN_BETA * F_W ** -0.5)
    w_o = nrm(ks[8], (L, D, D), DN_BETA * D ** -0.5)
    ln1_g = 1.0 + nrm(ks[9], (L, D), 0.02)
    ln1_b = nrm(ks[10], (L, D), 0.02)
    w_router = nrm(ks[11], (L, D, E), D ** -0.5)
    b_router = nrm(ks[12], (L, E), 0.01)
    w_gu = nrm(ks[13], (L, E, D, 2 * F), DN_BETA * D ** -0.5)
    b_gu = nrm(ks[14], (L, E, 2 * F), 0.02)
    w_dn = nrm(ks[15], (L, E, F, D), DN_BETA * F ** -0.5)
    b_dn = nrm(ks[16], (L, E, D), 0.02)
    ln2_g = 1.0 + nrm(ks[17], (L, D), 0.02)
    ln2_b = nrm(ks[18], (L, D), 0.02)
    return {"x": x, "w_in": w_in, "b_in": b_in, "m_conv_w": m_conv_w, "m_conv_b": m_conv_b,
            "m_norm_g": m_norm_g, "w_bm": w_bm, "w_bf": w_bf, "w_o": w_o,
            "ln1_g": ln1_g, "ln1_b": ln1_b, "w_router": w_router, "b_router": b_router,
            "w_gu": w_gu, "b_gu": b_gu, "w_dn": w_dn, "b_dn": b_dn,
            "ln2_g": ln2_g, "ln2_b": ln2_b}

def reference(x, w_in, b_in, m_conv_w, m_conv_b, m_norm_g, w_bm, w_bf, w_o, ln1_g, ln1_b,
              w_router, b_router, w_gu, b_gu, w_dn, b_dn, ln2_g, ln2_b):
    h = x
    for l in range(DEPTH):
        mix = hybrid_mixer(h, w_in[l], b_in[l], m_conv_w[l], m_conv_b[l], m_norm_g[l],
                           w_bm[l], w_bf[l], w_o[l])
        h = layer_norm(DN_ALPHA * h + mix, ln1_g[l], ln1_b[l])
        ffn = moe_ffn(h, w_router[l], b_router[l], w_gu[l], b_gu[l], w_dn[l], b_dn[l])
        h = layer_norm(DN_ALPHA * h + ffn, ln2_g[l], ln2_b[l])
    return h


_drawn_inputs = setup_inputs


def setup_inputs(seed=0):
    import zlib

    import numpy as np

    out = dict(_drawn_inputs(seed))
    spreads = {}
    factors = {'m_conv_b': 8.0,
     'm_norm_g': 31.057,
     'b_router': 6.943,
     'b_gu': 8.0,
     'b_dn': 6.31,
     'ln2_g': 23.808,
     'ln2_b': 24.01,
     'w_bf': 3.361}
    for name, (base, spread) in spreads.items():
        noise = np.random.default_rng([zlib.crc32(name.encode()), seed]).standard_normal(out[name].shape)
        drawn = base * np.exp(spread * noise) if base else spread * noise
        out[name] = __import__('jax').numpy.asarray(drawn.astype(out[name].dtype))
    for name, factor in factors.items():
        out[name] = (out[name] * factor).astype(out[name].dtype)
    return out
```

```python
from contextlib import ExitStack

import concourse.bass as bass
from concourse import mybir

F32 = mybir.dt.float32
BF16 = mybir.dt.bfloat16
I32 = mybir.dt.int32
U32 = mybir.dt.uint32
ALU = mybir.AluOpType
ACT = mybir.ActivationFunctionType
AX = mybir.AxisListType

P = 128
D = 1024
T = 256
TT = T // P
KC = D // P
M_HEADS, M_D = 4, 128
F_HEADS, F_D = 8, 64
CONV_W = 4
E = 32
TOP_K = 4
D_FF = 1024
SLOTS = 64
MAX_ITEMS = T * TOP_K // SLOTS + E - 1
ITEMS = MAX_ITEMS + 1
ALPHA = 2.0 ** 0.25
LN_EPS = 1e-5
SW_ALPHA, SW_LIMIT = 1.702, 7.0
NEG = -1e30
MQK, MV, MO, MI, MF, FQ, FK, FV, FF, GM, GF = 0, 1024, 1536, 2048, 2052, 2056, 2568, 3080, 3592, 3600, 4624

GROUPS = [MQK, MQK + 512, MV, FQ, FK, FV, MO, GM, GM + 512, GF, GF + 512]
TOKEN_MAJOR = {2, 5}
REGION = [0, 1, 2, 3, 4, 5, 0, 1, 2, 3, 0, 4, 5, 1, 2]
W_BM, W_BF, W_O0, W_O1 = 11, 12, 13, 14
REGIONS = 6
RWORDS = KC * 512
ARENA = 21660
SLOT_WORDS = 2 * D_FF
RING = 2 * REGIONS
GU_SLOTS = KC

UNITS = [(1, [2 * u, 2 * u + 1]) for u in range(4)] + [(0, [0, 1, 2, 3]), (0, [4, 5, 6, 7])]

STEPS = [
    ["S0"], ["S1"], ["T0", "S2"], ["T1", "S3"], ["T2", "S4"], ["T3", "S5"], ["T4", "B0"], ["T5", "B1"],
    ["N0", "V0"], ["B2", "V1"], ["N1", "V2"], ["B3", "V3"], ["N2"], ["N3"], [], [], [], [], [], [],
]

PARAM_ROWS = dict(mqk=0, mo=8, fq=12, fk=16, gm=20, gf=28, cw=36, cb=68, ng=76)
N_PARAM = 80


def build(nc, x, w_in, b_in, m_conv_w, m_conv_b, m_norm_g, w_bm, w_bf, w_o, ln1_g, ln1_b,
          w_router, b_router, w_gu, b_gu, w_dn, b_dn, ln2_g, ln2_b, out):
    with ExitStack() as ctx:
        def sb(name, shape, dt=F32):
            return ctx.enter_context(nc.sbuf_tensor(name, shape, dt))

        def sem(name):
            return ctx.enter_context(nc.semaphore(name))

        bank = [ctx.enter_context(nc.psum_tensor(f"bank{b}", [P, 512], F32)) for b in range(8)]

        ring = sb("ring", [P, REGIONS * RWORDS])

        def region(n):
            r = REGION[n]
            return ring[:, r * RWORDS:(r + 1) * RWORDS]

        wblk = [region(n).rearrange("p (c n) -> p c n", n=512) for n in range(11)]
        wbm_sb = region(W_BM).rearrange("p (c n) -> p c n", n=D)
        wbf_sb = region(W_BF).rearrange("p (c n) -> p c n", n=D)
        wo_sb = [region(n).rearrange("p (c n) -> p c n", n=512) for n in (W_O0, W_O1)]
        slot = [ring[:, k * SLOT_WORDS:(k + 1) * SLOT_WORDS] for k in range(RING)]
        bias_raw = ring[0:96, 5 * RWORDS:5 * RWORDS + 3 * D]

        h = sb("h", [P, TT, D])
        hT = sb("hT", [P, KC, T])
        bias3 = sb("bias3", [96, 3 * D], BF16)
        ident = sb("ident", [P, P])
        aident = sb("aident", [P, P])
        maskT = sb("maskT", [P, P], BF16)
        maskS = sb("maskS", [P, P], BF16)
        identb = sb("identb", [P, P], BF16)
        ones_b = sb("ones_b", [P, P], BF16)
        below = sb("below", [P, P], BF16)
        upto3 = sb("upto3", [32, 3, 32], BF16)
        start64 = sb("start64", [32, 32], BF16)
        param = sb("param", [P, N_PARAM])
        gbias = sb("gbias", [P, 1])
        wr = sb("wr", [P, KC, E])
        arena = sb("arena", [P, ARENA])
        at = [0]

        def take(words):
            at[0] += words
            return arena[:, at[0] - words:at[0]]

        qk = take(2048).rearrange("p (b t) -> p b t", t=T)
        hmT = qk[:, 0:4, :]
        fqT = take(1024).rearrange("p (b t) -> p b t", t=T)
        hfT = fqT
        fk_words = take(2048)
        fkz = fk_words.rearrange("p (b t) -> p b t", t=T)
        ln_g, ln_b = fk_words[:, 0:D], fk_words[:, D:2 * D]
        moe_at = at[0]
        gm = take(2048).rearrange("p (b t) -> p b t", t=T)
        gf = take(2048).rearrange("p (b t) -> p b t", t=T)
        mo = take(1024).rearrange("p (b t) -> p b t", t=T)
        moe_end, route_at = at[0], at[0]
        vm = take(TT * M_HEADS * (M_D + 1)).rearrange("p (a h d) -> p a h d", a=TT, h=M_HEADS)
        fv = take(TT * 512).rearrange("p (a n) -> p a n", a=TT)
        sel = take(F_HEADS * P).rearrange("p (h m) -> p h m", m=P)
        route_end = at[0]
        pt_words = take(6 * 512)
        PT = pt_words.rearrange("p (u n) -> p u n", n=512)
        yT = pt_words[:, 0:2048].rearrange("p (b t) -> p b t", t=T)
        tmp_rows = pt_words[0:64, 0:4 * T].rearrange("p (k t) -> p k t", t=T)
        p_words = take(1024)
        pr = p_words.rearrange("p (b n) -> p b n", n=512)
        wg = p_words[:, 0:KC * 96].rearrange("p (c n) -> p c n", n=96)
        d_words = take(4 * 384)
        dec = d_words[:, 0:768].rearrange("p (b n) -> p b n", n=384)
        ptm = d_words[:, 768:1536].rearrange("p (b n) -> p b n", n=384)
        param_raw = d_words[0:N_PARAM, 0:P]
        hml_words = take(1024)
        hml = hml_words.rearrange("p (a h d) -> p a h d", a=TT, h=M_HEADS)
        cv = hml_words[:, 0:512].rearrange("p (b t) -> p b t", t=T)
        sg_c = hml_words[:, 512:1024].rearrange("p (b t) -> p b t", t=T)
        ones256 = sg_c[0:64, 0, :]
        rowpack, rowM, rowF = take(T), take(T), take(T)
        upad = take(2 * (T + 4)).rearrange("p (b t) -> p b t", b=2)
        small = take(256)
        negmax = small[:, 0:32]
        rsum = small[:, 32:64]
        rrec = small[:, 64:96]
        msum = small[:, 96:128]
        hstat = small[:, 128:128 + 16]
        hrstd = small[:, 144:152]
        rden = small[:, 152:160]
        bn6 = small[:, 160:160 + 24]
        lstat = small[:, 184:184 + 4]
        lrstd = small[:, 188:190]
        colT = take(TT * 64).rearrange("p (a r) -> p a r", a=TT)
        em = take(8).rearrange("p (a h) -> p a h", a=TT)
        assert at[0] <= ARENA, at[0]

        at[0] = moe_at
        xgT = take(512).rearrange("p (c s) -> p c s", s=SLOTS)
        glu, sig, lin, half_act, act = (take(512) for _ in range(5))
        actT = take(512).rearrange("p (c s) -> p c s", s=P)
        ydn = take(512)
        pick = take(TT * SLOTS).rearrange("p (a s) -> p a s", a=TT)
        gated = take(TT * P).rearrange("p (a s) -> p a s", a=TT)
        gatedT = take(TT * P).rearrange("p (a t) -> p a t", a=TT)
        selb_w = take(SLOTS // 2)
        assert at[0] <= moe_end
        selb = selb_w.bitcast(BF16)[0:96, :]

        at[0] = route_at
        lg = take(TT * E).rearrange("p (a e) -> p a e", a=TT)
        br = take(E)
        top8 = take(TT * 8).rearrange("p (a k) -> p a k", a=TT)
        idx8 = take(TT * 8).rearrange("p (a k) -> p a k", a=TT)
        idxf = take(TT * 8).rearrange("p (a k) -> p a k", a=TT)
        ntop = take(2)
        gsum = take(2)
        mask = take(TT * E).rearrange("p (a e) -> p a e", a=TT)
        gexp = take(TT * E).rearrange("p (a e) -> p a e", a=TT)
        gpg = take(TT * 64).rearrange("p (a r) -> p a r", a=TT)
        gpgT = take(T).rearrange("p (a t) -> p a t", a=TT)[0:64]
        iota_e = take(E)
        iota_slot = take(SLOTS)
        iota_item = take(ITEMS)
        item_off = take(ITEMS)
        cnt = take(1)
        nb = take(1)
        st_col = take(1)
        start_sb = take(E)
        ownT = take(ITEMS)
        own = take(ITEMS)
        local = take(TT * ITEMS).rearrange("p (a i) -> p a i", a=TT)
        igate = take(TT * ITEMS).rearrange("p (a i) -> p a i", a=TT)
        slot1 = take(TT * E).rearrange("p (a e) -> p a e", a=TT)
        assert at[0] <= route_end, (at[0], route_end)
        mask3 = sb("mask3", [P, TT, 3, E], BF16)
        nbb = sb("nbb", [96, 1], BF16)
        nbB = sb("nbB", [32, P], BF16)
        own_b = sb("own_b", [32, ITEMS], BF16)
        iota_col = sb("iota_col", [32, 1], BF16)
        expert_row = sb("expert_row", [1, ITEMS], I32)
        n_items = sb("n_items", [1, 1], I32)

        x_in = sem("x_in"); wg_in = sem("wg_in"); par_in = sem("par_in"); gb_in = sem("gb_in")
        bias_in = sem("bias_in"); vb_in = sem("vb_in"); wr_in = sem("wr_in"); br_in = sem("br_in")
        ln1_in = sem("ln1_in"); ln2_in = sem("ln2_in")
        blk_in = [sem(f"blk_in{n}") for n in range(15)]
        slot_in = [sem(f"slot_in{k}") for k in range(RING)]
        out_done = sem("out_done")
        consts = sem("consts"); pool_chain = sem("pool_chain"); wg_zero = sem("wg_zero")
        bias3_done = sem("bias3_done"); iotas = sem("iotas")
        xT_ps = sem("xT_ps"); par_ps = sem("par_ps"); gate_ps = sem("gate_ps"); col_ps = sem("col_ps")
        proj_ps = sem("proj_ps"); S_ps = sem("S_ps"); T_ps = sem("T_ps"); V_ps = sem("V_ps")
        B_ps = sem("B_ps"); N_ps = sem("N_ps"); hm_ps = sem("hm_ps"); y_ps = sem("y_ps"); mix_ps = sem("mix_ps")
        hT_ps = sem("hT_ps"); lg_ps = sem("lg_ps"); cnt_ps = sem("cnt_ps"); end_ps = sem("end_ps")
        gpgT_ps = sem("gpgT_ps"); item_ps = sem("item_ps")
        released = sem("released")
        scat_ps = sem("scat_ps"); xg_ps = sem("xg_ps"); tr_ps = sem("tr_ps"); dn_ps = sem("dn_ps")
        xT_v = sem("xT_v"); xT_a = sem("xT_a"); par_sb = sem("par_sb"); u_sb = sem("u_sb"); qk_sb = sem("qk_sb")
        proj_sb = sem("proj_sb"); logexp = sem("logexp"); z_sb = sem("z_sb"); rows_sb = sem("rows_sb")
        col_sb = sem("col_sb"); em_sb = sem("em_sb"); conv_sb = sem("conv_sb"); csig = sem("csig")
        max_sb = sem("max_sb"); exp_sb = sem("exp_sb"); prob_sb = sem("prob_sb"); PT_sb = sem("PT_sb")
        hf_sb = sem("hf_sb"); dec_sb = sem("dec_sb"); ptm_sb = sem("ptm_sb"); num_sb = sem("num_sb")
        hvar = sem("hvar"); hstd = sem("hstd"); hn_sb = sem("hn_sb"); gates_sig = sem("gates_sig"); hm_sb = sem("hm_sb")
        y_sb = sem("y_sb"); var1 = sem("var1"); std1 = sem("std1"); h1_sb = sem("h1_sb")
        hT_v = sem("hT_v"); hT_a = sem("hT_a"); lgmax = sem("lgmax"); gexp_sb = sem("gexp_sb")
        mask_sb = sem("mask_sb"); nb_sb = sem("nb_sb"); gpg_sb = sem("gpg_sb"); gpgT_sb = sem("gpgT_sb"); own_sb = sem("own_sb")
        tables = sem("tables")
        v_chain = sem("v_chain"); a_chain = sem("a_chain")
        pick_sb = sem("pick_sb"); gated_sb = sem("gated_sb"); selb_sb = sem("selb_sb")
        glu_sb = sem("glu_sb"); sig_sb = sem("sig_sb"); act_sb = sem("act_sb"); moe_v = sem("moe_v")
        xg_sb = sem("xg_sb"); actT_sb = sem("actT_sb"); gatedT_sb = sem("gatedT_sb"); ydn_sb = sem("ydn_sb")
        var2 = sem("var2"); std2 = sem("std2"); fin_sb = sem("fin_sb")

        def chunks(w):
            return w.rearrange("(c p) n -> p c n", p=P)

        def rows(v):
            return v.rearrange("(r p) -> r p", p=P)

        win = w_in[0]
        bin_ = b_in[0]

        block = ctx.enter_context(nc.Block())

        @block.sync
        def _(sp):
            for tt in range(TT):
                sp.dma_start(h[:, tt, :], x[0, tt * P:(tt + 1) * P, :]).then_inc(x_in, 16)
            sp.wait_ge(wg_zero, 1)
            for dst, src, n in ((0, MF, 4), (32, FF, 8), (64, MI, 4)):
                sp.dma_start(wg[:, :, dst:dst + n], chunks(win[:, src:src + n])).then_inc(wg_in, 16)
                sp.dma_start(gbias[dst:dst + n, :], bin_[src:src + n].rearrange("(p a) -> p a", a=1)).then_inc(gb_in, 16)
            for name, src in (("mqk", bin_[MQK:MQK + 1024]), ("mo", bin_[MO:MO + 512]), ("fq", bin_[FQ:FQ + 1024]),
                              ("gm", bin_[GM:GM + 2048]), ("cw", m_conv_w[0].rearrange("j n -> (j n)")),
                              ("cb", m_conv_b[0]), ("ng", m_norm_g[0])):
                r = PARAM_ROWS[name]
                src = rows(src)
                sp.dma_start(param_raw[r:r + src.shape[0], :], src).then_inc(par_in, 16)

            def load_block(n):
                if n < 11:
                    sp.dma_start(wblk[n], chunks(win[:, GROUPS[n]:GROUPS[n] + 512])).then_inc(blk_in[n], 16)
                elif n == W_BM:
                    sp.dma_start(wbm_sb, chunks(w_bm[0])).then_inc(blk_in[n], 16)
                elif n == W_BF:
                    sp.dma_start(wbf_sb, chunks(w_bf[0])).then_inc(blk_in[n], 16)
                else:
                    j = n - W_O0
                    sp.dma_start(wo_sb[j], chunks(w_o[0][:, j * 512:(j + 1) * 512])).then_inc(blk_in[n], 16)

            for n in range(2):
                load_block(n)
            for g in range(3):
                sp.dma_start(bias_raw[32 * g:32 * g + 32, 0:2 * D], b_gu[0]).then_inc(bias_in, 16)
                sp.dma_start(bias_raw[32 * g:32 * g + 32, 2 * D:3 * D], b_dn[0]).then_inc(bias_in, 16)
            for tt in range(TT):
                sp.dma_start(vm[:, tt, :, 0:M_D], bin_[MV:MV + 512].rearrange("(a h d) -> a h d", a=1, h=M_HEADS)
                             .to_broadcast([P, M_HEADS, M_D])).then_inc(vb_in, 16)
                sp.dma_start(fv[:, tt, :], bin_[FV:FV + 512].rearrange("(a n) -> a n", a=1)
                             .to_broadcast([P, 512])).then_inc(vb_in, 16)
            for n in range(2, 5):
                load_block(n)
            sp.wait_ge(bias3_done, 1)
            load_block(5)
            sp.dma_start(wr[:, :, :], chunks(w_router[0])).then_inc(wr_in, 16)
            done_after = {0: 4, 1: 8, 2: 10, 3: 14, 4: 18, 5: 20, 6: 24, 7: 28, 8: 32, 9: 36, 10: 40}
            for n in (6, 7, 8, 9, W_BM, W_BF, 10, W_O0, W_O1):
                before = max(m for m in range(n) if REGION[m] == REGION[n])
                sp.wait_ge(proj_ps, done_after[before])
                load_block(n)
            sp.wait_ge(S_ps, len(UNITS))
            sp.dma_start(ln_g, ln1_g[0:1, :].to_broadcast([P, D])).then_inc(ln1_in, 16)
            sp.dma_start(ln_b, ln1_b[0:1, :].to_broadcast([P, D])).then_inc(ln1_in, 16)
            sp.wait_ge(N_ps, M_HEADS)
            sp.wait_ge(V_ps, 4)
            sp.dma_start(br, b_router[0:1, :].to_broadcast([P, E])).then_inc(br_in, 16)

            def load_slot(k, e):
                if k < GU_SLOTS:
                    src = w_gu[0, e, k * P:(k + 1) * P, :] if isinstance(e, int) else \
                        w_gu[0][bass.ds(e, 1), k * P:(k + 1) * P, :].rearrange("a p n -> p (a n)")
                    sp.dma_start(slot[k], src).then_inc(slot_in[k], 16)
                else:
                    f0 = (k - GU_SLOTS) * 2 * P
                    src = chunks(w_dn[0, e, f0:f0 + 2 * P, :]) if isinstance(e, int) else \
                        w_dn[0][bass.ds(e, 1), f0:f0 + 2 * P, :].rearrange("a (c p) n -> p (a c) n", p=P)
                    sp.dma_start(slot[k].rearrange("p (c n) -> p c n", n=D), src).then_inc(slot_in[k], 16)

            for slots, signal, value in (((6, 7), proj_ps, 36), ((0, 1), proj_ps, 40), ((8, 9, 10, 11), y_ps, KC),
                                         ((2, 3, 4, 5), mix_ps, 4)):
                sp.wait_ge(signal, value)
                for k in slots:
                    load_slot(k, 0)
            sp.wait_ge(tables, 2)
            n = sp.value_load(n_items[0:1, 0:1], min_val=E, max_val=MAX_ITEMS)
            with sp.Fori(1, n) as i:
                e = sp.value_load(expert_row[0:1, bass.ds(i, 1)], min_val=0, max_val=E - 1)
                for k in range(RING):
                    sp.wait_ge(released, i * RING + (k + 1 - RING))
                    load_slot(k, e)
            sp.wait_ge(h1_sb, 2)
            sp.dma_start(ln_g, ln2_g[0:1, :].to_broadcast([P, D])).then_inc(ln2_in, 16)
            sp.dma_start(ln_b, ln2_b[0:1, :].to_broadcast([P, D])).then_inc(ln2_in, 16)
            for tt in range(TT):
                sp.wait_ge(fin_sb, tt + 1)
                sp.dma_start(out[0, tt * P:(tt + 1) * P, :], h[:, tt, :]).then_inc(out_done, 16)
            sp.wait_ge(out_done, 16 * TT)

        @block.gpsimd
        def _(pool):
            count = [0]

            def link(ins):
                count[0] += 1
                ins.then_inc(pool_chain, 1)
                pool.wait_ge(pool_chain, count[0])

            pool.memset(gbias[:, :], 0.0)
            pool.memset(wg, 0.0).then_inc(wg_zero, 1)
            pool.memset(ident[:, :], 0.0)
            pool.memset(maskT[:, :], 0.0)
            pool.memset(maskS[:, :], 0.0)
            pool.memset(below[:, :], 1.0)
            pool.memset(upto3[:, :, :], 1.0)
            pool.memset(start64[:, :], float(SLOTS))
            link(pool.memset(sel, 0.0))
            pool.affine_select(out=ident[:, :], in_=ident[:, :], compare_op=ALU.not_equal, fill=1.0, base=0,
                               pattern=[[-1, P]], channel_multiplier=1).then_inc(consts, 1)
            pool.memset(ones_b[:, :], 1.0)
            pool.memset(ones256, 1.0)
            pool.affine_select(out=maskT[:, :], in_=maskT[:, :], compare_op=ALU.is_ge, fill=NEG, base=0,
                               pattern=[[1, P]], channel_multiplier=-1)
            pool.affine_select(out=maskS[:, :], in_=maskS[:, :], compare_op=ALU.is_ge, fill=NEG, base=0,
                               pattern=[[-1, P]], channel_multiplier=1)
            pool.affine_select(out=sel, in_=sel, compare_op=ALU.not_equal, fill=1.0, base=0,
                               pattern=[[-1, F_HEADS], [0, P]], channel_multiplier=1)
            pool.affine_select(out=below[:, :], in_=below[:, :], compare_op=ALU.is_gt, fill=0.0, base=0,
                               pattern=[[1, P]], channel_multiplier=-1)
            pool.affine_select(out=upto3[:, :, :], in_=upto3[:, :, :], compare_op=ALU.is_ge, fill=0.0, base=0,
                               pattern=[[0, 3], [1, 32]], channel_multiplier=-1)
            pool.affine_select(out=start64[:, :], in_=start64[:, :], compare_op=ALU.is_gt, fill=0.0, base=0,
                               pattern=[[1, 32]], channel_multiplier=-1)
            pool.memset(rowpack, 0.0)
            pool.memset(rowM, 0.0)
            link(pool.memset(rowF, 0.0))
            pool.tensor_copy(identb[:, :], ident[:, :])
            pool.tensor_scalar(aident[:, :], ident[:, :], ALPHA, None, ALU.mult)
            pool.memset(fkz, 0.0)
            for b in range(2):
                pool.memset(upad[:, b, 0:4], 0.0)
            link(pool.memset(vm[:, :, :, M_D:M_D + 1], 1.0))
            pool.iota(iota_col[:, :], pattern=[[0, 1]], base=0, channel_multiplier=1,
                      allow_small_or_imprecise_dtypes=True).then_inc(consts, 1)
            pool.wait_ge(consts, 2)
            pool.wait_ge(bias_in, 96)
            link(pool.tensor_copy(bias3[:, :], bias_raw))
            for first in (32, 64):
                for g in range(first, 96, 32):
                    rest = pool.tensor_tensor(bias_raw[g:g + 32, :], bias_raw[g:g + 32, :], bias3[g:g + 32, :], ALU.subtract)
                link(rest)
                for g in range(first, 96, 32):
                    last = pool.tensor_copy(bias3[g:g + 32, :], bias_raw[g:g + 32, :])
                if first == 32:
                    link(last)
            last.then_inc(bias3_done, 1)
            pool.wait_ge(N_ps, M_HEADS)
            pool.wait_ge(V_ps, 4)
            kw = dict(allow_small_or_imprecise_dtypes=True, channel_multiplier=0)
            pool.iota(iota_e, pattern=[[1, E]], base=0, **kw)
            pool.iota(iota_slot, pattern=[[1, SLOTS]], base=0, **kw)
            pool.iota(iota_item, pattern=[[1, ITEMS]], base=0, **kw)
            pool.iota(item_off, pattern=[[SLOTS, ITEMS]], base=1, **kw).then_inc(iotas, 1)

        @block.tensor
        def _(pe):
            def transposes(src, banks, done, idn=ident):
                for g in range(4):
                    for c in range(2):
                        for tt in range(TT):
                            last = pe.transpose(bank[banks[g]][:, (c * TT + tt) * P:(c * TT + tt + 1) * P],
                                                src[:, tt, (2 * g + c) * P:(2 * g + c + 1) * P], idn[:, :])
                    last.then_inc(done, 1)

            pe.wait_ge(consts, 1)
            pe.wait_ge(x_in, 16 * TT)
            transposes(h, [4, 5, 6, 7], xT_ps)
            pe.wait_ge(par_in, 16 * 7)
            pe.transpose(bank[3][:, 0:N_PARAM], param_raw, ident[0:N_PARAM, 0:N_PARAM]).then_inc(par_ps, 1)
            pe.wait_ge(wg_in, 48)
            pe.wait_ge(xT_v, 2)
            pe.wait_ge(xT_a, 2)
            for c in range(KC):
                last = pe.matmul(bank[2][0:96, 0:T], wg[:, c, :], hT[:, c, :], start=(c == 0), stop=(c == KC - 1))
            last.then_inc(gate_ps, 1)

            state = {"block": 0}

            def free_bank(n):
                m = n - 2
                if 0 <= m < 8:
                    pe.wait_ge(u_sb, m + 1)
                elif m >= 8:
                    pe.wait_ge(proj_sb, m - 7)

            def project(g, b):
                n = state["block"]
                if b == 0:
                    pe.wait_ge(blk_in[g], 16)
                free_bank(n)
                for c in range(KC):
                    if g in TOKEN_MAJOR:
                        last = pe.matmul(bank[n % 2][:, :], hT[:, c, b * P:(b + 1) * P], wblk[g][:, c, :],
                                         start=(c == 0), stop=(c == KC - 1))
                    else:
                        last = pe.matmul(bank[n % 2][:, 0:T], wblk[g][:, c, b * P:(b + 1) * P], hT[:, c, :],
                                         start=(c == 0), stop=(c == KC - 1))
                last.then_inc(proj_ps, 1)
                state["block"] += 1

            for b in range(4):
                project(0, b)
            pe.wait_ge(rows_sb, 1)
            pe.wait_ge(par_sb, 1)
            for tt in range(TT):
                last = pe.transpose(bank[3][:, tt * P:(tt + 1) * P], rowpack[:, tt * P:(tt + 1) * P], ident[:, :])
            last.then_inc(col_ps, 1)
            for g in range(1, 6):
                for b in range(2 if g in TOKEN_MAJOR else 4):
                    project(g, b)

            def scores(u):
                tt, heads = UNITS[u]
                if u == 0:
                    pe.wait_ge(proj_sb, 12)
                    pe.wait_ge(rows_sb, 1)
                    pe.wait_ge(consts, 2)
                    pe.wait_ge(col_sb, 1)
                if u >= 2:
                    pe.wait_ge(exp_sb, u - 1)
                n = (tt + 1) * P
                for j, hd in enumerate(heads):
                    o = bank[2 + u % 2][:, j * n:(j + 1) * n]
                    pe.matmul(o, fqT[:, hd // 2, tt * P:(tt + 1) * P], fkz[:, hd, 0:n], start=True, stop=False)
                    pe.matmul(o, sel[:, hd, :], rowF[:, 0:n], start=False, stop=False)
                    last = pe.matmul(o[:, n - P:n], identb[:, :], maskS[:, :], start=False, stop=True)
                last.then_inc(S_ps, 1)

            def turn(u):
                pe.wait_ge(prob_sb, u + 1)
                if u >= 2:
                    pe.wait_ge(PT_sb, u - 1)
                for j in range(4):
                    last = pe.transpose(bank[4 + u % 2][:, j * P:(j + 1) * P], pr[:, u % 2, j * P:(j + 1) * P], ident[:, :])
                last.then_inc(T_ps, 1)

            def values(pair):
                pe.wait_ge(PT_sb, 6)
                if pair >= 2:
                    pe.wait_ge(hf_sb, pair - 1)
                for j in range(2):
                    hd = 2 * pair + j
                    o = bank[6 + pair % 2][64 * j:64 * j + 64, :]
                    pe.matmul(o[:, 0:P], fv[:, 0, hd * F_D:(hd + 1) * F_D],
                              PT[:, 4 + pair // 2, (hd % 4) * P:(hd % 4 + 1) * P], start=True, stop=True)
                    for s in range(2):
                        last = pe.matmul(o[:, P:T], fv[:, s, hd * F_D:(hd + 1) * F_D],
                                         PT[:, pair, (2 * j + s) * P:(2 * j + s + 1) * P],
                                         start=(s == 0), stop=(s == 1))
                last.then_inc(V_ps, 1)

            def decay(hd):
                if hd == 0:
                    pe.wait_ge(exp_sb, 6)
                    pe.wait_ge(qk_sb, 8)
                else:
                    pe.wait_ge(dec_sb, 2 * hd)
                    pe.wait_ge(ptm_sb, hd)
                pe.matmul(bank[2][:, 0:T], sel[:, hd, :], rowM, start=True, stop=False)
                pe.matmul(bank[2][:, 0:P], identb[:, :], maskT[:, :], start=False, stop=True)
                pe.matmul(bank[2][:, T:T + P], sel[:, hd, :], rowM[:, P:T], start=True, stop=False)
                pe.matmul(bank[2][:, T:T + P], identb[:, :], maskT[:, :], start=False, stop=True)
                pe.matmul(bank[3][:, 0:T], qk[:, 4 + hd, 0:P], qk[:, hd, :], start=True, stop=True)
                pe.matmul(bank[3][:, T:T + P], qk[:, 4 + hd, P:T], qk[:, hd, P:T], start=True, stop=True).then_inc(B_ps, 1)

            def numerators(hd):
                pe.wait_ge(ptm_sb, hd + 1)
                if hd == 0:
                    pe.wait_ge(PT_sb, 6)
                if hd >= 2:
                    pe.wait_ge(num_sb, hd - 1)
                o = bank[4 + hd % 2]
                w = ptm[:, hd % 2, :]
                pe.matmul(o[:, 0:M_D + 1], w[:, 0:P], vm[:, 0, hd, :], start=True, stop=True)
                pe.matmul(o[:, T:T + M_D + 1], w[:, P:T], vm[:, 0, hd, :], start=True, stop=False)
                pe.matmul(o[:, T:T + M_D + 1], w[:, T:T + P], vm[:, 1, hd, :], start=False, stop=True).then_inc(N_ps, 1)

            kinds = {"S": scores, "T": turn, "V": values, "B": decay, "N": numerators}
            for k, steps in enumerate(STEPS):
                for s in steps:
                    kinds[s[0]](int(s[1]))
                project(6 + k // 4, k % 4)

            pe.wait_ge(hn_sb, 1)
            for b in range(2):
                for j in range(2):
                    for tt in range(TT):
                        last = pe.transpose(bank[2 + b][:, (j * TT + tt) * P:(j * TT + tt + 1) * P],
                                            hml[:, tt, 2 * b + j, :], ident[:, :])
                last.then_inc(hm_ps, 1)
            for f in range(KC):
                if f == 0:
                    pe.wait_ge(hm_sb, 4)
                    pe.wait_ge(hf_sb, 4)
                    pe.wait_ge(num_sb, 4)
                    pe.wait_ge(blk_in[W_BM], 16)
                    pe.wait_ge(blk_in[W_BF], 16)
                if f >= 2:
                    pe.wait_ge(y_sb, f - 1)
                for c in range(4):
                    pe.matmul(bank[4 + f % 2][:, 0:T], wbm_sb[:, c, f * P:(f + 1) * P], hmT[:, c, :],
                              start=(c == 0), stop=(c == 3))
                for c in range(4):
                    last = pe.matmul(bank[6 + f % 2][:, 0:T], wbf_sb[:, c, f * P:(f + 1) * P], hfT[:, c, :],
                                     start=(c == 0), stop=(c == 3))
                last.then_inc(y_ps, 1)
            for tt in range(TT):
                for j in range(2):
                    if tt == 0:
                        pe.wait_ge(blk_in[W_O0 + j], 16)
                    pe.wait_ge(y_sb, KC)
                    for c in range(KC):
                        last = pe.matmul(bank[2 * tt + j][:, :], yT[:, c, tt * P:(tt + 1) * P], wo_sb[j][:, c, :],
                                         start=(c == 0), stop=(c == KC - 1))
                    last.then_inc(mix_ps, 1)

            pe.wait_ge(h1_sb, 2)
            transposes(h, [4, 5, 6, 7], hT_ps)
            pe.wait_ge(hT_v, 2)
            pe.wait_ge(hT_a, 2)
            pe.wait_ge(wr_in, 16)
            for tt in range(TT):
                for c in range(KC):
                    last = pe.matmul(bank[0][:, tt * E:(tt + 1) * E], hT[:, c, tt * P:(tt + 1) * P], wr[:, c, :],
                                     start=(c == 0), stop=(c == KC - 1))
            last.then_inc(lg_ps, 1)
            for tt in range(TT):
                for j in range(2):
                    pe.matmul(bank[4 + 2 * tt + j][:, :], aident[:, :], h[:, tt, j * 512:(j + 1) * 512],
                              start=True, stop=False, skip_group_check=True)
            pe.wait_ge(mask_sb, 1)
            for tt in range(TT):
                pe.matmul(bank[1][0:96, 0:1], mask3[:, tt, :, :].rearrange("p g e -> p (g e)"), ones_b[:, 0:1],
                          start=(tt == 0), stop=(tt == TT - 1)).then_inc(cnt_ps, 1)
            pe.matmul(bank[2][:, 0:E], below[:, :], mask3[:, 0, 0, :], start=True, stop=True)
            pe.matmul(bank[2][:, E:2 * E], ones_b[:, :], mask3[:, 0, 0, :], start=True, stop=False)
            pe.matmul(bank[2][:, E:2 * E], below[:, :], mask3[:, 1, 0, :], start=False, stop=True).then_inc(cnt_ps, 1)
            pe.wait_ge(nb_sb, 1)
            pe.matmul(bank[1][0:96, 1:2], upto3[:, :, :].rearrange("p g e -> p (g e)"), nbb[0:32, :], start=True, stop=True)
            pe.matmul(bank[3][0:1, 0:1], nbb[0:32, :], ones_b[0:32, 0:1], start=True, stop=True)
            pe.matmul(bank[0][:, 0:E], nbB[:, :], start64[:, :], start=True, stop=True).then_inc(end_ps, 1)
            pe.wait_ge(gpg_sb, 1)
            for tt in range(TT):
                last = pe.transpose(bank[0][0:64, 64 + tt * P:64 + (tt + 1) * P], gpg[:, tt, :], ident[:, :])
            last.then_inc(gpgT_ps, 1)
            pe.wait_ge(gpgT_sb, 1)
            pe.wait_ge(own_sb, 1)
            pe.matmul(bank[3][0:1, 0:ITEMS], iota_col[:, :], own_b[:, :], start=True, stop=True)
            for tt in range(TT):
                pe.matmul(bank[1][:, tt * ITEMS:(tt + 1) * ITEMS], gpgT[0:32, tt, :], own[0:32, :], start=True, stop=True)
                last = pe.matmul(bank[2][:, tt * ITEMS:(tt + 1) * ITEMS], gpgT[32:64, tt, :], own[32:64, :],
                                 start=True, stop=True)
            last.then_inc(item_ps, 1)

            def gather():
                for c in range(KC):
                    for tt in range(TT):
                        last = pe.matmul(bank[3][:, c * SLOTS:(c + 1) * SLOTS], h[:, tt, c * P:(c + 1) * P],
                                         pick[:, tt, :], start=(tt == 0), stop=(tt == TT - 1))
                last.then_inc(xg_ps, 1)

            def scatter():
                for tt in range(TT):
                    for j in range(2):
                        last = pe.matmul(bank[4 + 2 * tt + j][:, :], gatedT[64 * j:64 * j + 64, tt, :],
                                         ydn[64 * j:64 * j + 64, :], start=False, stop=False, skip_group_check=True)
                last.then_inc(scat_ps, 1)

            pe.wait_ge(tables, 2)
            n = pe.value_load(n_items[0:1, 0:1], min_val=E, max_val=MAX_ITEMS)
            pe.wait_ge(pick_sb, 1)
            gather()
            with pe.Fori(0, n) as i:
                pe.wait_ge(xg_sb, i + 1)
                pe.wait_ge(actT_sb, i + 1)
                pe.wait_ge(gatedT_sb, i + 1)
                for k in range(GU_SLOTS):
                    pe.wait_ge(slot_in[k], i * 16 + 16)
                    for b in range(2):
                        for j in range(2):
                            o = D_FF * b + 512 * j
                            last = pe.matmul(bank[b][64 * j:64 * j + 64, :], xgT[:, k, :], slot[k][:, o:o + 512],
                                             start=(k == 0), stop=(k == GU_SLOTS - 1))
                    last.then_inc(released, 1)
                    if k == GU_SLOTS - 2:
                        pe.wait_ge(selb_sb, i + 1)
                        for b in range(2):
                            for j in range(2):
                                o = D_FF * b + 512 * j
                                pe.matmul(bank[b][64 * j:64 * j + 64, :], selb, bias3[:, o:o + 512],
                                          start=False, stop=False)
                pe.wait_ge(ydn_sb, i + 1)
                scatter()
                pe.wait_ge(pick_sb, i + 2)
                gather()
                pe.wait_ge(act_sb, i + 1)
                pe.wait_ge(gated_sb, i + 1)
                for q in range(4):
                    pe.transpose(bank[0][:, q * P:(q + 1) * P], act[:, q * P:(q + 1) * P], ident[:, :])
                for tt in range(TT):
                    last = pe.transpose(bank[1][:, tt * P:(tt + 1) * P], gated[:, tt, :], ident[:, :])
                last.then_inc(tr_ps, 1)
                for j in range(2):
                    o = 2 * D + 512 * j
                    pe.matmul(bank[2][64 * j:64 * j + 64, :], selb, bias3[:, o:o + 512], start=True, stop=False)
                pe.wait_ge(actT_sb, i + 2)
                for k in range(GU_SLOTS, RING):
                    pe.wait_ge(slot_in[k], i * 16 + 16)
                    for c in range(2):
                        f = 2 * (k - GU_SLOTS) + c
                        for j in range(2):
                            last = pe.matmul(bank[2][64 * j:64 * j + 64, :],
                                             actT[:, f % 4, 64 * (f // 4):64 * (f // 4) + 64],
                                             slot[k][:, c * D + 512 * j:c * D + 512 * j + 512],
                                             start=False, stop=(f == KC - 1))
                    last.then_inc(released, 1)
            pe.wait_ge(ydn_sb, n + 1)
            scatter()

        @block.scalar
        def _(sc):
            count = [0]

            def link(ins):
                count[0] += 1
                ins.then_inc(a_chain, 1)
                sc.wait_ge(a_chain, count[0])

            for g in (2, 3):
                sc.wait_ge(xT_ps, g + 1)
                sc.copy(hT[:, 2 * g:2 * g + 2, :], bank[4 + g][:, :].rearrange("p (c t) -> p c t", t=T)).then_inc(xT_a, 1)
            sc.wait_ge(z_sb, 1)
            link(sc.activation(tmp_rows[:, 2, :], tmp_rows[:, 1, :], ACT.Exp))
            sc.activation(tmp_rows[:, 1, :], tmp_rows[:, 2, :], ACT.Ln, bias=1.0).then_inc(logexp, 1)

            def conv_sigmoid(b):
                sc.wait_ge(conv_sb, b + 1)
                if b >= 2:
                    sc.wait_ge(qk_sb, b - 1)
                sc.activation(sg_c[:, b % 2, :], cv[:, b % 2, :], ACT.Sigmoid).then_inc(csig, 1)

            for b in range(8):
                sc.wait_ge(proj_ps, b + 1)
                if b == 0:
                    sc.wait_ge(par_sb, 1)
                    sc.wait_ge(consts, 2)
                if b >= 2:
                    sc.wait_ge(conv_sb, b - 1)
                sc.activation(upad[:, b % 2, 3:3 + T], bank[b % 2][:, 0:T], ACT.Identity,
                              bias=param[:, b:b + 1]).then_inc(u_sb, 1)
                if b >= 1:
                    conv_sigmoid(b - 1)
            conv_sigmoid(7)
            sc.wait_ge(col_sb, 1)
            sc.activation(em, colT[:, :, 32:36], ACT.Exp).then_inc(em_sb, 1)

            def softmax_exp(u):
                tt, heads = UNITS[u]
                n = (tt + 1) * P
                sc.wait_ge(max_sb, u + 1)
                if u >= 2:
                    sc.wait_ge(T_ps, u - 1)
                for j in range(len(heads)):
                    last = sc.activation(pr[:, u % 2, j * n:(j + 1) * n], bank[2 + u % 2][:, j * n:(j + 1) * n], ACT.Exp,
                                         bias=negmax[:, 4 * u + j:4 * u + j + 1],
                                         accum_out=rsum[:, 4 * u + j:4 * u + j + 1])
                last.then_inc(exp_sb, 1)

            def decay_exp(hd):
                sc.wait_ge(B_ps, hd + 1)
                if hd >= 2:
                    sc.wait_ge(ptm_sb, hd - 1)
                for s, (o, n) in enumerate(((0, T), (T, P))):
                    sc.activation(dec[:, hd % 2, o:o + n], bank[2][:, o:o + n], ACT.Exp,
                                  bias=colT[:, s, hd:hd + 1]).then_inc(dec_sb, 1)

            for steps in STEPS:
                for s in steps:
                    if s[0] == "S":
                        softmax_exp(int(s[1]))
                    if s[0] == "B":
                        decay_exp(int(s[1]))
            sc.wait_ge(hvar, 1)
            sc.activation(hrstd, hrstd, ACT.Sqrt).then_inc(hstd, 1)
            sc.wait_ge(proj_sb, 32)
            sc.activation(mo, mo, ACT.Sigmoid).then_inc(gates_sig, 1)
            sc.activation(gm, gm, ACT.Sigmoid).then_inc(gates_sig, 1)
            sc.activation(gf, gf, ACT.Sigmoid).then_inc(gates_sig, 1)
            sc.wait_ge(var1, 1)
            sc.activation(lrstd, lrstd, ACT.Sqrt).then_inc(std1, 1)
            for g in (2, 3):
                sc.wait_ge(hT_ps, g + 1)
                sc.copy(hT[:, 2 * g:2 * g + 2, :], bank[4 + g][:, :].rearrange("p (c t) -> p c t", t=T)).then_inc(hT_a, 1)
            sc.wait_ge(lgmax, 1)
            for tt in range(TT):
                last = sc.activation(gexp[:, tt, :], lg[:, tt, :], ACT.Exp, bias=ntop[:, tt:tt + 1])
            last.then_inc(gexp_sb, 1)

            sc.wait_ge(tables, 2)
            n = sc.value_load(n_items[0:1, 0:1], min_val=E, max_val=MAX_ITEMS)

            def take_tokens():
                sc.copy(xgT, bank[3][:, :].rearrange("p (c s) -> p c s", s=SLOTS)).then_inc(xg_sb, 1)

            sc.wait_ge(xg_ps, 1)
            take_tokens()
            with sc.Fori(0, n) as i:
                sc.wait_ge(glu_sb, i + 1)
                sc.activation(sig, glu, ACT.Sigmoid, scale=SW_ALPHA).then_inc(sig_sb, 1)
                sc.wait_ge(xg_ps, i + 2)
                take_tokens()
                sc.wait_ge(tr_ps, i + 1)
                sc.copy(gatedT, bank[1][:, 0:T].rearrange("p (a t) -> p a t", a=TT)).then_inc(gatedT_sb, 1)
                sc.wait_ge(released, i * RING + RING)
                sc.copy(ydn, bank[2][:, :]).then_inc(ydn_sb, 1)
            sc.wait_ge(var2, 1)
            sc.activation(lrstd, lrstd, ACT.Sqrt).then_inc(std2, 1)

        @block.vector
        def _(v):
            count = [0]

            def link(ins):
                count[0] += 1
                ins.then_inc(v_chain, 1)
                v.wait_ge(v_chain, count[0])

            for g in (0, 1):
                v.wait_ge(xT_ps, g + 1)
                v.tensor_copy(hT[:, 2 * g:2 * g + 2, :], bank[4 + g][:, :].rearrange("p (c t) -> p c t", t=T)).then_inc(xT_v, 1)
            v.wait_ge(par_ps, 1)
            v.tensor_copy(param[:, :], bank[3][:, 0:N_PARAM]).then_inc(par_sb, 1)

            v.wait_ge(gate_ps, 1)
            v.wait_ge(gb_in, 48)
            z, ln1p, logf, gate_in = (tmp_rows[:, k, :] for k in range(4))
            link(v.tensor_scalar(z, bank[2][0:64, 0:T], gbias[0:64, :], None, ALU.add))
            v.scalar_tensor_tensor(out=ln1p, in0=z, scalar=-1.0, in1=z, op0=ALU.mult, op1=ALU.min).then_inc(z_sb, 1)
            v.tensor_scalar(gate_in[0:4, :], bank[2][64:68, 0:T], gbias[64:68, :], None, ALU.add)
            v.wait_ge(logexp, 1)
            link(v.scalar_tensor_tensor(out=logf, in0=z, scalar=0.0, in1=ln1p, op0=ALU.min, op1=ALU.subtract))
            v.wait_ge(consts, 2)
            link(v.tensor_tensor_scan(z, ones256, logf, 0.0, ALU.mult, ALU.add))
            link(v.tensor_tensor(rowpack[0:4, :], gate_in[0:4, :], z[0:4, :], ALU.subtract))
            link(v.tensor_tensor_scan(ln1p[0:4, :], rowpack[0:4, :], rowpack[0:4, :], 0.0, ALU.max, ALU.max))
            v.tensor_scalar(rowM[0:4, :], ln1p[0:4, :], -1.0, None, ALU.mult)
            v.scalar_tensor_tensor(out=rowpack[32:36, :], in0=z[0:4, :], scalar=-1.0, in1=ln1p[0:4, :],
                                   op0=ALU.mult, op1=ALU.subtract)
            v.tensor_scalar(rowF[0:8, :], z[32:40, :], -1.0, None, ALU.mult).then_inc(rows_sb, 1)

            def conv(b):
                v.wait_ge(u_sb, b + 1)
                if b >= 2:
                    v.wait_ge(qk_sb, b - 1)
                cw = PARAM_ROWS["cw"]
                u, o = upad[:, b % 2, :], cv[:, b % 2, :]
                link(v.tensor_scalar(o, u[:, 0:T], param[:, cw + b:cw + b + 1],
                                     param[:, PARAM_ROWS["cb"] + b:PARAM_ROWS["cb"] + b + 1], ALU.mult, ALU.add))
                for j in range(1, CONV_W):
                    w = param[:, cw + 8 * j + b:cw + 8 * j + b + 1]
                    last = v.scalar_tensor_tensor(out=o, in0=u[:, j:j + T], scalar=w, in1=o, op0=ALU.mult, op1=ALU.add)
                    if j < CONV_W - 1:
                        link(last)
                last.then_inc(conv_sb, 1)

            def silu(b):
                v.wait_ge(csig, b + 1)
                v.scalar_tensor_tensor(out=qk[:, b, :], in0=cv[:, b % 2, :], scalar=1.0 if b < 4 else M_D ** -0.5,
                                       in1=sg_c[:, b % 2, :], op0=ALU.mult, op1=ALU.mult).then_inc(qk_sb, 1)

            for b in range(8):
                conv(b)
                if b == 4:
                    v.wait_ge(col_ps, 1)
                    v.tensor_copy(colT, bank[3][:, 0:TT * P].rearrange("p (a r) -> p a r", a=TT)[:, :, 0:64]).then_inc(col_sb, 1)
                if b >= 1:
                    silu(b - 1)
            silu(7)

            v.wait_ge(vb_in, 64)
            for tt in range(TT):
                v.wait_ge(proj_ps, 9 + tt)
                v.tensor_tensor(vm[:, tt, :, 0:M_D], bank[tt % 2][:, :].rearrange("p (h d) -> p h d", h=M_HEADS),
                                vm[:, tt, :, 0:M_D], ALU.add).then_inc(proj_sb, 1)
            for b in range(4):
                v.wait_ge(proj_ps, 11 + b)
                v.tensor_scalar(fqT[:, b, :], bank[b % 2][:, 0:T], param[:, 12 + b:13 + b], F_D ** -0.5,
                                ALU.add, ALU.mult).then_inc(proj_sb, 1)
            for b in range(4):
                v.wait_ge(proj_ps, 15 + b)
                for j in range(2):
                    r = slice(64 * j, 64 * j + 64)
                    last = v.tensor_scalar(fkz[r, 2 * b + j, :], bank[b % 2][r, 0:T], param[r, 16 + b:17 + b], None, ALU.add)
                last.then_inc(proj_sb, 1)
            for tt in range(TT):
                v.wait_ge(proj_ps, 19 + tt)
                v.tensor_tensor(fv[:, tt, :], bank[tt % 2][:, :], fv[:, tt, :], ALU.add).then_inc(proj_sb, 1)

            def row_max(u):
                tt, heads = UNITS[u]
                k = len(heads)
                v.wait_ge(S_ps, u + 1)
                link(v.tensor_reduce(negmax[:, 4 * u:4 * u + k],
                                     bank[2 + u % 2][:, :].rearrange("p (k n) -> p k n", k=k), AX.X, ALU.max))
                v.tensor_scalar(negmax[:, 4 * u:4 * u + k], negmax[:, 4 * u:4 * u + k], -1.0, None, ALU.mult).then_inc(max_sb, 1)

            def normalise(u):
                tt, heads = UNITS[u]
                k = len(heads)
                v.wait_ge(exp_sb, u + 1)
                r = rrec[:, 4 * u:4 * u + k]
                link(v.reciprocal(r, rsum[:, 4 * u:4 * u + k]))
                pp = pr[:, u % 2, :].rearrange("p (k n) -> p k n", k=k)
                v.tensor_tensor(pp, pp, r.unsqueeze(2).to_broadcast([P, k, 512 // k]), ALU.mult).then_inc(prob_sb, 1)

            def take_turned(u):
                v.wait_ge(T_ps, u + 1)
                v.tensor_copy(PT[:, u, :], bank[4 + u % 2][:, :]).then_inc(PT_sb, 1)

            def take_values(pair):
                v.wait_ge(V_ps, pair + 1)
                v.tensor_copy(hfT[:, pair, :], bank[6 + pair % 2][:, 0:T]).then_inc(hf_sb, 1)

            def weigh(hd):
                v.wait_ge(dec_sb, 2 * hd + 2)
                if hd >= 2:
                    v.wait_ge(N_ps, hd - 1)
                v.tensor_tensor(ptm[:, hd % 2, :], bank[3][:, 0:384], dec[:, hd % 2, :], ALU.mult).then_inc(ptm_sb, 1)

            def divide(hd):
                v.wait_ge(N_ps, hd + 1)
                if hd == 0:
                    v.wait_ge(em_sb, 1)
                o = bank[4 + hd % 2][:, :].rearrange("p (a n) -> p a n", a=TT)
                den = msum[:, 2 * hd:2 * hd + 2].unsqueeze(2)
                total = o[:, :, M_D:M_D + 1]
                link(v.scalar_tensor_tensor(out=den, in0=total, scalar=-1.0, in1=em[:, :, hd:hd + 1],
                                            op0=ALU.mult, op1=ALU.max))
                link(v.tensor_tensor(den, total, den, ALU.max))
                r = rden[:, 2 * hd:2 * hd + 2]
                link(v.reciprocal(r, msum[:, 2 * hd:2 * hd + 2]))
                for tt in range(TT):
                    last = v.tensor_scalar(hml[:, tt, hd, :], o[:, tt, 0:M_D], r[:, tt:tt + 1], None, ALU.mult)
                last.then_inc(num_sb, 1)
                v.wait_ge(num_sb, hd + 1)
                for tt in range(TT):
                    link(v.bn_stats(bn6[:, 6 * tt:6 * tt + 6], hml[:, tt, hd, :]))
                    k = 2 * (tt * M_HEADS + hd)
                    v.bn_aggr(hstat[:, k:k + 2], bn6[:, 6 * tt:6 * tt + 6])

            after = {0: [], 1: ["n0"], 2: ["n1"], 3: ["n2"], 4: ["n3"], 5: ["n4"], 6: ["n5"], 7: ["w0"], 8: ["w1"],
                     10: ["w2"], 12: ["w3"]}
            kinds = {"S": row_max, "T": take_turned, "V": take_values, "N": divide, "n": normalise, "w": weigh}
            dest = [mo[:, b, :] for b in range(4)] + [gm[:, b, :] for b in range(8)] + [gf[:, b, :] for b in range(8)]
            pcol = [8 + b for b in range(4)] + [20 + b for b in range(8)] + [28 + b for b in range(8)]
            for k, steps in enumerate(STEPS):
                for s in after.get(k, []) + [s for s in steps if s[0] != "B"]:
                    kinds[s[0]](int(s[1]))
                v.wait_ge(proj_ps, 21 + k)
                v.tensor_scalar(dest[k], bank[k % 2][:, 0:T], param[:, pcol[k]:pcol[k] + 1], None, ALU.add).then_inc(proj_sb, 1)
                if k == 13:
                    v.wait_ge(proj_sb, 26)
                    v.tensor_scalar(hrstd, hstat.rearrange("p (k s) -> p k s", s=2)[:, :, 1], LN_EPS, None, ALU.add).then_inc(hvar, 1)
                if k == 15:
                    v.wait_ge(hstd, 1)
                    link(v.reciprocal(hrstd, hrstd))
                    for tt in range(TT):
                        for hd in range(M_HEADS):
                            j = tt * M_HEADS + hd
                            last = v.tensor_scalar(hml[:, tt, hd, :], hml[:, tt, hd, :], hstat[:, 2 * j:2 * j + 1],
                                                   hrstd[:, j:j + 1], ALU.subtract, ALU.mult)
                    last.then_inc(hn_sb, 1)

            v.wait_ge(gates_sig, 3)
            for hd in range(M_HEADS):
                v.wait_ge(hm_ps, hd // 2 + 1)
                ng = PARAM_ROWS["ng"] + hd
                v.scalar_tensor_tensor(out=hmT[:, hd, :], in0=bank[2 + hd // 2][:, (hd % 2) * T:(hd % 2 + 1) * T],
                                       scalar=param[:, ng:ng + 1], in1=mo[:, hd, :], op0=ALU.mult, op1=ALU.mult).then_inc(hm_sb, 1)
            yt = upad.rearrange("p b t -> p (b t)")[:, 0:2 * T].rearrange("p (b t) -> p b t", t=T)
            for f in range(KC):
                v.wait_ge(y_ps, f + 1)
                v.tensor_tensor(yT[:, f, :], bank[4 + f % 2][:, 0:T], gm[:, f, :], ALU.mult)
                link(v.tensor_tensor(yt[:, f % 2, :], bank[6 + f % 2][:, 0:T], gf[:, f, :], ALU.mult))
                v.tensor_tensor(yT[:, f, :], yT[:, f, :], yt[:, f % 2, :], ALU.add).then_inc(y_sb, 1)

            def statistics(src, tt):
                for j in range(2):
                    last = v.bn_stats(bn6[:, 12 * tt + 6 * j:12 * tt + 6 * j + 6], src(j))
                link(last)
                link(v.bn_aggr(lstat[:, 2 * tt:2 * tt + 2], bn6[:, 12 * tt:12 * tt + 12]))

            var = lstat.rearrange("p (k s) -> p k s", s=2)[:, :, 1]
            for tt in range(TT):
                for j in range(2):
                    v.wait_ge(mix_ps, 2 * tt + j + 1)
                    hs = h[:, tt, j * 512:(j + 1) * 512]
                    last = v.scalar_tensor_tensor(out=hs, in0=hs, scalar=ALPHA, in1=bank[2 * tt + j][:, :],
                                                  op0=ALU.mult, op1=ALU.add)
                link(last)
                statistics(lambda j: h[:, tt, j * 512:(j + 1) * 512], tt)
            v.tensor_scalar(lrstd, var, LN_EPS, None, ALU.add).then_inc(var1, 1)
            v.wait_ge(std1, 1)
            link(v.reciprocal(lrstd, lrstd))
            v.wait_ge(ln1_in, 32)

            def scale_and_shift(tt):
                link(v.tensor_tensor(h[:, tt, :], h[:, tt, :], ln_g, ALU.mult))
                return v.tensor_tensor(h[:, tt, :], h[:, tt, :], ln_b, ALU.add)

            for tt in range(TT):
                link(v.tensor_scalar(h[:, tt, :], h[:, tt, :], lstat[:, 2 * tt:2 * tt + 1], lrstd[:, tt:tt + 1],
                                     ALU.subtract, ALU.mult))
                scale_and_shift(tt).then_inc(h1_sb, 1)
            for g in (0, 1):
                v.wait_ge(hT_ps, g + 1)
                v.tensor_copy(hT[:, 2 * g:2 * g + 2, :], bank[4 + g][:, :].rearrange("p (c t) -> p c t", t=T)).then_inc(hT_v, 1)

            v.wait_ge(lg_ps, 1)
            v.wait_ge(br_in, 16)
            v.wait_ge(iotas, 1)
            link(v.tensor_tensor(lg, bank[0][:, 0:TT * E].rearrange("p (a e) -> p a e", a=TT),
                                 br.unsqueeze(1).to_broadcast([P, TT, E]), ALU.add))
            for tt in range(TT):
                link(v.max(top8[:, tt, :], lg[:, tt, :]))
                last = v.max_index(idx8[:, tt, :].bitcast(U32), top8[:, tt, :], lg[:, tt, :])
            link(last)
            v.tensor_scalar(ntop.unsqueeze(2), top8[:, :, 0:1], -1.0, None, ALU.mult).then_inc(lgmax, 1)
            link(v.tensor_copy(idxf, idx8.bitcast(U32)))
            for k in range(TOP_K):
                for tt in range(TT):
                    i_k = idxf[:, tt, k:k + 1]
                    if k == 0:
                        last = v.tensor_scalar(mask[:, tt, :], iota_e, i_k, None, ALU.is_equal)
                    else:
                        last = v.scalar_tensor_tensor(out=mask[:, tt, :], in0=iota_e, scalar=i_k, in1=mask[:, tt, :],
                                                      op0=ALU.is_equal, op1=ALU.add)
                link(last)
            v.tensor_copy(mask3[:, :, :, :], mask.unsqueeze(2).to_broadcast([P, TT, 3, E])).then_inc(mask_sb, 1)
            v.wait_ge(gexp_sb, 1)
            link(v.tensor_tensor(gexp, gexp, mask, ALU.mult))
            link(v.tensor_reduce(gsum, gexp, AX.X, ALU.add))
            link(v.reciprocal(gsum, gsum))
            v.tensor_tensor(gpg[:, :, E:2 * E], gexp, gsum.unsqueeze(2).to_broadcast([P, TT, E]), ALU.mult)
            v.wait_ge(cnt_ps, 3)
            v.tensor_scalar(slot1, bank[2][:, 0:TT * E].rearrange("p (a e) -> p a e", a=TT), 1.0, None, ALU.add)
            link(v.tensor_copy(cnt[0:96, :], bank[1][0:96, 0:1]))
            link(v.tensor_scalar(nb[0:96, :], cnt[0:96, :], float(SLOTS), 1.0, ALU.is_gt, ALU.add))
            for k in range(2, T // SLOTS):
                link(v.scalar_tensor_tensor(out=nb[0:96, :], in0=cnt[0:96, :], scalar=float(k * SLOTS), in1=nb[0:96, :],
                                            op0=ALU.is_gt, op1=ALU.add))
            v.tensor_copy(nbb[:, :], nb[0:96, :])
            v.tensor_copy(nbB[:, :], nb[0:32, :].to_broadcast([32, P])).then_inc(nb_sb, 1)
            v.wait_ge(end_ps, 1)
            link(v.tensor_copy(start_sb, bank[0][:, 0:E]))
            link(v.tensor_tensor(slot1, slot1, start_sb.unsqueeze(1).to_broadcast([P, TT, E]), ALU.add))
            v.tensor_tensor(gpg[:, :, 0:E], slot1, mask, ALU.mult).then_inc(gpg_sb, 1)
            link(v.tensor_copy(cnt[0:96, :], bank[1][0:96, 1:2]))
            link(v.tensor_tensor(st_col[0:96, :], cnt[0:96, :], nb[0:96, :], ALU.subtract))
            link(v.tensor_scalar(ownT[0:96, :], iota_item[0:96, :], cnt[0:96, :], None, ALU.is_lt))
            link(v.scalar_tensor_tensor(out=own[0:96, :], in0=iota_item[0:96, :], scalar=st_col[0:96, :],
                                        in1=ownT[0:96, :], op0=ALU.is_ge, op1=ALU.mult))
            v.tensor_copy(n_items[:, :], bank[3][0:1, 0:1]).then_inc(tables, 1)
            v.tensor_copy(own_b[:, :], own[0:32, :]).then_inc(own_sb, 1)
            v.wait_ge(gpgT_ps, 1)
            v.tensor_copy(gpgT, bank[0][0:64, 64:64 + T].rearrange("p (a t) -> p a t", a=TT)).then_inc(gpgT_sb, 1)
            v.wait_ge(item_ps, 1)
            v.tensor_copy(expert_row[:, :], bank[3][0:1, 0:ITEMS]).then_inc(tables, 1)
            v.tensor_tensor(local, bank[1][:, 0:TT * ITEMS].rearrange("p (a i) -> p a i", a=TT),
                            item_off.unsqueeze(1).to_broadcast([P, TT, ITEMS]), ALU.subtract)
            link(v.tensor_copy(igate, bank[2][:, 0:TT * ITEMS].rearrange("p (a i) -> p a i", a=TT)))

            def pick_tokens(i):
                for tt in range(TT):
                    last = v.tensor_scalar(pick[:, tt, :], iota_slot, local[:, tt, bass.ds(i, 1)], None, ALU.is_equal)
                last.then_inc(pick_sb, 1)

            def gate_tokens(i):
                for tt in range(TT):
                    for j in range(2):
                        last = v.tensor_scalar(gated[:, tt, 64 * j:64 * j + 64], iota_slot, local[:, tt, bass.ds(i, 1)],
                                               igate[:, tt, bass.ds(i, 1)], ALU.is_equal, ALU.mult)
                last.then_inc(gated_sb, 1)

            def select_bias(i):
                v.tensor_scalar(selb, ones_b[0:96, 0:SLOTS], own[0:96, bass.ds(i, 1)], None, ALU.mult).then_inc(selb_sb, 1)

            v.wait_ge(tables, 2)
            n = v.value_load(n_items[0:1, 0:1], min_val=E, max_val=MAX_ITEMS)
            pick_tokens(0)
            gate_tokens(0)
            select_bias(0)
            v.memset(ydn, 0.0).then_inc(ydn_sb, 1)
            v.memset(gatedT, 0.0).then_inc(gatedT_sb, 1)
            v.memset(actT, 0.0).then_inc(actT_sb, 1)
            with v.Fori(0, n) as i:
                v.wait_ge(xg_ps, i + 1)
                pick_tokens(i + 1)
                v.wait_ge(released, i * RING + GU_SLOTS)
                v.tensor_scalar(glu, bank[0][:, :], SW_LIMIT, None, ALU.min).then_inc(glu_sb, 1)
                v.tensor_scalar(lin, bank[1][:, :], SW_LIMIT, -SW_LIMIT, ALU.min, ALU.max).then_inc(moe_v, 1)
                v.wait_ge(moe_v, i * 2 + 1)
                v.scalar_tensor_tensor(out=half_act, in0=lin, scalar=1.0, in1=glu, op0=ALU.add, op1=ALU.mult).then_inc(moe_v, 1)
                v.wait_ge(moe_v, i * 2 + 2)
                v.wait_ge(sig_sb, i + 1)
                v.tensor_tensor(act, half_act, sig, ALU.mult).then_inc(act_sb, 1)
                v.wait_ge(tr_ps, i + 1)
                v.tensor_copy(actT, bank[0][:, :].rearrange("p (c s) -> p c s", s=P)).then_inc(actT_sb, 1)
                gate_tokens(i + 1)
                v.wait_ge(released, i * RING + RING)
                select_bias(i + 1)

            v.wait_ge(scat_ps, n + 1)
            for tt in range(TT):
                statistics(lambda j: bank[4 + 2 * tt + j][:, :], tt)
            v.tensor_scalar(lrstd, var, LN_EPS, None, ALU.add).then_inc(var2, 1)
            v.wait_ge(std2, 1)
            link(v.reciprocal(lrstd, lrstd))
            v.wait_ge(ln2_in, 32)
            for tt in range(TT):
                for j in range(2):
                    last = v.tensor_scalar(h[:, tt, j * 512:(j + 1) * 512], bank[4 + 2 * tt + j][:, :],
                                           lstat[:, 2 * tt:2 * tt + 1], lrstd[:, tt:tt + 1], ALU.subtract, ALU.mult)
                link(last)
                scale_and_shift(tt).then_inc(fin_sb, 1)


NAMES = ["x", "w_in", "b_in", "m_conv_w", "m_conv_b", "m_norm_g", "w_bm", "w_bf", "w_o", "ln1_g", "ln1_b",
         "w_router", "b_router", "w_gu", "b_gu", "w_dn", "b_dn", "ln2_g", "ln2_b"]


def kernel(**inputs):
    import concourse.bacc as bacc
    import numpy as np
    from concourse.bass_utils import run_bass_kernel_spmd

    nc = bacc.Bacc("TRN2", target_bir_lowering=False, num_devices=1)
    arrays, args = {}, {}
    for name in NAMES:
        a = np.ascontiguousarray(inputs[name])
        arrays[f"in_{name}"] = a
        args[name] = nc.dram_tensor(f"in_{name}", a.shape, mybir.dt.from_np(a.dtype), kind="ExternalInput").ap()
    out = nc.dram_tensor("out_h", (1, T, D), F32, kind="ExternalOutput").ap()
    build(nc, out=out, **args)
    r = run_bass_kernel_spmd(nc, [arrays], core_ids=[0])
    return r.results[0]["out_h"]
```

```python
from contextlib import ExitStack

import concourse.bass as bass
from concourse import mybir

F32 = mybir.dt.float32
BF16 = mybir.dt.bfloat16
F32R = mybir.dt.float32r
I32 = mybir.dt.int32
U32 = mybir.dt.uint32
ALU = mybir.AluOpType
ACT = mybir.ActivationFunctionType
AX = mybir.AxisListType

P = 128
D = 1024
T = 256
TT = T // P
KC = D // P
M_HEADS, M_D = 4, 128
F_HEADS, F_D = 8, 64
CONV_W = 4
E = 32
TOP_K = 4
D_FF = 1024
SLOTS = 64
MAX_ITEMS = T * TOP_K // SLOTS + E - 1
ITEMS = MAX_ITEMS + 1
ALPHA = 2.0 ** 0.25
LN_EPS = 1e-5
SW_ALPHA, SW_LIMIT = 1.702, 7.0
NEG = -1e30
MQK, MV, MO, MI, MF, FQ, FK, FV, FF, GM, GF = 0, 1024, 1536, 2048, 2052, 2056, 2568, 3080, 3592, 3600, 4624

GROUPS = [MQK, MQK + 512, MV, FQ, FK, FV, MO, GM, GM + 512, GF, GF + 512]
TOKEN_MAJOR = {2, 5}
W_BM, W_BF, W_O0, W_O1, WO_MID = 11, 12, 13, 14, 15
RAW_REGIONS = 3
REGIONS = 6
RWORDS = KC * 512
ARENA = 9372
SLOT_WORDS = 2 * D_FF
SLOTS_E = 12
HALF = SLOTS_E // 2
THIRD = HALF * SLOT_WORDS
GU_SLOTS = KC

SPLITS = 4
TAIL = ["Y0", "Y1", "Y2", "O0", "Y3", "O1", "Y4", "O2", "Y5", "O3", "Y6", "Y7", "O4", "O5", "O6", "O7"]
TAIL_AT = 4 * len(GROUPS)
N_SPLIT = TAIL_AT + len(TAIL)
BLOCK_UNIT, BLOCK_BANK = [], []
for _g in range(len(GROUPS)):
    if _g in TOKEN_MAJOR:
        BLOCK_UNIT += [4 * _g + 3] * TT
        BLOCK_BANK += [6, 7]
    else:
        BLOCK_UNIT += [4 * _g + q for q in range(4)]
        BLOCK_BANK += [0, 1, 0, 1]


def tail_unit(name):
    return TAIL_AT + TAIL.index(name)


def last_unit(n):
    return 4 * n + 3 if n < 11 else tail_unit({W_BM: "Y7", W_BF: "Y7", W_O0: "O3", W_O1: "O7"}[n])


UNITS = [(1, [2 * u, 2 * u + 1]) for u in range(4)] + [(0, [0, 1, 2, 3]), (0, [4, 5, 6, 7])]

STEPS = [
    ["S0"], ["S1"], ["T0", "S2"], ["T1", "S3"], ["T2", "S4"], ["T3", "S5"], ["T4", "B0"], ["T5", "B1"],
    ["N0", "V0"], ["B2", "V1"], ["N1", "V2"], ["B3", "V3"], ["N2"], ["N3"], [], [], [], [], [], [],
]

PARAM_ROWS = dict(mqk=0, mo=8, fq=12, fk=16, gm=20, gf=28, cw=36, cb=68, ng=76)
N_PARAM = 80


def build(nc, x, w_in, b_in, m_conv_w, m_conv_b, m_norm_g, w_bm, w_bf, w_o, ln1_g, ln1_b,
          w_router, b_router, w_gu, b_gu, w_dn, b_dn, ln2_g, ln2_b, out):
    with ExitStack() as ctx:
        def sb(name, shape, dt=F32):
            return ctx.enter_context(nc.sbuf_tensor(name, shape, dt))

        def sem(name):
            return ctx.enter_context(nc.semaphore(name))

        bank = [ctx.enter_context(nc.psum_tensor(f"bank{b}", [P, 512], F32)) for b in range(8)]

        with ExitStack() as early:
            early.enter_context(nc.sbuf_tensor("below_split", [P, 2 * THIRD], F32))
            split = early.enter_context(nc.sbuf_tensor("split", [P, THIRD], F32R))
        with ExitStack() as early:
            early.enter_context(nc.sbuf_tensor("below_heads", [P, THIRD - 4096], F32))
            heads_split = early.enter_context(nc.sbuf_tensor("heads_split", [P, 4096], F32R))
        ring = sb("ring", [P, 3 * THIRD])
        first = ring[:, 0:THIRD]
        arena = sb("arena", [P, ARENA])
        place, at = [first], [0]

        def parts(words, n, t):
            w = n * t
            return [words[:, k * w:(k + 1) * w].rearrange("p (b t) -> p b t", t=t) for k in range(2)]

        x_hi, x_lo = parts(split[:, 0:2 * KC * T], KC, T)
        y_hi, y_lo = x_hi, x_lo
        w_split = [split[:, 2 * KC * T + 2 * KC * P * k:2 * KC * T + 2 * KC * P * (k + 1)] for k in range(SPLITS)]
        wo_mid = sb("wo_mid", [P, 2 * D])
        hm_hi, hm_lo = parts(heads_split[:, 0:2048], 4, T)
        hf_hi, hf_lo = parts(heads_split[:, 2048:4096], 4, T)

        def region(n):
            o = THIRD + (n % RAW_REGIONS) * RWORDS
            return ring[:, o:o + RWORDS]

        def raw_pieces(k):
            if k < TAIL_AT:
                g, q = k // 4, k % 4
                w = region(g).rearrange("p (c n) -> p c n", n=512)
                return g, [w[:, 2 * q:2 * q + 2, :] if g in TOKEN_MAJOR else w[:, :, q * P:(q + 1) * P]]
            kind, f = TAIL[k - TAIL_AT][0], int(TAIL[k - TAIL_AT][1])
            if kind == "Y":
                return W_BF, [region(n).rearrange("p (c n) -> p c n", n=D)[:, :, f * P:(f + 1) * P] for n in (W_BM, W_BF)]
            if f // 2 == 2:
                return WO_MID, [wo_mid[:, (f % 2) * D:(f % 2 + 1) * D]]
            n = W_O0 + f // 4
            return n, [region(n).rearrange("p (c n) -> p c n", n=D)[:, f % 4, :]]

        def split_pieces(k, part):
            w = w_split[k % SPLITS][:, part * KC * P:(part + 1) * KC * P]
            if k < TAIL_AT and k // 4 in TOKEN_MAJOR:
                return [w.rearrange("p (c n) -> p c n", n=512)]
            if k < TAIL_AT:
                return [w.rearrange("p (c n) -> p c n", n=P)]
            if TAIL[k - TAIL_AT][0] == "Y":
                return [w[:, b * 512:(b + 1) * 512].rearrange("p (c n) -> p c n", n=P) for b in range(2)]
            return [w]

        def slot(half, k):
            o = half % 3 * THIRD + k % HALF * SLOT_WORDS
            return ring[:, o:o + SLOT_WORDS]

        h = sb("h", [P, TT, D])
        bias3 = sb("bias3", [96, 3 * D], BF16)
        ident = sb("ident", [P, P])
        aident = sb("aident", [P, P])
        maskT = sb("maskT", [P, P], BF16)
        maskS = sb("maskS", [P, P], BF16)
        identb = sb("identb", [P, P], BF16)
        ones_b = sb("ones_b", [P, P], BF16)
        below = sb("below", [P, P], BF16)
        upto3 = sb("upto3", [32, 3, 32], BF16)
        start64 = sb("start64", [32, 32], BF16)
        param = sb("param", [P, N_PARAM])
        gbias = sb("gbias", [P, 1])
        wr = sb("wr", [P, KC, E])

        def take(words):
            at[0] += words
            return place[0][:, at[0] - words:at[0]]

        pt_words = take(6 * 512)
        PT = pt_words.rearrange("p (u n) -> p u n", n=512)
        bias_raw = pt_words[0:96, :]
        p_words = take(1024)
        pr = p_words.rearrange("p (b n) -> p b n", n=512)
        wg = p_words[:, 0:KC * 96].rearrange("p (c n) -> p c n", n=96)
        ones256 = p_words[0:64, KC * 96:KC * 96 + T]
        d_words = take(4 * 384)
        dec = d_words[:, 0:768].rearrange("p (b n) -> p b n", n=384)
        ptm = d_words[:, 768:1536].rearrange("p (b n) -> p b n", n=384)
        param_raw = d_words[0:N_PARAM, 0:P]
        tmp_rows = d_words[0:64, 512:512 + 4 * T].rearrange("p (k t) -> p k t", t=T)
        hml_words = take(1024)
        hml = hml_words.rearrange("p (a h d) -> p a h d", a=TT, h=M_HEADS)
        cv = hml_words[:, 0:512].rearrange("p (b t) -> p b t", t=T)
        sg_c = hml_words[:, 512:1024].rearrange("p (b t) -> p b t", t=T)
        rowM, rowF = take(T), take(T)
        fqT = take(1024).rearrange("p (b t) -> p b t", t=T)
        hfT = fqT
        assert at[0] == 4 * SLOT_WORDS
        qk = take(2048).rearrange("p (b t) -> p b t", t=T)
        fkz = take(2048).rearrange("p (b t) -> p b t", t=T)
        assert at[0] == THIRD

        place[0], at[0] = arena, 0
        ln_g, ln_b = wo_mid[:, 0:D], wo_mid[:, D:2 * D]
        moe_at = at[0]
        gm = take(2048).rearrange("p (b t) -> p b t", t=T)
        gf = take(2048).rearrange("p (b t) -> p b t", t=T)
        mo = take(1024).rearrange("p (b t) -> p b t", t=T)
        hmT = mo
        hT = gf
        moe_end, route_at = at[0], at[0]
        vm = take(TT * M_HEADS * (M_D + 1)).rearrange("p (a h d) -> p a h d", a=TT, h=M_HEADS)
        fv = take(TT * 512).rearrange("p (a n) -> p a n", a=TT)
        sel = take(F_HEADS * P).rearrange("p (h m) -> p h m", m=P)
        route_end = at[0]
        rowpack = take(T)
        upad = take(2 * (T + 4)).rearrange("p (b t) -> p b t", b=2)
        small = take(256)
        negmax = small[:, 0:32]
        rsum = small[:, 32:64]
        rrec = small[:, 64:96]
        msum = small[:, 96:128]
        hstat = small[:, 128:128 + 16]
        hrstd = small[:, 144:152]
        rden = small[:, 152:160]
        bn6 = small[:, 160:160 + 24]
        lstat = small[:, 184:184 + 4]
        lrstd = small[:, 188:190]
        colT = take(TT * 64).rearrange("p (a r) -> p a r", a=TT)
        em = take(8).rearrange("p (a h) -> p a h", a=TT)
        assert at[0] <= ARENA, at[0]

        at[0] = moe_at
        xgT = take(512).rearrange("p (c s) -> p c s", s=SLOTS)
        glu, sig, lin, half_act, act = (take(512) for _ in range(5))
        actT = take(512).rearrange("p (c s) -> p c s", s=P)
        ydn = take(512)
        pick = take(TT * SLOTS).rearrange("p (a s) -> p a s", a=TT)
        gated = take(TT * P).rearrange("p (a s) -> p a s", a=TT)
        gatedT = take(TT * P).rearrange("p (a t) -> p a t", a=TT)
        selb_w = take(SLOTS // 2)
        assert at[0] <= moe_end
        selb = selb_w.bitcast(BF16)[0:96, :]

        at[0] = route_at
        lg = take(TT * E).rearrange("p (a e) -> p a e", a=TT)
        br = take(E)
        top8 = take(TT * 8).rearrange("p (a k) -> p a k", a=TT)
        idx8 = take(TT * 8).rearrange("p (a k) -> p a k", a=TT)
        idxf = take(TT * 8).rearrange("p (a k) -> p a k", a=TT)
        ntop = take(2)
        gsum = take(2)
        mask = take(TT * E).rearrange("p (a e) -> p a e", a=TT)
        gexp = take(TT * E).rearrange("p (a e) -> p a e", a=TT)
        gpg = take(TT * 64).rearrange("p (a r) -> p a r", a=TT)
        gpgT = take(T).rearrange("p (a t) -> p a t", a=TT)[0:64]
        iota_e = take(E)
        iota_slot = take(SLOTS)
        iota_item = take(ITEMS)
        item_off = take(ITEMS)
        cnt = take(1)
        nb = take(1)
        st_col = take(1)
        start_sb = take(E)
        ownT = take(ITEMS)
        own = take(ITEMS)
        local = take(TT * ITEMS).rearrange("p (a i) -> p a i", a=TT)
        igate = take(TT * ITEMS).rearrange("p (a i) -> p a i", a=TT)
        slot1 = take(TT * E).rearrange("p (a e) -> p a e", a=TT)
        assert at[0] <= route_end, (at[0], route_end)
        mask3 = sb("mask3", [P, TT, 3, E], BF16)
        nbb = sb("nbb", [96, 1], BF16)
        nbB = sb("nbB", [32, P], BF16)
        table = upad.rearrange("p b t -> p (b t)")[0:1, :].bitcast(I32)
        items_end = table[:, 0:E + 1]
        last_item = table[:, E + 1:2 * E + 1]

        x_in = sem("x_in"); wg_in = sem("wg_in"); par_in = sem("par_in"); gb_in = sem("gb_in")
        bias_in = sem("bias_in"); vb_in = sem("vb_in"); wr_in = sem("wr_in"); br_in = sem("br_in")
        ln1_in = sem("ln1_in"); ln2_in = sem("ln2_in")
        blk_in = [sem(f"blk_in{n}") for n in range(16)]
        half_in = [sem(f"half_in{b}") for b in range(2)]
        hi_sb = sem("hi_sb"); lo_sb = sem("lo_sb"); unit_used = sem("unit_used")
        slot_in = [sem(f"slot_in{k}") for k in range(SLOTS_E)]
        out_done = sem("out_done")
        consts = sem("consts"); pool_chain = sem("pool_chain"); wg_zero = sem("wg_zero")
        bias3_done = sem("bias3_done"); iotas = sem("iotas")
        xT_ps = sem("xT_ps"); par_ps = sem("par_ps"); gate_ps = sem("gate_ps"); col_ps = sem("col_ps")
        S_ps = sem("S_ps"); T_ps = sem("T_ps"); V_ps = sem("V_ps")
        B_ps = sem("B_ps"); N_ps = sem("N_ps"); hm_ps = sem("hm_ps"); mix_ps = sem("mix_ps")
        hT_ps = sem("hT_ps"); lg_ps = sem("lg_ps"); cnt_ps = sem("cnt_ps"); end_ps = sem("end_ps")
        gpgT_ps = sem("gpgT_ps"); item_ps = sem("item_ps")
        released = sem("released")
        scat_ps = sem("scat_ps"); xg_ps = sem("xg_ps"); tr_ps = sem("tr_ps"); dn_ps = sem("dn_ps")
        x_hi_sb = sem("x_hi_sb"); x_lo_sb = sem("x_lo_sb"); xT_a = sem("xT_a"); hf_hi_sb = sem("hf_hi_sb")
        hf_lo_sb = sem("hf_lo_sb"); hm_hi_sb = sem("hm_hi_sb"); hm_lo_sb = sem("hm_lo_sb"); par_sb = sem("par_sb"); u_sb = sem("u_sb"); qk_sb = sem("qk_sb")
        proj_sb = sem("proj_sb"); logexp = sem("logexp"); z_sb = sem("z_sb"); rows_sb = sem("rows_sb")
        col_sb = sem("col_sb"); em_sb = sem("em_sb"); conv_sb = sem("conv_sb"); csig = sem("csig")
        max_sb = sem("max_sb"); exp_sb = sem("exp_sb"); prob_sb = sem("prob_sb"); PT_sb = sem("PT_sb")
        hf_sb = sem("hf_sb"); dec_sb = sem("dec_sb"); ptm_sb = sem("ptm_sb"); num_sb = sem("num_sb")
        hvar = sem("hvar"); heads_stat = sem("heads_stat"); hstd = sem("hstd"); hn_sb = sem("hn_sb"); gates_sig = sem("gates_sig"); hm_sb = sem("hm_sb")
        y_sb = sem("y_sb"); var1 = sem("var1"); std1 = sem("std1"); h1_sb = sem("h1_sb")
        hT_v = sem("hT_v"); hT_a = sem("hT_a"); lgmax = sem("lgmax"); gexp_sb = sem("gexp_sb")
        mask_sb = sem("mask_sb"); nb_sb = sem("nb_sb"); gpg_sb = sem("gpg_sb"); gpgT_sb = sem("gpgT_sb"); own_sb = sem("own_sb")
        tables = sem("tables")
        v_chain = sem("v_chain"); a_chain = sem("a_chain")
        pick_sb = sem("pick_sb"); gated_sb = sem("gated_sb"); selb_sb = sem("selb_sb")
        glu_sb = sem("glu_sb"); sig_sb = sem("sig_sb"); act_sb = sem("act_sb"); moe_v = sem("moe_v")
        xg_sb = sem("xg_sb"); actT_sb = sem("actT_sb"); gatedT_sb = sem("gatedT_sb"); ydn_sb = sem("ydn_sb")
        var2 = sem("var2"); std2 = sem("std2"); fin_sb = sem("fin_sb")

        def chunks(w):
            return w.rearrange("(c p) n -> p c n", p=P)

        def rows(v):
            return v.rearrange("(r p) -> r p", p=P)

        win = w_in[0]
        bin_ = b_in[0]

        block = ctx.enter_context(nc.Block())

        @block.sync
        def _(sp):
            for tt in range(TT):
                sp.dma_start(h[:, tt, :], x[0, tt * P:(tt + 1) * P, :]).then_inc(x_in, 16)

            def load_block(n):
                if n == WO_MID:
                    sp.dma_start(wo_mid[:, :].rearrange("p (c n) -> p c n", n=D), chunks(w_o[0][512:768, :])).then_inc(blk_in[n], 16)
                elif n == W_O1:
                    sp.dma_start(region(n).rearrange("p (c n) -> p c n", n=D)[:, 2:4, :],
                                 chunks(w_o[0][768:D, :])).then_inc(blk_in[n], 16)
                elif n == 0:
                    for b in range(2):
                        o = GROUPS[0] + 256 * b
                        sp.dma_start(region(n).rearrange("p (c n) -> p c n", n=512)[:, :, 256 * b:256 * b + 256],
                                     chunks(win[:, o:o + 256])).then_inc(half_in[b], 16)
                elif n < 11:
                    sp.dma_start(region(n).rearrange("p (c n) -> p c n", n=512),
                                 chunks(win[:, GROUPS[n]:GROUPS[n] + 512])).then_inc(blk_in[n], 16)
                else:
                    src = {W_BM: w_bm[0], W_BF: w_bf[0], W_O0: w_o[0][0:512, :]}[n]
                    sp.dma_start(region(n).rearrange("p (c n) -> p c n", n=D), chunks(src)).then_inc(blk_in[n], 16)

            load_block(0)
            sp.wait_ge(wg_zero, 1)
            for dst, src, n in ((0, MF, 4), (32, FF, 8), (64, MI, 4)):
                sp.dma_start(wg[:, :, dst:dst + n], chunks(win[:, src:src + n])).then_inc(wg_in, 16)
                sp.dma_start(gbias[dst:dst + n, :], bin_[src:src + n].rearrange("(p a) -> p a", a=1)).then_inc(gb_in, 16)
            for name, src in (("mqk", bin_[MQK:MQK + 1024]), ("mo", bin_[MO:MO + 512]), ("fq", bin_[FQ:FQ + 1024]),
                              ("gm", bin_[GM:GM + 2048]), ("cw", m_conv_w[0].rearrange("j n -> (j n)")),
                              ("cb", m_conv_b[0]), ("ng", m_norm_g[0])):
                r = PARAM_ROWS[name]
                src = rows(src)
                sp.dma_start(param_raw[r:r + src.shape[0], :], src).then_inc(par_in, 16)

            load_block(1)
            load_block(2)
            for g in range(3):
                sp.dma_start(bias_raw[32 * g:32 * g + 32, 0:2 * D], b_gu[0]).then_inc(bias_in, 16)
                sp.dma_start(bias_raw[32 * g:32 * g + 32, 2 * D:3 * D], b_dn[0]).then_inc(bias_in, 16)
            for tt in range(TT):
                sp.dma_start(vm[:, tt, :, 0:M_D], bin_[MV:MV + 512].rearrange("(a h d) -> a h d", a=1, h=M_HEADS)
                             .to_broadcast([P, M_HEADS, M_D])).then_inc(vb_in, 16)
                sp.dma_start(fv[:, tt, :], bin_[FV:FV + 512].rearrange("(a n) -> a n", a=1)
                             .to_broadcast([P, 512])).then_inc(vb_in, 16)
            sp.dma_start(wr[:, :, :], chunks(w_router[0])).then_inc(wr_in, 16)

            def load_when_split(n):
                sp.wait_ge(lo_sb, last_unit(n - RAW_REGIONS) + 1)
                load_block(n)

            load_block(WO_MID)
            for n in range(3, W_O1):
                load_when_split(n)
            sp.wait_ge(N_ps, M_HEADS)
            sp.wait_ge(V_ps, 4)
            sp.dma_start(br, b_router[0:1, :].to_broadcast([P, E])).then_inc(br_in, 16)
            def load_slot(k, e, half):
                dst = slot(half, k)
                if k < GU_SLOTS:
                    src = w_gu[0, e, k * P:(k + 1) * P, :] if isinstance(e, int) else \
                        w_gu[0][bass.ds(e, 1), k * P:(k + 1) * P, :].rearrange("a p n -> p (a n)")
                    sp.dma_start(dst, src).then_inc(slot_in[k], 16)
                else:
                    f0 = (k - GU_SLOTS) * 2 * P
                    src = chunks(w_dn[0, e, f0:f0 + 2 * P, :]) if isinstance(e, int) else \
                        w_dn[0][bass.ds(e, 1), f0:f0 + 2 * P, :].rearrange("a (c p) n -> p (a c) n", p=P)
                    sp.dma_start(dst.rearrange("p (c n) -> p c n", n=D), src).then_inc(slot_in[k], 16)

            sp.wait_ge(hm_ps, 2)
            sp.wait_ge(hf_lo_sb, 1)
            for k in range(4):
                load_slot(k, 0, 0)
            load_when_split(W_O1)
            for n in (W_BF, W_O0):
                sp.wait_ge(lo_sb, last_unit(n) + 1)
                for k in range(HALF + 2 * (n % RAW_REGIONS), HALF + 2 * (n % RAW_REGIONS) + 2):
                    load_slot(k, 0, 1)
            sp.wait_ge(lo_sb, tail_unit("O5") + 1)
            sp.dma_start(ln_g, ln1_g[0:1, :].to_broadcast([P, D])).then_inc(ln1_in, 16)
            sp.dma_start(ln_b, ln1_b[0:1, :].to_broadcast([P, D])).then_inc(ln1_in, 16)
            sp.wait_ge(unit_used, tail_unit("Y7") + 1)
            for k in (4, 5):
                load_slot(k, 0, 0)
            sp.wait_ge(lo_sb, N_SPLIT)
            for k in (SLOTS_E - 2, SLOTS_E - 1):
                load_slot(k, 0, 1)
            sp.wait_ge(mix_ps, 2 * TT)
            for k in range(HALF):
                sp.wait_ge(slot_in[k], 16)
                load_slot(k, 1, 2)
            sp.wait_ge(h1_sb, 2 * TT)
            sp.dma_start(ln_g, ln2_g[0:1, :].to_broadcast([P, D])).then_inc(ln2_in, 16)
            sp.dma_start(ln_b, ln2_b[0:1, :].to_broadcast([P, D])).then_inc(ln2_in, 16)
            sp.wait_ge(tables, 1)

            def load_half(e, loaded, first, half, e_last):
                last = sp.value_load(last_item[0:1, bass.ds(e_last, 1)], min_val=0, max_val=MAX_ITEMS - 1)
                for k in range(first, first + HALF):
                    sp.wait_ge(slot_in[k], loaded)
                for k in range(first, first + HALF):
                    sp.wait_ge(released, last * SLOTS_E + ((k + HALF) % SLOTS_E + 1))
                    load_slot(k, e, half)

            load_half(1, 16, HALF, 0, 0)
            with sp.Fori(0, (E - 2) // 3) as j:
                for step in range(3):
                    e = j * 3 + (2 + step)
                    load_half(e, j * 48 + 16 * (2 + step), 0, 2 * (2 + step), j * 3 + step)
                    load_half(e, j * 48 + 16 * (2 + step), HALF, 2 * (2 + step) + 1, j * 3 + (step + 1))
            for tt in range(TT):
                sp.wait_ge(fin_sb, tt + 1)
                sp.dma_start(out[0, tt * P:(tt + 1) * P, :], h[:, tt, :]).then_inc(out_done, 16)
            sp.wait_ge(out_done, 16 * TT)

        @block.gpsimd
        def _(pool):
            count = [0]

            def link(ins):
                count[0] += 1
                ins.then_inc(pool_chain, 1)
                pool.wait_ge(pool_chain, count[0])

            pool.memset(gbias[:, :], 0.0)
            pool.memset(wg, 0.0).then_inc(wg_zero, 1)
            pool.memset(ident[:, :], 0.0)
            pool.memset(maskT[:, :], 0.0)
            pool.memset(maskS[:, :], 0.0)
            pool.memset(below[:, :], 1.0)
            pool.memset(upto3[:, :, :], 1.0)
            pool.memset(start64[:, :], float(SLOTS))
            link(pool.memset(sel, 0.0))
            pool.affine_select(out=ident[:, :], in_=ident[:, :], compare_op=ALU.not_equal, fill=1.0, base=0,
                               pattern=[[-1, P]], channel_multiplier=1).then_inc(consts, 1)
            pool.memset(ones_b[:, :], 1.0)
            pool.memset(ones256, 1.0)
            pool.affine_select(out=maskT[:, :], in_=maskT[:, :], compare_op=ALU.is_ge, fill=NEG, base=0,
                               pattern=[[1, P]], channel_multiplier=-1)
            pool.affine_select(out=maskS[:, :], in_=maskS[:, :], compare_op=ALU.is_ge, fill=NEG, base=0,
                               pattern=[[-1, P]], channel_multiplier=1)
            pool.affine_select(out=sel, in_=sel, compare_op=ALU.not_equal, fill=1.0, base=0,
                               pattern=[[-1, F_HEADS], [0, P]], channel_multiplier=1)
            pool.affine_select(out=below[:, :], in_=below[:, :], compare_op=ALU.is_gt, fill=0.0, base=0,
                               pattern=[[1, P]], channel_multiplier=-1)
            pool.affine_select(out=upto3[:, :, :], in_=upto3[:, :, :], compare_op=ALU.is_ge, fill=0.0, base=0,
                               pattern=[[0, 3], [1, 32]], channel_multiplier=-1)
            pool.affine_select(out=start64[:, :], in_=start64[:, :], compare_op=ALU.is_gt, fill=0.0, base=0,
                               pattern=[[1, 32]], channel_multiplier=-1)
            pool.memset(rowpack, 0.0)
            pool.memset(rowM, 0.0)
            link(pool.memset(rowF, 0.0))
            pool.tensor_copy(identb[:, :], ident[:, :])
            pool.tensor_scalar(aident[:, :], ident[:, :], ALPHA, None, ALU.mult)
            pool.memset(fkz, 0.0)
            for b in range(2):
                pool.memset(upad[:, b, 0:4], 0.0)
            pool.memset(vm[:, :, :, M_D:M_D + 1], 1.0).then_inc(consts, 1)
            pool.wait_ge(consts, 2)
            pool.wait_ge(bias_in, 96)
            link(pool.tensor_copy(bias3[:, :], bias_raw))
            for first in (32, 64):
                for g in range(first, 96, 32):
                    rest = pool.tensor_tensor(bias_raw[g:g + 32, :], bias_raw[g:g + 32, :], bias3[g:g + 32, :], ALU.subtract)
                link(rest)
                for g in range(first, 96, 32):
                    last = pool.tensor_copy(bias3[g:g + 32, :], bias_raw[g:g + 32, :])
                if first == 32:
                    link(last)
            last.then_inc(bias3_done, 1)
            pool.wait_ge(N_ps, M_HEADS)
            pool.wait_ge(V_ps, 4)
            kw = dict(allow_small_or_imprecise_dtypes=True, channel_multiplier=0)
            pool.iota(iota_e, pattern=[[1, E]], base=0, **kw)
            pool.iota(iota_slot, pattern=[[1, SLOTS]], base=0, **kw)
            pool.iota(iota_item, pattern=[[1, ITEMS]], base=0, **kw)
            pool.iota(item_off, pattern=[[SLOTS, ITEMS]], base=1, **kw).then_inc(iotas, 1)

        @block.tensor
        def _(pe):
            def transposes(src, banks, done, idn=ident):
                for g in range(4):
                    for c in range(2):
                        for tt in range(TT):
                            last = pe.transpose(bank[banks[g]][:, (c * TT + tt) * P:(c * TT + tt + 1) * P],
                                                src[:, tt, (2 * g + c) * P:(2 * g + c + 1) * P], idn[:, :])
                    last.then_inc(done, 1)

            pe.wait_ge(consts, 1)
            pe.wait_ge(x_in, 16 * TT)
            transposes(h, [4, 5, 6, 7], xT_ps)
            pe.wait_ge(par_in, 16 * 7)
            pe.transpose(bank[3][:, 0:N_PARAM], param_raw, ident[0:N_PARAM, 0:N_PARAM]).then_inc(par_ps, 1)

            def product(out, stationary, moving, start, stop):
                (s_hi, s_lo), (m_hi, m_lo) = stationary, moving
                pe.matmul(out, s_hi, m_hi, start=start, stop=False)
                pe.matmul(out, s_hi, m_lo, start=False, stop=False)
                return pe.matmul(out, s_lo, m_hi, start=False, stop=stop)

            state = {"unit": 0}

            def project(g, q):
                k = state["unit"]
                state["unit"] += 1
                pe.wait_ge(lo_sb, k + 1)
                w = [split_pieces(k, part)[0] for part in range(2)]
                if g in TOKEN_MAJOR:
                    if q == 0 and g > min(TOKEN_MAJOR):
                        pe.wait_ge(proj_sb, 2)
                    for tt in range(TT):
                        for c in range(2):
                            f = 2 * q + c
                            last = product(bank[6 + tt][:, :], [x[:, f, tt * P:(tt + 1) * P] for x in (x_hi, x_lo)],
                                           [p[:, c, :] for p in w], f == 0, f == KC - 1)
                else:
                    n = BLOCK_UNIT.index(k)
                    before = [m for m in range(n) if BLOCK_BANK[m] == BLOCK_BANK[n]]
                    if before and before[-1] < 8:
                        pe.wait_ge(u_sb, before[-1] + 1)
                    elif before:
                        pe.wait_ge(proj_sb, before[-1] - 7)
                    for c in range(KC):
                        last = product(bank[BLOCK_BANK[n]][:, 0:T], [p[:, c, :] for p in w],
                                       (x_hi[:, c, :], x_lo[:, c, :]), c == 0, c == KC - 1)
                last.then_inc(unit_used, 1)

            pe.wait_ge(x_lo_sb, 4)
            project(0, 0)
            project(0, 1)
            pe.wait_ge(wg_in, 48)
            pe.wait_ge(xT_a, 4)
            for c in range(KC):
                last = pe.matmul(bank[2][0:96, 0:T], wg[:, c, :], hT[:, c, :], start=(c == 0), stop=(c == KC - 1))
            last.then_inc(gate_ps, 1)
            for k in range(2, 24):
                project(k // 4, k % 4)
                if k == 8:
                    pe.wait_ge(rows_sb, 1)
                    pe.wait_ge(par_sb, 1)
                    for tt in range(TT):
                        last = pe.transpose(bank[3][:, tt * P:(tt + 1) * P], rowpack[:, tt * P:(tt + 1) * P], ident[:, :])
                    last.then_inc(col_ps, 1)

            def scores(u):
                tt, heads = UNITS[u]
                if u == 0:
                    pe.wait_ge(proj_sb, 10)
                    pe.wait_ge(rows_sb, 1)
                    pe.wait_ge(consts, 2)
                    pe.wait_ge(col_sb, 1)
                if u >= 2:
                    pe.wait_ge(exp_sb, u - 1)
                n = (tt + 1) * P
                for j, hd in enumerate(heads):
                    o = bank[2 + u % 2][:, j * n:(j + 1) * n]
                    pe.matmul(o, fqT[:, hd // 2, tt * P:(tt + 1) * P], fkz[:, hd, 0:n], start=True, stop=False)
                    pe.matmul(o, sel[:, hd, :], rowF[:, 0:n], start=False, stop=False)
                    last = pe.matmul(o[:, n - P:n], identb[:, :], maskS[:, :], start=False, stop=True)
                last.then_inc(S_ps, 1)

            def turn(u):
                pe.wait_ge(prob_sb, u + 1)
                if u >= 2:
                    pe.wait_ge(PT_sb, u - 1)
                for j in range(4):
                    last = pe.transpose(bank[4 + u % 2][:, j * P:(j + 1) * P], pr[:, u % 2, j * P:(j + 1) * P], ident[:, :])
                last.then_inc(T_ps, 1)

            def values(pair):
                pe.wait_ge(PT_sb, 6)
                if pair >= 2:
                    pe.wait_ge(hf_sb, pair - 1)
                for j in range(2):
                    hd = 2 * pair + j
                    o = bank[6 + pair % 2][64 * j:64 * j + 64, :]
                    pe.matmul(o[:, 0:P], fv[:, 0, hd * F_D:(hd + 1) * F_D],
                              PT[:, 4 + pair // 2, (hd % 4) * P:(hd % 4 + 1) * P], start=True, stop=True)
                    for s in range(2):
                        last = pe.matmul(o[:, P:T], fv[:, s, hd * F_D:(hd + 1) * F_D],
                                         PT[:, pair, (2 * j + s) * P:(2 * j + s + 1) * P],
                                         start=(s == 0), stop=(s == 1))
                last.then_inc(V_ps, 1)

            def decay(hd):
                if hd == 0:
                    pe.wait_ge(exp_sb, 6)
                    pe.wait_ge(qk_sb, 8)
                else:
                    pe.wait_ge(dec_sb, 2 * hd)
                    pe.wait_ge(ptm_sb, hd)
                pe.matmul(bank[2][:, 0:T], sel[:, hd, :], rowM, start=True, stop=False)
                pe.matmul(bank[2][:, 0:P], identb[:, :], maskT[:, :], start=False, stop=True)
                pe.matmul(bank[2][:, T:T + P], sel[:, hd, :], rowM[:, P:T], start=True, stop=False)
                pe.matmul(bank[2][:, T:T + P], identb[:, :], maskT[:, :], start=False, stop=True)
                pe.matmul(bank[3][:, 0:T], qk[:, 4 + hd, 0:P], qk[:, hd, :], start=True, stop=True)
                pe.matmul(bank[3][:, T:T + P], qk[:, 4 + hd, P:T], qk[:, hd, P:T], start=True, stop=True).then_inc(B_ps, 1)

            def numerators(hd):
                pe.wait_ge(ptm_sb, hd + 1)
                if hd == 0:
                    pe.wait_ge(PT_sb, 6)
                if hd >= 2:
                    pe.wait_ge(num_sb, hd - 1)
                o = bank[4 + hd % 2]
                w = ptm[:, hd % 2, :]
                pe.matmul(o[:, 0:M_D + 1], w[:, 0:P], vm[:, 0, hd, :], start=True, stop=True)
                pe.matmul(o[:, T:T + M_D + 1], w[:, P:T], vm[:, 0, hd, :], start=True, stop=False)
                pe.matmul(o[:, T:T + M_D + 1], w[:, T:T + P], vm[:, 1, hd, :], start=False, stop=True).then_inc(N_ps, 1)

            kinds = {"S": scores, "T": turn, "V": values, "B": decay, "N": numerators}
            for k, steps in enumerate(STEPS):
                for s in steps:
                    kinds[s[0]](int(s[1]))
                if k == 17:
                    pe.wait_ge(hn_sb, 1)
                    for b in range(2):
                        for j in range(2):
                            for tt in range(TT):
                                last = pe.transpose(bank[2 + b][:, (j * TT + tt) * P:(j * TT + tt + 1) * P],
                                                    hml[:, tt, 2 * b + j, :], ident[:, :])
                        last.then_inc(hm_ps, 1)
                project(6 + k // 4, k % 4)

            def branches(f):
                k = tail_unit(f"Y{f}")
                if f == 0:
                    pe.wait_ge(hm_lo_sb, 2)
                    pe.wait_ge(hf_lo_sb, 1)
                    pe.wait_ge(num_sb, 4)
                if f >= 2:
                    pe.wait_ge(y_sb, f - 1)
                pe.wait_ge(lo_sb, k + 1)
                for b, (hi, lo) in enumerate(((hm_hi, hm_lo), (hf_hi, hf_lo))):
                    w = [split_pieces(k, part)[b] for part in range(2)]
                    for c in range(4):
                        last = product(bank[4 + 2 * b + f % 2][:, 0:T], [p[:, c, :] for p in w], (hi[:, c, :], lo[:, c, :]),
                                       c == 0, c == 3)
                last.then_inc(unit_used, 1)

            def mix(c, tt, j):
                w = [split_pieces(tail_unit(f"O{c}"), part)[0][:, j * 512:(j + 1) * 512] for part in range(2)]
                return product(bank[2 * tt + j][:, :], [y[:, c, tt * P:(tt + 1) * P] for y in (y_hi, y_lo)], w,
                               c == 0, c == KC - 1)

            def mix_both(c):
                if c == 0:
                    pe.wait_ge(proj_sb, 32)
                    pe.wait_ge(hm_sb, 2)
                pe.wait_ge(lo_sb, tail_unit(f"O{c}") + 1)
                pe.wait_ge(y_sb, c + 1)
                for tt in range(TT):
                    for j in range(2):
                        last = mix(c, tt, j)
                last.then_inc(unit_used, 1)

            for name in TAIL[:-SPLITS]:
                (branches if name[0] == "Y" else mix_both)(int(name[1]))
            for tt in range(TT):
                for j in range(2):
                    for c in range(KC - SPLITS, KC):
                        if tt == 0 and j == 0:
                            pe.wait_ge(lo_sb, tail_unit(f"O{c}") + 1)
                            pe.wait_ge(y_sb, c + 1)
                        last = mix(c, tt, j)
                    last.then_inc(mix_ps, 1)

            pe.wait_ge(wr_in, 16)
            for tt in range(TT):
                for g in range(2):
                    pe.wait_ge(h1_sb, 2 * tt + g + 1)
                    for c in range(4):
                        f = 4 * g + c
                        last = pe.transpose(bank[4 + 2 * tt + g][:, c * P:(c + 1) * P], h[:, tt, f * P:(f + 1) * P], ident[:, :])
                    last.then_inc(hT_ps, 1)
                for c in range(KC):
                    if c % 4 == 0:
                        pe.wait_ge((hT_v, hT_a)[c // 4], tt + 1)
                    last = pe.matmul(bank[tt][:, 0:E], hT[:, c, tt * P:(tt + 1) * P], wr[:, c, :],
                                     start=(c == 0), stop=(c == KC - 1))
                last.then_inc(lg_ps, 1)

            def open_sums(tt):
                for j in range(2):
                    pe.matmul(bank[4 + 2 * tt + j][:, :], aident[:, :], h[:, tt, j * 512:(j + 1) * 512],
                              start=True, stop=False, skip_group_check=True)

            for tt in range(TT):
                pe.wait_ge(mask_sb, tt + 1)
                pe.matmul(bank[3][0:96, 0:1], mask3[:, tt, :, :].rearrange("p g e -> p (g e)"), ones_b[:, 0:1],
                          start=(tt == 0), stop=(tt == TT - 1)).then_inc(cnt_ps, 1)
            pe.matmul(bank[2][:, 0:E], below[:, :], mask3[:, 0, 0, :], start=True, stop=True)
            pe.matmul(bank[2][:, E:2 * E], ones_b[:, :], mask3[:, 0, 0, :], start=True, stop=False)
            pe.matmul(bank[2][:, E:2 * E], below[:, :], mask3[:, 1, 0, :], start=False, stop=True).then_inc(cnt_ps, 1)
            pe.wait_ge(nb_sb, 1)
            pe.matmul(bank[1][0:96, 1:2], upto3[:, :, :].rearrange("p g e -> p (g e)"), nbb[0:32, :], start=True, stop=True)
            pe.matmul(bank[3][0:1, 0:E], nbb[0:32, :], upto3[:, 0, :], start=True, stop=True)
            pe.matmul(bank[0][:, 0:E], nbB[:, :], start64[:, :], start=True, stop=True).then_inc(end_ps, 1)
            pe.wait_ge(gpg_sb, 1)
            for tt in range(TT):
                last = pe.transpose(bank[0][0:64, 64 + tt * P:64 + (tt + 1) * P], gpg[:, tt, :], ident[:, :])
            last.then_inc(gpgT_ps, 1)
            open_sums(0)
            pe.wait_ge(gpgT_sb, 1)
            pe.wait_ge(own_sb, 1)
            for tt in range(TT):
                pe.matmul(bank[1][:, tt * ITEMS:(tt + 1) * ITEMS], gpgT[0:32, tt, :], own[0:32, :], start=True, stop=True)
                last = pe.matmul(bank[2][:, tt * ITEMS:(tt + 1) * ITEMS], gpgT[32:64, tt, :], own[32:64, :],
                                 start=True, stop=True)
            last.then_inc(item_ps, 1)
            open_sums(1)

            def gather():
                for c in range(KC):
                    for tt in range(TT):
                        last = pe.matmul(bank[3][:, c * SLOTS:(c + 1) * SLOTS], h[:, tt, c * P:(c + 1) * P],
                                         pick[:, tt, :], start=(tt == 0), stop=(tt == TT - 1))
                last.then_inc(xg_ps, 1)

            def scatter():
                for tt in range(TT):
                    for j in range(2):
                        last = pe.matmul(bank[4 + 2 * tt + j][:, :], gatedT[64 * j:64 * j + 64, tt, :],
                                         ydn[64 * j:64 * j + 64, :], start=False, stop=False, skip_group_check=True)
                last.then_inc(scat_ps, 1)

            pe.wait_ge(tables, 1)
            n = pe.value_load(items_end[0:1, E:E + 1], min_val=E, max_val=MAX_ITEMS)
            pe.wait_ge(pick_sb, 1)
            gather()

            def expert(e, third):
                begin, end = (pe.value_load(items_end[0:1, bass.ds(e + k, 1)], min_val=k, max_val=MAX_ITEMS) for k in range(2))
                with pe.Fori(begin, end) as i:
                    pe.wait_ge(xg_sb, i + 1)
                    pe.wait_ge(actT_sb, i + 1)
                    pe.wait_ge(gatedT_sb, i + 1)
                    for k in range(GU_SLOTS):
                        pe.wait_ge(slot_in[k], e * 16 + 16)
                        for b in range(2):
                            for j in range(2):
                                o = D_FF * b + 512 * j
                                last = pe.matmul(bank[b][64 * j:64 * j + 64, :], xgT[:, k, :], slot(2 * third + k // HALF, k)[:, o:o + 512],
                                                 start=(k == 0), stop=(k == GU_SLOTS - 1))
                        last.then_inc(released, 1)
                        if k == GU_SLOTS - 2:
                            pe.wait_ge(selb_sb, i + 1)
                            for b in range(2):
                                for j in range(2):
                                    o = D_FF * b + 512 * j
                                    pe.matmul(bank[b][64 * j:64 * j + 64, :], selb, bias3[:, o:o + 512],
                                              start=False, stop=False)
                    pe.wait_ge(ydn_sb, i + 1)
                    scatter()
                    pe.wait_ge(pick_sb, i + 2)
                    gather()
                    pe.wait_ge(act_sb, i + 1)
                    pe.wait_ge(gated_sb, i + 1)
                    for q in range(4):
                        pe.transpose(bank[0][:, q * P:(q + 1) * P], act[:, q * P:(q + 1) * P], ident[:, :])
                    for tt in range(TT):
                        last = pe.transpose(bank[1][:, tt * P:(tt + 1) * P], gated[:, tt, :], ident[:, :])
                    last.then_inc(tr_ps, 1)
                    for j in range(2):
                        o = 2 * D + 512 * j
                        pe.matmul(bank[2][64 * j:64 * j + 64, :], selb, bias3[:, o:o + 512], start=True, stop=False)
                    pe.wait_ge(actT_sb, i + 2)
                    for k in range(GU_SLOTS, SLOTS_E):
                        pe.wait_ge(slot_in[k], e * 16 + 16)
                        for c in range(2):
                            f = 2 * (k - GU_SLOTS) + c
                            for j in range(2):
                                last = pe.matmul(bank[2][64 * j:64 * j + 64, :],
                                                 actT[:, f % 4, 64 * (f // 4):64 * (f // 4) + 64],
                                                 slot(2 * third + k // HALF, k)[:, c * D + 512 * j:c * D + 512 * j + 512],
                                                 start=False, stop=(f == KC - 1))
                        last.then_inc(released, 1)

            with pe.Fori(0, E // 3) as t:
                for step in range(3):
                    expert(t * 3 + step, step)
            for e in range(E - E % 3, E):
                expert(e, e % 3)
            pe.wait_ge(ydn_sb, n + 1)
            scatter()

        @block.scalar
        def _(sc):
            count = [0]

            def link(ins):
                count[0] += 1
                ins.then_inc(a_chain, 1)
                sc.wait_ge(a_chain, count[0])

            def split_high(k):
                n, pieces = raw_pieces(k)
                if n == 0:
                    sc.wait_ge(half_in[k // 2], 16)
                elif k == TAIL_AT or raw_pieces(k - 1)[0] != n:
                    sc.wait_ge(blk_in[n], 16)
                    if n == W_BF:
                        sc.wait_ge(blk_in[W_BM], 16)
                if k >= SPLITS:
                    sc.wait_ge(unit_used, k - SPLITS + 1)
                for src, dst in zip(pieces, split_pieces(k, 0)):
                    last = sc.copy(dst, src)
                last.then_inc(hi_sb, 1)

            for g in range(4):
                sc.wait_ge(xT_ps, g + 1)
                sc.copy(x_hi[:, 2 * g:2 * g + 2, :], bank[4 + g][:, :].rearrange("p (c t) -> p c t", t=T)).then_inc(x_hi_sb, 1)
            for k in range(2):
                split_high(k)
            for g in range(4):
                sc.wait_ge(x_lo_sb, g + 1)
                sc.copy(hT[:, 2 * g:2 * g + 2, :], bank[4 + g][:, :].rearrange("p (c t) -> p c t", t=T)).then_inc(xT_a, 1)
            for k in range(2, SPLITS):
                split_high(k)

            def conv_sigmoid(b):
                sc.wait_ge(conv_sb, b + 1)
                if b >= 2:
                    sc.wait_ge(qk_sb, b - 1)
                sc.activation(sg_c[:, b % 2, :], cv[:, b % 2, :], ACT.Sigmoid).then_inc(csig, 1)

            for b in range(8):
                sc.wait_ge(unit_used, b + 1)
                if b == 0:
                    sc.wait_ge(par_sb, 1)
                    sc.wait_ge(consts, 2)
                if b >= 2:
                    sc.wait_ge(conv_sb, b - 1)
                sc.activation(upad[:, b % 2, 3:3 + T], bank[b % 2][:, 0:T], ACT.Identity,
                              bias=param[:, b:b + 1]).then_inc(u_sb, 1)
                split_high(b + SPLITS)
                if b >= 1:
                    conv_sigmoid(b - 1)
                if b == 2:
                    sc.wait_ge(z_sb, 1)
                    link(sc.activation(tmp_rows[:, 2, :], tmp_rows[:, 1, :], ACT.Exp))
                    sc.activation(tmp_rows[:, 1, :], tmp_rows[:, 2, :], ACT.Ln, bias=1.0).then_inc(logexp, 1)
            conv_sigmoid(7)
            for k in range(8, 24):
                split_high(k + SPLITS)
                if k == 12:
                    sc.wait_ge(col_sb, 1)
                    sc.activation(em, colT[:, :, 32:36], ACT.Exp).then_inc(em_sb, 1)

            def softmax_exp(u):
                tt, heads = UNITS[u]
                n = (tt + 1) * P
                sc.wait_ge(max_sb, u + 1)
                if u >= 2:
                    sc.wait_ge(T_ps, u - 1)
                for j in range(len(heads)):
                    last = sc.activation(pr[:, u % 2, j * n:(j + 1) * n], bank[2 + u % 2][:, j * n:(j + 1) * n], ACT.Exp,
                                         bias=negmax[:, 4 * u + j:4 * u + j + 1],
                                         accum_out=rsum[:, 4 * u + j:4 * u + j + 1])
                last.then_inc(exp_sb, 1)

            def decay_exp(hd):
                sc.wait_ge(B_ps, hd + 1)
                if hd >= 2:
                    sc.wait_ge(ptm_sb, hd - 1)
                for s, (o, n) in enumerate(((0, T), (T, P))):
                    sc.activation(dec[:, hd % 2, o:o + n], bank[2][:, o:o + n], ACT.Exp,
                                  bias=colT[:, s, hd:hd + 1]).then_inc(dec_sb, 1)

            def open_gate(g, blocks):
                sc.wait_ge(proj_sb, blocks)
                sc.activation(g, g, ACT.Sigmoid).then_inc(gates_sig, 1)

            for k, steps in enumerate(STEPS):
                for s in steps:
                    if s[0] == "S":
                        softmax_exp(int(s[1]))
                    if s[0] == "B":
                        decay_exp(int(s[1]))
                if k == 14:
                    sc.wait_ge(hvar, 1)
                    sc.activation(hrstd, hrstd, ACT.Sqrt).then_inc(hstd, 1)
                if k == 18:
                    for b in range(2):
                        sc.wait_ge(hm_sb, b + 1)
                        sc.copy(hm_hi[:, 2 * b:2 * b + 2, :], hmT[:, 2 * b:2 * b + 2, :]).then_inc(hm_hi_sb, 1)
                split_high(24 + k + SPLITS)
                if k == 12:
                    open_gate(mo, 16)
                if k == 13:
                    sc.wait_ge(hf_sb, 4)
                    sc.copy(hf_hi, hfT).then_inc(hf_hi_sb, 1)
                if k == 14:
                    open_gate(gm[:, 0:4, :], 24)
                if k == 15:
                    open_gate(gm[:, 4:8, :], 24)
                if k == 17:
                    open_gate(gf[:, 0:4, :], 28)
            open_gate(gf[:, 4:8, :], 32)
            for k in range(TAIL_AT + SPLITS, N_SPLIT):
                split_high(k)
            for tt in range(TT):
                sc.wait_ge(var1, tt + 1)
                sc.activation(lrstd[:, tt:tt + 1], lrstd[:, tt:tt + 1], ACT.Sqrt).then_inc(std1, 1)
            for tt in range(TT):
                sc.wait_ge(hT_ps, 2 * tt + 2)
                sc.copy(hT[:, 4:8, tt * P:(tt + 1) * P], bank[5 + 2 * tt][:, :].rearrange("p (c t) -> p c t", t=P)).then_inc(hT_a, 1)
            for tt in range(TT):
                sc.wait_ge(lgmax, tt + 1)
                sc.activation(gexp[:, tt, :], lg[:, tt, :], ACT.Exp, bias=ntop[:, tt:tt + 1]).then_inc(gexp_sb, 1)

            sc.wait_ge(tables, 1)
            n = sc.value_load(items_end[0:1, E:E + 1], min_val=E, max_val=MAX_ITEMS)

            def take_tokens():
                sc.copy(xgT, bank[3][:, :].rearrange("p (c s) -> p c s", s=SLOTS)).then_inc(xg_sb, 1)

            sc.wait_ge(xg_ps, 1)
            take_tokens()
            with sc.Fori(0, n) as i:
                sc.wait_ge(glu_sb, i + 1)
                sc.activation(sig, glu, ACT.Sigmoid, scale=SW_ALPHA).then_inc(sig_sb, 1)
                sc.wait_ge(xg_ps, i + 2)
                take_tokens()
                sc.wait_ge(tr_ps, i + 1)
                sc.copy(gatedT, bank[1][:, 0:T].rearrange("p (a t) -> p a t", a=TT)).then_inc(gatedT_sb, 1)
                sc.wait_ge(released, i * SLOTS_E + SLOTS_E)
                sc.copy(ydn, bank[2][:, :]).then_inc(ydn_sb, 1)
            sc.wait_ge(var2, 1)
            sc.activation(lrstd, lrstd, ACT.Sqrt).then_inc(std2, 1)

        @block.vector
        def _(v):
            count = [0]

            def link(ins):
                count[0] += 1
                ins.then_inc(v_chain, 1)
                v.wait_ge(v_chain, count[0])

            def split_low(k):
                v.wait_ge(hi_sb, k + 1)
                for src, hi, lo in zip(raw_pieces(k)[1], split_pieces(k, 0), split_pieces(k, 1)):
                    last = v.tensor_tensor(lo, src, hi.bitcast(F32), ALU.subtract)
                last.then_inc(lo_sb, 1)

            for g in range(4):
                v.wait_ge(x_hi_sb, g + 1)
                v.tensor_tensor(x_lo[:, 2 * g:2 * g + 2, :], bank[4 + g][:, :].rearrange("p (c t) -> p c t", t=T),
                                x_hi[:, 2 * g:2 * g + 2, :].bitcast(F32), ALU.subtract).then_inc(x_lo_sb, 1)
            v.wait_ge(par_ps, 1)
            v.tensor_copy(param[:, :], bank[3][:, 0:N_PARAM]).then_inc(par_sb, 1)
            for k in range(SPLITS):
                split_low(k)

            z, ln1p, logf, gate_in = (tmp_rows[:, k, :] for k in range(4))

            def gate_inputs():
                v.wait_ge(gate_ps, 1)
                v.wait_ge(gb_in, 48)
                link(v.tensor_scalar(z, bank[2][0:64, 0:T], gbias[0:64, :], None, ALU.add))
                v.scalar_tensor_tensor(out=ln1p, in0=z, scalar=-1.0, in1=z, op0=ALU.mult, op1=ALU.min).then_inc(z_sb, 1)
                v.tensor_scalar(gate_in[0:4, :], bank[2][64:68, 0:T], gbias[64:68, :], None, ALU.add)

            def gate_rows():
                v.wait_ge(logexp, 1)
                link(v.scalar_tensor_tensor(out=logf, in0=z, scalar=0.0, in1=ln1p, op0=ALU.min, op1=ALU.subtract))
                v.wait_ge(consts, 2)
                link(v.tensor_tensor_scan(z, ones256, logf, 0.0, ALU.mult, ALU.add))
                link(v.tensor_tensor(rowpack[0:4, :], gate_in[0:4, :], z[0:4, :], ALU.subtract))
                link(v.tensor_tensor_scan(ln1p[0:4, :], rowpack[0:4, :], rowpack[0:4, :], 0.0, ALU.max, ALU.max))
                v.tensor_scalar(rowM[0:4, :], ln1p[0:4, :], -1.0, None, ALU.mult)
                v.scalar_tensor_tensor(out=rowpack[32:36, :], in0=z[0:4, :], scalar=-1.0, in1=ln1p[0:4, :],
                                       op0=ALU.mult, op1=ALU.subtract)
                v.tensor_scalar(rowF[0:8, :], z[32:40, :], -1.0, None, ALU.mult).then_inc(rows_sb, 1)

            def conv(b):
                v.wait_ge(u_sb, b + 1)
                if b >= 2:
                    v.wait_ge(qk_sb, b - 1)
                cw = PARAM_ROWS["cw"]
                u, o = upad[:, b % 2, :], cv[:, b % 2, :]
                link(v.tensor_scalar(o, u[:, 0:T], param[:, cw + b:cw + b + 1],
                                     param[:, PARAM_ROWS["cb"] + b:PARAM_ROWS["cb"] + b + 1], ALU.mult, ALU.add))
                for j in range(1, CONV_W):
                    w = param[:, cw + 8 * j + b:cw + 8 * j + b + 1]
                    last = v.scalar_tensor_tensor(out=o, in0=u[:, j:j + T], scalar=w, in1=o, op0=ALU.mult, op1=ALU.add)
                    if j < CONV_W - 1:
                        link(last)
                last.then_inc(conv_sb, 1)

            def silu(b):
                v.wait_ge(csig, b + 1)
                v.scalar_tensor_tensor(out=qk[:, b, :], in0=cv[:, b % 2, :], scalar=1.0 if b < 4 else M_D ** -0.5,
                                       in1=sg_c[:, b % 2, :], op0=ALU.mult, op1=ALU.mult).then_inc(qk_sb, 1)

            for b in range(8):
                conv(b)
                split_low(b + SPLITS)
                if b == 1:
                    gate_inputs()
                if b == 3:
                    gate_rows()
                if b >= 1:
                    silu(b - 1)
            silu(7)

            for k in range(8, 24):
                v.wait_ge(unit_used, k + 1)
                b = k % 4
                if k == 11:
                    v.wait_ge(vb_in, 64)
                    for tt in range(TT):
                        v.tensor_tensor(vm[:, tt, :, 0:M_D], bank[6 + tt][:, :].rearrange("p (h d) -> p h d", h=M_HEADS),
                                        vm[:, tt, :, 0:M_D], ALU.add).then_inc(proj_sb, 1)
                elif 12 <= k < 16:
                    v.tensor_scalar(fqT[:, b, :], bank[b % 2][:, 0:T], param[:, 12 + b:13 + b], F_D ** -0.5,
                                    ALU.add, ALU.mult).then_inc(proj_sb, 1)
                elif 16 <= k < 20:
                    for j in range(2):
                        r = slice(64 * j, 64 * j + 64)
                        last = v.tensor_scalar(fkz[r, 2 * b + j, :], bank[b % 2][r, 0:T], param[r, 16 + b:17 + b], None, ALU.add)
                    last.then_inc(proj_sb, 1)
                elif k == 23:
                    for tt in range(TT):
                        v.tensor_tensor(fv[:, tt, :], bank[6 + tt][:, :], fv[:, tt, :], ALU.add).then_inc(proj_sb, 1)
                split_low(k + SPLITS)
                if k == 9:
                    v.wait_ge(col_ps, 1)
                    v.tensor_copy(colT, bank[3][:, 0:TT * P].rearrange("p (a r) -> p a r", a=TT)[:, :, 0:64]).then_inc(col_sb, 1)

            def row_max(u):
                tt, heads = UNITS[u]
                k = len(heads)
                v.wait_ge(S_ps, u + 1)
                link(v.tensor_reduce(negmax[:, 4 * u:4 * u + k],
                                     bank[2 + u % 2][:, :].rearrange("p (k n) -> p k n", k=k), AX.X, ALU.max))
                v.tensor_scalar(negmax[:, 4 * u:4 * u + k], negmax[:, 4 * u:4 * u + k], -1.0, None, ALU.mult).then_inc(max_sb, 1)

            def normalise(u):
                tt, heads = UNITS[u]
                k = len(heads)
                v.wait_ge(exp_sb, u + 1)
                r = rrec[:, 4 * u:4 * u + k]
                link(v.reciprocal(r, rsum[:, 4 * u:4 * u + k]))
                pp = pr[:, u % 2, :].rearrange("p (k n) -> p k n", k=k)
                v.tensor_tensor(pp, pp, r.unsqueeze(2).to_broadcast([P, k, 512 // k]), ALU.mult).then_inc(prob_sb, 1)

            def take_turned(u):
                v.wait_ge(T_ps, u + 1)
                if u == 0:
                    v.wait_ge(bias3_done, 1)
                v.tensor_copy(PT[:, u, :], bank[4 + u % 2][:, :]).then_inc(PT_sb, 1)

            def take_values(pair):
                v.wait_ge(V_ps, pair + 1)
                v.tensor_copy(hfT[:, pair, :], bank[6 + pair % 2][:, 0:T]).then_inc(hf_sb, 1)

            def weigh(hd):
                v.wait_ge(dec_sb, 2 * hd + 2)
                if hd >= 2:
                    v.wait_ge(N_ps, hd - 1)
                v.tensor_tensor(ptm[:, hd % 2, :], bank[3][:, 0:384], dec[:, hd % 2, :], ALU.mult).then_inc(ptm_sb, 1)

            def divide(hd):
                v.wait_ge(N_ps, hd + 1)
                if hd == 0:
                    v.wait_ge(em_sb, 1)
                o = bank[4 + hd % 2][:, :].rearrange("p (a n) -> p a n", a=TT)
                den = msum[:, 2 * hd:2 * hd + 2].unsqueeze(2)
                total = o[:, :, M_D:M_D + 1]
                link(v.scalar_tensor_tensor(out=den, in0=total, scalar=-1.0, in1=em[:, :, hd:hd + 1],
                                            op0=ALU.mult, op1=ALU.max))
                link(v.tensor_tensor(den, total, den, ALU.max))
                r = rden[:, 2 * hd:2 * hd + 2]
                link(v.reciprocal(r, msum[:, 2 * hd:2 * hd + 2]))
                for tt in range(TT):
                    last = v.tensor_scalar(hml[:, tt, hd, :], o[:, tt, 0:M_D], r[:, tt:tt + 1], None, ALU.mult)
                last.then_inc(num_sb, 1)
                v.wait_ge(num_sb, hd + 1)
                for tt in range(TT):
                    link(v.bn_stats(bn6[:, 6 * tt:6 * tt + 6], hml[:, tt, hd, :]))
                    k = 2 * (tt * M_HEADS + hd)
                    last = v.bn_aggr(hstat[:, k:k + 2], bn6[:, 6 * tt:6 * tt + 6])
                last.then_inc(heads_stat, 1)

            before = {1: "n0", 2: "n1", 3: "n2", 4: "n3", 5: "n4", 6: "n5"}
            after = {6: "w0", 7: "w1", 9: "w2", 11: "w3"}
            kinds = {"S": row_max, "T": take_turned, "V": take_values, "N": divide, "n": normalise, "w": weigh}
            dest = [mo[:, b, :] for b in range(4)] + [gm[:, b, :] for b in range(8)] + [gf[:, b, :] for b in range(8)]
            pcol = [8 + b for b in range(4)] + [20 + b for b in range(8)] + [28 + b for b in range(8)]
            for k, steps in enumerate(STEPS):
                for s in [before.get(k)] + [s for s in steps if s[0] != "B"] + [after.get(k)]:
                    if s:
                        kinds[s[0]](int(s[1]))
                if k == 13:
                    v.wait_ge(heads_stat, M_HEADS)
                    v.tensor_scalar(hrstd, hstat.rearrange("p (k s) -> p k s", s=2)[:, :, 1], LN_EPS, None, ALU.add).then_inc(hvar, 1)
                if k == 17:
                    v.wait_ge(gates_sig, 1)
                    for b in range(2):
                        v.wait_ge(hm_ps, b + 1)
                        for hd in (2 * b, 2 * b + 1):
                            ng = PARAM_ROWS["ng"] + hd
                            last = v.scalar_tensor_tensor(out=hmT[:, hd, :], in0=bank[2 + b][:, (hd % 2) * T:(hd % 2 + 1) * T],
                                                          scalar=param[:, ng:ng + 1], in1=mo[:, hd, :],
                                                          op0=ALU.mult, op1=ALU.mult)
                        last.then_inc(hm_sb, 1)
                if k == 18:
                    for b in range(2):
                        v.wait_ge(hm_hi_sb, b + 1)
                        v.tensor_tensor(hm_lo[:, 2 * b:2 * b + 2, :], hmT[:, 2 * b:2 * b + 2, :],
                                        hm_hi[:, 2 * b:2 * b + 2, :].bitcast(F32), ALU.subtract).then_inc(hm_lo_sb, 1)
                v.wait_ge(unit_used, 24 + k + 1)
                v.tensor_scalar(dest[k], bank[k % 2][:, 0:T], param[:, pcol[k]:pcol[k] + 1], None, ALU.add).then_inc(proj_sb, 1)
                split_low(24 + k + SPLITS)
                if k == 15:
                    v.wait_ge(hstd, 1)
                    link(v.reciprocal(hrstd, hrstd))
                    for tt in range(TT):
                        for hd in range(M_HEADS):
                            j = tt * M_HEADS + hd
                            last = v.tensor_scalar(hml[:, tt, hd, :], hml[:, tt, hd, :], hstat[:, 2 * j:2 * j + 1],
                                                   hrstd[:, j:j + 1], ALU.subtract, ALU.mult)
                    last.then_inc(hn_sb, 1)
                if k == 16:
                    v.wait_ge(hf_hi_sb, 1)
                    v.tensor_tensor(hf_lo, hfT, hf_hi.bitcast(F32), ALU.subtract).then_inc(hf_lo_sb, 1)

            def merge(f):
                v.wait_ge(unit_used, tail_unit(f"Y{f}") + 1)
                v.wait_ge(gates_sig, 5 if f >= 4 else 4)
                v.tensor_tensor(gm[:, f, :], bank[4 + f % 2][:, 0:T], gm[:, f, :], ALU.mult)
                link(v.tensor_tensor(gf[:, f, :], bank[6 + f % 2][:, 0:T], gf[:, f, :], ALU.mult))
                link(v.tensor_tensor(gm[:, f, :], gm[:, f, :], gf[:, f, :], ALU.add))
                link(v.tensor_copy(y_hi[:, f, :], gm[:, f, :]))
                v.tensor_tensor(y_lo[:, f, :], gm[:, f, :], y_hi[:, f, :].bitcast(F32), ALU.subtract).then_inc(y_sb, 1)

            for t, name in enumerate(TAIL):
                if name[0] == "Y":
                    merge(int(name[1]))
                if t + SPLITS < len(TAIL):
                    split_low(TAIL_AT + t + SPLITS)

            def statistics(src, tt):
                for j in range(2):
                    last = v.bn_stats(bn6[:, 12 * tt + 6 * j:12 * tt + 6 * j + 6], src(j))
                link(last)
                link(v.bn_aggr(lstat[:, 2 * tt:2 * tt + 2], bn6[:, 12 * tt:12 * tt + 12]))

            var = lstat.rearrange("p (k s) -> p k s", s=2)[:, :, 1]
            for tt in range(TT):
                for j in range(2):
                    v.wait_ge(mix_ps, 2 * tt + j + 1)
                    hs = h[:, tt, j * 512:(j + 1) * 512]
                    link(v.scalar_tensor_tensor(out=hs, in0=hs, scalar=ALPHA, in1=bank[2 * tt + j][:, :],
                                                op0=ALU.mult, op1=ALU.add))
                    link(v.bn_stats(bn6[:, 12 * tt + 6 * j:12 * tt + 6 * j + 6], hs))
                link(v.bn_aggr(lstat[:, 2 * tt:2 * tt + 2], bn6[:, 12 * tt:12 * tt + 12]))
                v.tensor_scalar(lrstd[:, tt:tt + 1], lstat[:, 2 * tt + 1:2 * tt + 2], LN_EPS, None, ALU.add).then_inc(var1, 1)
                if tt == 0:
                    v.wait_ge(ln1_in, 32)
                link(v.scalar_tensor_tensor(out=h[:, tt, :], in0=h[:, tt, :], scalar=lstat[:, 2 * tt:2 * tt + 1], in1=ln_g,
                                            op0=ALU.subtract, op1=ALU.mult))
                v.wait_ge(std1, tt + 1)
                link(v.reciprocal(lrstd[:, tt:tt + 1], lrstd[:, tt:tt + 1]))
                for j in range(2):
                    cols = slice(j * 512, (j + 1) * 512)
                    v.scalar_tensor_tensor(out=h[:, tt, cols], in0=h[:, tt, cols], scalar=lrstd[:, tt:tt + 1],
                                           in1=ln_b[:, cols], op0=ALU.mult, op1=ALU.add).then_inc(h1_sb, 1)

            v.wait_ge(br_in, 16)
            v.wait_ge(iotas, 1)
            for tt in range(TT):
                v.wait_ge(hT_ps, 2 * tt + 1)
                v.tensor_copy(hT[:, 0:4, tt * P:(tt + 1) * P], bank[4 + 2 * tt][:, :].rearrange("p (c t) -> p c t", t=P)).then_inc(hT_v, 1)
            for tt in range(TT):
                v.wait_ge(lg_ps, tt + 1)
                link(v.tensor_tensor(lg[:, tt, :], bank[tt][:, 0:E], br, ALU.add))
                link(v.max(top8[:, tt, :], lg[:, tt, :]))
                v.tensor_scalar(ntop[:, tt:tt + 1], top8[:, tt, 0:1], -1.0, None, ALU.mult).then_inc(lgmax, 1)
                link(v.max_index(idx8[:, tt, :].bitcast(U32), top8[:, tt, :], lg[:, tt, :]))
                link(v.tensor_copy(idxf[:, tt, :], idx8[:, tt, :].bitcast(U32)))
                link(v.tensor_scalar(mask[:, tt, :], iota_e, idxf[:, tt, 0:1], None, ALU.is_equal))
                for k in range(1, TOP_K):
                    link(v.scalar_tensor_tensor(out=mask[:, tt, :], in0=iota_e, scalar=idxf[:, tt, k:k + 1],
                                                in1=mask[:, tt, :], op0=ALU.is_equal, op1=ALU.add))
                v.tensor_copy(mask3[:, tt, :, :], mask[:, tt, :].unsqueeze(1).to_broadcast([P, 3, E])).then_inc(mask_sb, 1)
            v.wait_ge(gexp_sb, 2)
            link(v.tensor_tensor(gexp, gexp, mask, ALU.mult))
            link(v.tensor_reduce(gsum, gexp, AX.X, ALU.add))
            link(v.reciprocal(gsum, gsum))
            v.tensor_tensor(gpg[:, :, E:2 * E], gexp, gsum.unsqueeze(2).to_broadcast([P, TT, E]), ALU.mult)
            v.wait_ge(cnt_ps, 3)
            v.tensor_scalar(slot1, bank[2][:, 0:TT * E].rearrange("p (a e) -> p a e", a=TT), 1.0, None, ALU.add)
            tokens = bank[3][0:96, 0:1]
            link(v.tensor_scalar(nb[0:96, :], tokens, float(SLOTS), 1.0, ALU.is_gt, ALU.add))
            for k in range(2, T // SLOTS):
                link(v.scalar_tensor_tensor(out=nb[0:96, :], in0=tokens, scalar=float(k * SLOTS), in1=nb[0:96, :],
                                            op0=ALU.is_gt, op1=ALU.add))
            v.tensor_copy(nbb[:, :], nb[0:96, :])
            v.tensor_copy(nbB[:, :], nb[0:32, :].to_broadcast([32, P])).then_inc(nb_sb, 1)
            v.wait_ge(end_ps, 1)
            link(v.tensor_copy(start_sb, bank[0][:, 0:E]))
            link(v.tensor_tensor(slot1, slot1, start_sb.unsqueeze(1).to_broadcast([P, TT, E]), ALU.add))
            v.tensor_tensor(gpg[:, :, 0:E], slot1, mask, ALU.mult).then_inc(gpg_sb, 1)
            link(v.tensor_copy(cnt[0:96, :], bank[1][0:96, 1:2]))
            link(v.tensor_tensor(st_col[0:96, :], cnt[0:96, :], nb[0:96, :], ALU.subtract))
            link(v.tensor_scalar(ownT[0:96, :], iota_item[0:96, :], cnt[0:96, :], None, ALU.is_lt))
            v.scalar_tensor_tensor(out=own[0:96, :], in0=iota_item[0:96, :], scalar=st_col[0:96, :],
                                   in1=ownT[0:96, :], op0=ALU.is_ge, op1=ALU.mult).then_inc(own_sb, 1)
            v.memset(items_end[:, 0:1], 0)
            v.tensor_copy(items_end[:, 1:E + 1], bank[3][0:1, 0:E])
            v.tensor_scalar(last_item[:, :], bank[3][0:1, 0:E], -1.0, None, ALU.add).then_inc(tables, 1)
            v.wait_ge(gpgT_ps, 1)
            v.tensor_copy(gpgT, bank[0][0:64, 64:64 + T].rearrange("p (a t) -> p a t", a=TT)).then_inc(gpgT_sb, 1)
            v.wait_ge(item_ps, 1)
            v.tensor_tensor(local, bank[1][:, 0:TT * ITEMS].rearrange("p (a i) -> p a i", a=TT),
                            item_off.unsqueeze(1).to_broadcast([P, TT, ITEMS]), ALU.subtract)
            link(v.tensor_copy(igate, bank[2][:, 0:TT * ITEMS].rearrange("p (a i) -> p a i", a=TT)))

            def pick_tokens(i):
                for tt in range(TT):
                    last = v.tensor_scalar(pick[:, tt, :], iota_slot, local[:, tt, bass.ds(i, 1)], None, ALU.is_equal)
                last.then_inc(pick_sb, 1)

            def gate_tokens(i):
                for tt in range(TT):
                    for j in range(2):
                        last = v.tensor_scalar(gated[:, tt, 64 * j:64 * j + 64], iota_slot, local[:, tt, bass.ds(i, 1)],
                                               igate[:, tt, bass.ds(i, 1)], ALU.is_equal, ALU.mult)
                last.then_inc(gated_sb, 1)

            def select_bias(i):
                v.tensor_scalar(selb, ones_b[0:96, 0:SLOTS], own[0:96, bass.ds(i, 1)], None, ALU.mult).then_inc(selb_sb, 1)

            v.wait_ge(own_sb, 1)
            v.wait_ge(tables, 1)
            n = v.value_load(items_end[0:1, E:E + 1], min_val=E, max_val=MAX_ITEMS)
            pick_tokens(0)
            gate_tokens(0)
            select_bias(0)
            v.memset(ydn, 0.0).then_inc(ydn_sb, 1)
            v.memset(gatedT, 0.0).then_inc(gatedT_sb, 1)
            v.memset(actT, 0.0).then_inc(actT_sb, 1)
            with v.Fori(0, n) as i:
                v.wait_ge(xg_ps, i + 1)
                pick_tokens(i + 1)
                v.wait_ge(released, i * SLOTS_E + GU_SLOTS)
                v.tensor_scalar(glu, bank[0][:, :], SW_LIMIT, None, ALU.min).then_inc(glu_sb, 1)
                v.tensor_scalar(lin, bank[1][:, :], SW_LIMIT, -SW_LIMIT, ALU.min, ALU.max).then_inc(moe_v, 1)
                v.wait_ge(moe_v, i * 2 + 1)
                v.scalar_tensor_tensor(out=half_act, in0=lin, scalar=1.0, in1=glu, op0=ALU.add, op1=ALU.mult).then_inc(moe_v, 1)
                v.wait_ge(moe_v, i * 2 + 2)
                v.wait_ge(sig_sb, i + 1)
                v.tensor_tensor(act, half_act, sig, ALU.mult).then_inc(act_sb, 1)
                v.wait_ge(tr_ps, i + 1)
                v.tensor_copy(actT, bank[0][:, :].rearrange("p (c s) -> p c s", s=P)).then_inc(actT_sb, 1)
                gate_tokens(i + 1)
                v.wait_ge(released, i * SLOTS_E + SLOTS_E)
                select_bias(i + 1)

            v.wait_ge(scat_ps, n + 1)
            for tt in range(TT):
                statistics(lambda j: bank[4 + 2 * tt + j][:, :], tt)
            v.tensor_scalar(lrstd, var, LN_EPS, None, ALU.add).then_inc(var2, 1)
            v.wait_ge(std2, 1)
            v.wait_ge(ln2_in, 32)
            link(v.reciprocal(lrstd, lrstd))
            for tt in range(TT):
                for j in range(2):
                    cols = slice(j * 512, (j + 1) * 512)
                    link(v.scalar_tensor_tensor(out=h[:, tt, cols], in0=bank[4 + 2 * tt + j][:, :],
                                                scalar=lstat[:, 2 * tt:2 * tt + 1], in1=ln_g[:, cols],
                                                op0=ALU.subtract, op1=ALU.mult))
                    last = v.scalar_tensor_tensor(out=h[:, tt, cols], in0=h[:, tt, cols], scalar=lrstd[:, tt:tt + 1],
                                                  in1=ln_b[:, cols], op0=ALU.mult, op1=ALU.add)
                last.then_inc(fin_sb, 1)


NAMES = ["x", "w_in", "b_in", "m_conv_w", "m_conv_b", "m_norm_g", "w_bm", "w_bf", "w_o", "ln1_g", "ln1_b",
         "w_router", "b_router", "w_gu", "b_gu", "w_dn", "b_dn", "ln2_g", "ln2_b"]


def kernel(**inputs):
    import concourse.bacc as bacc
    import numpy as np
    from concourse.bass_utils import run_bass_kernel_spmd

    nc = bacc.Bacc("TRN2", target_bir_lowering=False, num_devices=1)
    arrays, args = {}, {}
    for name in NAMES:
        a = np.ascontiguousarray(inputs[name])
        arrays[f"in_{name}"] = a
        args[name] = nc.dram_tensor(f"in_{name}", a.shape, mybir.dt.from_np(a.dtype), kind="ExternalInput").ap()
    out = nc.dram_tensor("out_h", (1, T, D), F32, kind="ExternalOutput").ap()
    build(nc, out=out, **args)
    r = run_bass_kernel_spmd(nc, [arrays], core_ids=[0])
    return r.results[0]["out_h"]
```

```python
from contextlib import ExitStack

import concourse.bass as bass
from concourse import mybir

F32 = mybir.dt.float32
BF16 = mybir.dt.bfloat16
F32R = mybir.dt.float32r
I32 = mybir.dt.int32
U32 = mybir.dt.uint32
ALU = mybir.AluOpType
ACT = mybir.ActivationFunctionType
AX = mybir.AxisListType

P = 128
D = 1024
T = 256
TT = T // P
KC = D // P
M_HEADS, M_D = 4, 128
F_HEADS, F_D = 8, 64
CONV_W = 4
E = 32
TOP_K = 4
D_FF = 1024
SLOTS = 64
MAX_ITEMS = T * TOP_K // SLOTS + E - 1
ITEMS = MAX_ITEMS + 1
GATHER_FIRST = 7
ALPHA = 2.0 ** 0.25
LN_EPS = 1e-5
SW_ALPHA, SW_LIMIT = 1.702, 7.0
NEG = -1e30
MQK, MV, MO, MI, MF, FQ, FK, FV, FF, GM, GF = 0, 1024, 1536, 2048, 2052, 2056, 2568, 3080, 3592, 3600, 4624

GROUPS = [MQK, MQK + 512, MV, FQ, FK, FV, MO, GM, GM + 512, GF, GF + 512]
TOKEN_MAJOR = {2, 5}
W_B0, W_B1, W_O0, W_O1, WO_MID = 11, 12, 13, 14, 15
RAW_REGIONS = 3
REGIONS = 6
RWORDS = KC * 512
ARENA = 9372
SLOT_WORDS = 2 * D_FF
SLOTS_E = 12
HALF = SLOTS_E // 2
THIRD = HALF * SLOT_WORDS
GU_SLOTS = KC

SPLITS = 4
TAIL = ["Y0", "Y1", "Y2", "O0", "Y3", "O1", "Y4", "O2", "Y5", "O3", "Y6", "Y7", "O4", "O5", "O6", "O7"]
TAIL_AT = 4 * len(GROUPS)
N_SPLIT = TAIL_AT + len(TAIL)
BLOCK_UNIT, BLOCK_BANK = [], []
for _g in range(len(GROUPS)):
    if _g in TOKEN_MAJOR:
        BLOCK_UNIT += [4 * _g + 3] * TT
        BLOCK_BANK += [6, 7]
    else:
        BLOCK_UNIT += [4 * _g + q for q in range(4)]
        BLOCK_BANK += [0, 1, 0, 1]


def tail_unit(name):
    return TAIL_AT + TAIL.index(name)


def last_unit(n):
    return 4 * n + 3 if n < 11 else tail_unit({W_B0: "Y3", W_B1: "Y7", W_O0: "O3", W_O1: "O7"}[n])


UNITS = [(1, [2 * u, 2 * u + 1]) for u in range(4)] + [(0, [0, 1, 2, 3]), (0, [4, 5, 6, 7])]

STEPS = [
    ["S0"], ["S1"], ["T0", "S2"], ["T1", "S3"], ["T2", "S4"], ["T3", "S5"], ["T4"], ["B0"],
    ["T5", "B1", "N0"], ["B2", "N1", "V0"], ["B3", "N2", "V1"], ["N3", "V2"], ["V3"], [], [], [], [], [], [], [],
]
V_STEPS = [
    ["S0"], ["S1"], ["T0", "S2"], ["T1", "S3"], ["T2", "S4"], ["T3", "S5"], ["T4"],
    ["w0"], ["T5", "w1", "N0"], ["w2", "N1", "V0"], ["w3", "N2", "V1"], ["N3", "V2"], ["V3"], [], [], [], [], [], [], [],
]

PARAM_ROWS = dict(mqk=0, mo=8, fq=12, fk=16, gm=20, gf=28, cw=36, cb=68, ng=76)
N_PARAM = 80


def build(nc, x, w_in, b_in, m_conv_w, m_conv_b, m_norm_g, w_bm, w_bf, w_o, ln1_g, ln1_b,
          w_router, b_router, w_gu, b_gu, w_dn, b_dn, ln2_g, ln2_b, out):
    with ExitStack() as ctx:
        def sb(name, shape, dt=F32):
            return ctx.enter_context(nc.sbuf_tensor(name, shape, dt))

        def sem(name):
            return ctx.enter_context(nc.semaphore(name))

        bank = [ctx.enter_context(nc.psum_tensor(f"bank{b}", [P, 512], F32)) for b in range(8)]

        with ExitStack() as early:
            early.enter_context(nc.sbuf_tensor("below_split", [P, 2 * THIRD], F32))
            split = early.enter_context(nc.sbuf_tensor("split", [P, THIRD], F32R))
        with ExitStack() as early:
            early.enter_context(nc.sbuf_tensor("below_heads", [P, THIRD - 4096], F32))
            heads_split = early.enter_context(nc.sbuf_tensor("heads_split", [P, 4096], F32R))
        ring = sb("ring", [P, 3 * THIRD])
        first = ring[:, 0:THIRD]
        arena = sb("arena", [P, ARENA])
        place, at = [first], [0]

        def parts(words, n, t):
            w = n * t
            return [words[:, k * w:(k + 1) * w].rearrange("p (b t) -> p b t", t=t) for k in range(2)]

        x_hi, x_lo = parts(split[:, 0:2 * KC * T], KC, T)
        y_hi, y_lo = x_hi, x_lo
        w_split = [split[:, 2 * KC * T + 2 * KC * P * k:2 * KC * T + 2 * KC * P * (k + 1)] for k in range(SPLITS)]
        wo_mid = sb("wo_mid", [P, 2 * D])
        hm_hi, hm_lo = parts(heads_split[:, 0:2048], 4, T)
        hf_hi, hf_lo = parts(heads_split[:, 2048:4096], 4, T)

        def region(n):
            o = THIRD + (n % RAW_REGIONS) * RWORDS
            return ring[:, o:o + RWORDS]

        def raw_pieces(k):
            if k < TAIL_AT:
                g, q = k // 4, k % 4
                w = region(g).rearrange("p (c n) -> p c n", n=512)
                return g, [w[:, 2 * q:2 * q + 2, :] if g in TOKEN_MAJOR else w[:, :, q * P:(q + 1) * P]]
            kind, f = TAIL[k - TAIL_AT][0], int(TAIL[k - TAIL_AT][1])
            if kind == "Y":
                n = W_B0 + f // 4
                return n, [region(n).rearrange("p (c n) -> p c n", n=512)[:, :, f % 4 * P:(f % 4 + 1) * P]]
            if f // 2 == 2:
                return WO_MID, [wo_mid[:, (f % 2) * D:(f % 2 + 1) * D]]
            n = W_O0 + f // 4
            return n, [region(n).rearrange("p (c n) -> p c n", n=D)[:, f % 4, :]]

        def split_pieces(k, part):
            w = w_split[k % SPLITS][:, part * KC * P:(part + 1) * KC * P]
            if k < TAIL_AT and k // 4 in TOKEN_MAJOR:
                return [w.rearrange("p (c n) -> p c n", n=512)]
            if k < TAIL_AT or TAIL[k - TAIL_AT][0] == "Y":
                return [w.rearrange("p (c n) -> p c n", n=P)]
            return [w]

        def slot(half, k):
            o = half % 3 * THIRD + k % HALF * SLOT_WORDS
            return ring[:, o:o + SLOT_WORDS]

        h = sb("h", [P, TT, D])
        bias3 = sb("bias3", [96, 3 * D], BF16)
        ident = sb("ident", [P, P])
        aident = sb("aident", [P, P])
        maskT = sb("maskT", [P, P], BF16)
        maskS = sb("maskS", [P, P], BF16)
        identb = sb("identb", [P, P], BF16)
        ones_b = sb("ones_b", [P, P], BF16)
        below = sb("below", [P, P], BF16)
        upto3 = sb("upto3", [32, 3, 32], BF16)
        start64 = sb("start64", [32, 32], BF16)
        param = sb("param", [P, N_PARAM])
        gbias = sb("gbias", [P, 1])
        wr = sb("wr", [P, KC, E])

        def take(words):
            at[0] += words
            return place[0][:, at[0] - words:at[0]]

        pt_words = take(6 * 512)
        PT = pt_words.rearrange("p (u n) -> p u n", n=512)
        bias_raw = pt_words[0:96, :]
        p_words = take(1024)
        pr = p_words.rearrange("p (b n) -> p b n", n=512)
        wg = p_words[:, 0:KC * 96].rearrange("p (c n) -> p c n", n=96)
        ones256 = p_words[0:64, KC * 96:KC * 96 + T]
        d_words = take(4 * 384)
        dec = d_words[:, 0:768].rearrange("p (b n) -> p b n", n=384)
        ptm = d_words[:, 768:1536].rearrange("p (b n) -> p b n", n=384)
        param_raw = d_words[0:N_PARAM, 0:P]
        tmp_rows = d_words[0:64, 512:512 + 4 * T].rearrange("p (k t) -> p k t", t=T)
        hml_words = take(1024)
        hml = hml_words.rearrange("p (a h d) -> p a h d", a=TT, h=M_HEADS)
        cv = hml_words[:, 0:512].rearrange("p (b t) -> p b t", t=T)
        sg_c = hml_words[:, 512:1024].rearrange("p (b t) -> p b t", t=T)
        rows_MF = take(2 * T)
        rowM, rowF = rows_MF[:, 0:T], rows_MF[:, T:2 * T]
        fqT = take(1024).rearrange("p (b t) -> p b t", t=T)
        hfT = fqT
        assert at[0] == 4 * SLOT_WORDS
        qk = take(2048).rearrange("p (b t) -> p b t", t=T)
        fkz = take(2048).rearrange("p (b t) -> p b t", t=T)
        assert at[0] == THIRD

        place[0], at[0] = arena, 0
        ln_g, ln_b = wo_mid[:, 0:D], wo_mid[:, D:2 * D]
        moe_at = at[0]
        gm = take(2048).rearrange("p (b t) -> p b t", t=T)
        gf = take(2048).rearrange("p (b t) -> p b t", t=T)
        mo = take(1024).rearrange("p (b t) -> p b t", t=T)
        hmT = mo
        hT = gf
        moe_end, route_at = at[0], at[0]
        vm = take(TT * M_HEADS * (M_D + 1)).rearrange("p (a h d) -> p a h d", a=TT, h=M_HEADS)
        fv = take(TT * 512).rearrange("p (a n) -> p a n", a=TT)
        sel = take(F_HEADS * P // 2).bitcast(BF16)[0:96, :].rearrange("p (h m) -> p h m", m=P)
        row3 = take(T).bitcast(BF16)[0:96, :]
        row3M, row3F = row3[:, 0:T], row3[:, T:2 * T]
        row_mid = take(T).bitcast(BF16)
        route_end = at[0]
        rowpack = take(T)
        upad = take(2 * (T + 4)).rearrange("p (b t) -> p b t", b=2)
        small = take(256)
        negmax = small[:, 0:32]
        rsum = small[:, 32:64]
        rrec = small[:, 64:96]
        msum = small[:, 96:128]
        hstat = small[:, 128:128 + 16]
        hrstd = small[:, 144:152]
        rden = small[:, 152:160]
        bn6 = small[:, 160:160 + 24]
        lstat = small[:, 184:184 + 4]
        lrstd = small[:, 188:190]
        colT = take(TT * 64).rearrange("p (a r) -> p a r", a=TT)
        em = take(8).rearrange("p (a h) -> p a h", a=TT)
        assert at[0] <= ARENA, at[0]

        at[0] = moe_at
        xgT = take(512).rearrange("p (c s) -> p c s", s=SLOTS)
        glu, sig, lin, half_act, act = (take(512) for _ in range(5))
        actT = take(512).rearrange("p (c s) -> p c s", s=P)
        ydn = take(512)
        pick = take(TT * SLOTS).rearrange("p (a s) -> p a s", a=TT)
        gated = take(TT * P).rearrange("p (a s) -> p a s", a=TT)
        gatedT = take(TT * P).rearrange("p (a t) -> p a t", a=TT)
        selb_w = take(SLOTS // 2)
        assert at[0] <= moe_end
        selb = selb_w.bitcast(BF16)[0:96, :]

        at[0] = route_at
        lg = take(TT * E).rearrange("p (a e) -> p a e", a=TT)
        br = take(E)
        top8 = take(TT * 8).rearrange("p (a k) -> p a k", a=TT)
        idx8 = take(TT * 8).rearrange("p (a k) -> p a k", a=TT)
        idxf = take(TT * 8).rearrange("p (a k) -> p a k", a=TT)
        ntop = take(2)
        gsum = take(2)
        mask = take(TT * E).rearrange("p (a e) -> p a e", a=TT)
        gexp = take(TT * E).rearrange("p (a e) -> p a e", a=TT)
        gpg = take(TT * 64).rearrange("p (a r) -> p a r", a=TT)
        gpgT = take(T).rearrange("p (a t) -> p a t", a=TT)[0:64]
        iota_e = take(E)
        iota_slot = take(SLOTS)
        iota_item = take(ITEMS)
        item_off = take(ITEMS)
        cnt = take(1)
        nb = take(1)
        st_col = take(1)
        start_sb = take(E)
        ownT = take(ITEMS)
        own = take(ITEMS)
        local = take(TT * ITEMS).rearrange("p (a i) -> p a i", a=TT)
        igate = take(TT * ITEMS).rearrange("p (a i) -> p a i", a=TT)
        slot1 = take(TT * E).rearrange("p (a e) -> p a e", a=TT)
        assert at[0] <= route_end, (at[0], route_end)
        mask3 = sb("mask3", [P, TT, 3, E], BF16)
        nbb = sb("nbb", [96, 1], BF16)
        nbB = sb("nbB", [32, P], BF16)
        table = upad.rearrange("p b t -> p (b t)")[0:1, :].bitcast(I32)
        items_end = table[:, 0:E + 1]
        last_item = table[:, E + 1:2 * E + 1]

        x_in = sem("x_in"); wg_in = sem("wg_in"); par_in = sem("par_in"); gb_in = sem("gb_in")
        bias_in = sem("bias_in"); vb_in = sem("vb_in"); wr_in = sem("wr_in"); br_in = sem("br_in")
        ln1_in = sem("ln1_in"); ln2_in = sem("ln2_in")
        blk_in = [sem(f"blk_in{n}") for n in range(16)]
        half_in = [sem(f"half_in{b}") for b in range(2)]
        hi_sb = sem("hi_sb"); lo_sb = sem("lo_sb"); unit_used = sem("unit_used")
        slot_in = [sem(f"slot_in{k}") for k in range(SLOTS_E)]
        out_done = sem("out_done")
        consts = sem("consts"); pool_chain = sem("pool_chain"); wg_zero = sem("wg_zero")
        bias3_done = sem("bias3_done"); iotas = sem("iotas")
        xT_ps = sem("xT_ps"); par_ps = sem("par_ps"); gate_ps = sem("gate_ps"); col_ps = sem("col_ps")
        S_ps = sem("S_ps"); T_ps = sem("T_ps"); V_ps = sem("V_ps")
        B_ps = sem("B_ps"); N_ps = sem("N_ps"); hm_ps = sem("hm_ps"); mix_ps = sem("mix_ps")
        hT_ps = sem("hT_ps"); lg_ps = sem("lg_ps"); cnt_ps = sem("cnt_ps"); end_ps = sem("end_ps")
        gpgT_ps = sem("gpgT_ps"); item_ps = sem("item_ps")
        released = sem("released")
        final_ps = sem("final_ps"); xg_ps = sem("xg_ps"); tr_ps = sem("tr_ps"); gates_ps = sem("gates_ps"); dn_ps = sem("dn_ps")
        x_hi_sb = sem("x_hi_sb"); x_lo_sb = sem("x_lo_sb"); xT_a = sem("xT_a"); hf_hi_sb = sem("hf_hi_sb")
        hf_lo_sb = sem("hf_lo_sb"); hm_hi_sb = sem("hm_hi_sb"); hm_lo_sb = sem("hm_lo_sb"); par_sb = sem("par_sb"); u_sb = sem("u_sb"); qk_sb = sem("qk_sb")
        proj_sb = sem("proj_sb"); logexp = sem("logexp"); z_sb = sem("z_sb"); rows_sb = sem("rows_sb")
        col_sb = sem("col_sb"); em_sb = sem("em_sb"); row3_sb = sem("row3_sb"); conv_sb = sem("conv_sb"); tap_sb = sem("tap_sb"); csig = sem("csig")
        max_sb = sem("max_sb"); exp_sb = sem("exp_sb"); prob_sb = sem("prob_sb"); PT_sb = sem("PT_sb")
        hf_sb = sem("hf_sb"); dec_sb = sem("dec_sb"); ptm_sb = sem("ptm_sb"); num_sb = sem("num_sb")
        hvar = sem("hvar"); heads_stat = sem("heads_stat"); hstd = sem("hstd"); hn_sb = sem("hn_sb"); gates_sig = sem("gates_sig"); hm_sb = sem("hm_sb")
        y_sb = sem("y_sb"); y_sum = sem("y_sum"); y_hi_sb = sem("y_hi_sb"); var1 = sem("var1"); std1 = sem("std1"); h1_sb = sem("h1_sb")
        hT_a = sem("hT_a"); lgmax = sem("lgmax"); gexp_sb = sem("gexp_sb")
        mask_sb = sem("mask_sb"); nb_sb = sem("nb_sb"); gpg_sb = sem("gpg_sb"); gpgT_sb = sem("gpgT_sb"); own_sb = sem("own_sb")
        tables = sem("tables")
        v_chain = sem("v_chain"); a_chain = sem("a_chain")
        pick_sb = sem("pick_sb"); gated_sb = sem("gated_sb"); selb_sb = sem("selb_sb")
        glu_sb = sem("glu_sb"); sig_sb = sem("sig_sb"); act_sb = sem("act_sb"); moe_v = sem("moe_v")
        xg_sb = sem("xg_sb"); actT_sb = sem("actT_sb"); gatedT_sb = sem("gatedT_sb"); ydn_sb = sem("ydn_sb")
        var2 = sem("var2"); std2 = sem("std2"); fin_sb = sem("fin_sb")

        def chunks(w):
            return w.rearrange("(c p) n -> p c n", p=P)

        def rows(v):
            return v.rearrange("(r p) -> r p", p=P)

        win = w_in[0]
        bin_ = b_in[0]

        block = ctx.enter_context(nc.Block())

        @block.sync
        def _(sp):
            for tt in range(TT):
                sp.dma_start(h[:, tt, :], x[0, tt * P:(tt + 1) * P, :]).then_inc(x_in, 16)

            def load_block(n):
                if n == WO_MID:
                    sp.dma_start(wo_mid[:, :].rearrange("p (c n) -> p c n", n=D), chunks(w_o[0][512:768, :])).then_inc(blk_in[n], 16)
                elif n == W_O1:
                    sp.dma_start(region(n).rearrange("p (c n) -> p c n", n=D)[:, 2:4, :],
                                 chunks(w_o[0][768:D, :])).then_inc(blk_in[n], 16)
                elif n == 0:
                    for b in range(2):
                        o = GROUPS[0] + 256 * b
                        sp.dma_start(region(n).rearrange("p (c n) -> p c n", n=512)[:, :, 256 * b:256 * b + 256],
                                     chunks(win[:, o:o + 256])).then_inc(half_in[b], 16)
                elif n < 11:
                    sp.dma_start(region(n).rearrange("p (c n) -> p c n", n=512),
                                 chunks(win[:, GROUPS[n]:GROUPS[n] + 512])).then_inc(blk_in[n], 16)
                elif n in (W_B0, W_B1):
                    for b, w in enumerate((w_bm, w_bf)):
                        sp.dma_start(region(n).rearrange("p (c n) -> p c n", n=512)[:, 4 * b:4 * b + 4, :],
                                     chunks(w[0][:, 512 * (n - W_B0):512 * (n - W_B0 + 1)])).then_inc(blk_in[n], 16)
                else:
                    sp.dma_start(region(n).rearrange("p (c n) -> p c n", n=D), chunks(w_o[0][0:512, :])).then_inc(blk_in[n], 16)

            load_block(0)
            sp.wait_ge(wg_zero, 1)
            for dst, src, n in ((0, MF, 4), (32, FF, 8), (64, MI, 4)):
                sp.dma_start(wg[:, :, dst:dst + n], chunks(win[:, src:src + n])).then_inc(wg_in, 16)
                sp.dma_start(gbias[dst:dst + n, :], bin_[src:src + n].rearrange("(p a) -> p a", a=1)).then_inc(gb_in, 16)
            for name, src in (("mqk", bin_[MQK:MQK + 1024]), ("mo", bin_[MO:MO + 512]), ("fq", bin_[FQ:FQ + 1024]),
                              ("gm", bin_[GM:GM + 2048]), ("cw", m_conv_w[0].rearrange("j n -> (j n)")),
                              ("cb", m_conv_b[0]), ("ng", m_norm_g[0])):
                r = PARAM_ROWS[name]
                src = rows(src)
                sp.dma_start(param_raw[r:r + src.shape[0], :], src).then_inc(par_in, 16)

            load_block(1)
            load_block(2)
            for g in range(3):
                sp.dma_start(bias_raw[32 * g:32 * g + 32, 0:2 * D], b_gu[0]).then_inc(bias_in, 16)
                sp.dma_start(bias_raw[32 * g:32 * g + 32, 2 * D:3 * D], b_dn[0]).then_inc(bias_in, 16)
            for tt in range(TT):
                sp.dma_start(vm[:, tt, :, 0:M_D], bin_[MV:MV + 512].rearrange("(a h d) -> a h d", a=1, h=M_HEADS)
                             .to_broadcast([P, M_HEADS, M_D])).then_inc(vb_in, 16)
                sp.dma_start(fv[:, tt, :], bin_[FV:FV + 512].rearrange("(a n) -> a n", a=1)
                             .to_broadcast([P, 512])).then_inc(vb_in, 16)
            sp.dma_start(wr[:, :, :], chunks(w_router[0])).then_inc(wr_in, 16)

            def load_when_split(n):
                sp.wait_ge(lo_sb, last_unit(n - RAW_REGIONS) + 1)
                load_block(n)

            load_block(WO_MID)
            for n in range(3, W_O1):
                load_when_split(n)
            sp.wait_ge(N_ps, M_HEADS)
            sp.wait_ge(V_ps, 4)
            sp.dma_start(br, b_router[0:1, :].to_broadcast([P, E])).then_inc(br_in, 16)
            def load_slot(k, e, half):
                dst = slot(half, k)
                if k < GU_SLOTS:
                    src = w_gu[0, e, k * P:(k + 1) * P, :] if isinstance(e, int) else \
                        w_gu[0][bass.ds(e, 1), k * P:(k + 1) * P, :].rearrange("a p n -> p (a n)")
                    sp.dma_start(dst, src).then_inc(slot_in[k], 16)
                else:
                    f0 = (k - GU_SLOTS) * 2 * P
                    src = chunks(w_dn[0, e, f0:f0 + 2 * P, :]) if isinstance(e, int) else \
                        w_dn[0][bass.ds(e, 1), f0:f0 + 2 * P, :].rearrange("a (c p) n -> p (a c) n", p=P)
                    sp.dma_start(dst.rearrange("p (c n) -> p c n", n=D), src).then_inc(slot_in[k], 16)

            sp.wait_ge(hm_ps, 2)
            sp.wait_ge(hf_lo_sb, 1)
            for k in range(4):
                load_slot(k, 0, 0)
            load_when_split(W_O1)
            load_slot(SLOTS_E - 2, 0, 1)
            sp.wait_ge(lo_sb, last_unit(W_B1) + 1)
            for k in range(HALF, HALF + 2):
                load_slot(k, 0, 1)
            sp.wait_ge(lo_sb, tail_unit("O5") + 1)
            sp.dma_start(ln_g, ln1_g[0:1, :].to_broadcast([P, D])).then_inc(ln1_in, 16)
            sp.dma_start(ln_b, ln1_b[0:1, :].to_broadcast([P, D])).then_inc(ln1_in, 16)
            for k in range(HALF + 2, HALF + 4):
                load_slot(k, 0, 1)
            sp.wait_ge(unit_used, tail_unit("Y7") + 1)
            for k in (4, 5):
                load_slot(k, 0, 0)
            sp.wait_ge(lo_sb, N_SPLIT)
            load_slot(SLOTS_E - 1, 0, 1)
            sp.wait_ge(mix_ps, 2 * TT)
            for k in range(HALF):
                sp.wait_ge(slot_in[k], 16)
                load_slot(k, 1, 2)
            sp.wait_ge(h1_sb, 2 * TT)
            sp.dma_start(ln_g, ln2_g[0:1, :].to_broadcast([P, D])).then_inc(ln2_in, 16)
            sp.dma_start(ln_b, ln2_b[0:1, :].to_broadcast([P, D])).then_inc(ln2_in, 16)
            sp.wait_ge(tables, 1)

            def load_half(e, loaded, first, half, e_last):
                last = sp.value_load(last_item[0:1, bass.ds(e_last, 1)], min_val=0, max_val=MAX_ITEMS - 1)
                for k in range(first, first + HALF):
                    sp.wait_ge(slot_in[k], loaded)
                for k in range(first, first + HALF):
                    sp.wait_ge(released, last * SLOTS_E + ((k + HALF) % SLOTS_E + 1))
                    load_slot(k, e, half)

            load_half(1, 16, HALF, 0, 0)
            with sp.Fori(0, (E - 2) // 3) as j:
                for step in range(3):
                    e = j * 3 + (2 + step)
                    load_half(e, j * 48 + 16 * (2 + step), 0, 2 * (2 + step), j * 3 + step)
                    load_half(e, j * 48 + 16 * (2 + step), HALF, 2 * (2 + step) + 1, j * 3 + (step + 1))
            for tt in range(TT):
                for j in range(2):
                    cols = slice(j * 512, (j + 1) * 512)
                    sp.wait_ge(fin_sb, 2 * tt + j + 1)
                    sp.dma_start(out[0, tt * P:(tt + 1) * P, cols], h[:, tt, cols]).then_inc(out_done, 16)
            sp.wait_ge(out_done, 16 * 2 * TT)

        @block.gpsimd
        def _(pool):
            count = [0]

            def link(ins):
                count[0] += 1
                ins.then_inc(pool_chain, 1)
                pool.wait_ge(pool_chain, count[0])

            pool.memset(gbias[:, :], 0.0)
            pool.memset(wg, 0.0).then_inc(wg_zero, 1)
            pool.memset(ident[:, :], 0.0)
            pool.memset(maskT[:, :], 0.0)
            pool.memset(maskS[:, :], 0.0)
            pool.memset(below[:, :], 1.0)
            pool.memset(upto3[:, :, :], 1.0)
            pool.memset(start64[:, :], float(SLOTS))
            link(pool.memset(sel, 0.0))
            pool.affine_select(out=ident[:, :], in_=ident[:, :], compare_op=ALU.not_equal, fill=1.0, base=0,
                               pattern=[[-1, P]], channel_multiplier=1).then_inc(consts, 1)
            pool.memset(ones_b[:, :], 1.0)
            pool.memset(ones256, 1.0)
            pool.affine_select(out=maskT[:, :], in_=maskT[:, :], compare_op=ALU.is_ge, fill=NEG, base=0,
                               pattern=[[1, P]], channel_multiplier=-1)
            link(pool.affine_select(out=maskS[:, :], in_=maskS[:, :], compare_op=ALU.is_ge, fill=NEG, base=0,
                                    pattern=[[-1, P]], channel_multiplier=1))
            for g in range(3):
                link(pool.affine_select(out=sel[32 * g:32 * g + 32, :, :], in_=sel[32 * g:32 * g + 32, :, :],
                                        compare_op=ALU.not_equal, fill=1.0, base=0,
                                        pattern=[[-1, F_HEADS], [0, P]], channel_multiplier=1))
            pool.affine_select(out=below[:, :], in_=below[:, :], compare_op=ALU.is_gt, fill=0.0, base=0,
                               pattern=[[1, P]], channel_multiplier=-1)
            pool.affine_select(out=upto3[:, :, :], in_=upto3[:, :, :], compare_op=ALU.is_ge, fill=0.0, base=0,
                               pattern=[[0, 3], [1, 32]], channel_multiplier=-1)
            pool.affine_select(out=start64[:, :], in_=start64[:, :], compare_op=ALU.is_gt, fill=0.0, base=0,
                               pattern=[[1, 32]], channel_multiplier=-1)
            pool.memset(rowpack, 0.0)
            pool.memset(rowM, 0.0)
            pool.memset(row3, 0.0)
            link(pool.memset(rowF, 0.0))
            pool.tensor_copy(identb[:, :], ident[:, :])
            pool.tensor_scalar(aident[:, :], ident[:, :], ALPHA, None, ALU.mult)
            pool.memset(fkz, 0.0)
            for b in range(2):
                pool.memset(upad[:, b, 0:4], 0.0)
            pool.memset(vm[:, :, :, M_D:M_D + 1], 1.0).then_inc(consts, 1)
            pool.wait_ge(consts, 2)
            pool.wait_ge(bias_in, 96)
            link(pool.tensor_copy(bias3[:, :], bias_raw))
            for first in (32, 64):
                for g in range(first, 96, 32):
                    rest = pool.tensor_tensor(bias_raw[g:g + 32, :], bias_raw[g:g + 32, :], bias3[g:g + 32, :], ALU.subtract)
                link(rest)
                for g in range(first, 96, 32):
                    last = pool.tensor_copy(bias3[g:g + 32, :], bias_raw[g:g + 32, :])
                if first == 32:
                    link(last)
            last.then_inc(bias3_done, 1)
            pool.wait_ge(N_ps, M_HEADS)
            pool.wait_ge(V_ps, 4)
            kw = dict(allow_small_or_imprecise_dtypes=True, channel_multiplier=0)
            pool.iota(iota_e, pattern=[[1, E]], base=0, **kw)
            pool.iota(iota_slot, pattern=[[1, SLOTS]], base=0, **kw)
            pool.iota(iota_item, pattern=[[1, ITEMS]], base=0, **kw)
            pool.iota(item_off, pattern=[[SLOTS, ITEMS]], base=1, **kw).then_inc(iotas, 1)

        @block.tensor
        def _(pe):
            def transposes(src, banks, done, idn=ident):
                for g in range(4):
                    for c in range(2):
                        for tt in range(TT):
                            last = pe.transpose(bank[banks[g]][:, (c * TT + tt) * P:(c * TT + tt + 1) * P],
                                                src[:, tt, (2 * g + c) * P:(2 * g + c + 1) * P], idn[:, :])
                    last.then_inc(done, 1)

            def keep_busy(n, b):
                for _ in range(n):
                    pe.matmul(bank[b][:, 0:P], identb[:, :], ones_b[:, :], start=True, stop=True)

            pe.wait_ge(consts, 1)
            pe.wait_ge(x_in, 16 * TT)
            transposes(h, [4, 5, 6, 7], xT_ps)

            def product(out, stationary, moving, start, stop):
                (s_hi, s_lo), (m_hi, m_lo) = stationary, moving
                pe.matmul(out, s_hi, m_hi, start=start, stop=False)
                pe.matmul(out, s_hi, m_lo, start=False, stop=False)
                return pe.matmul(out, s_lo, m_hi, start=False, stop=stop)

            state = {"unit": 0}

            def project(g, q):
                k = state["unit"]
                state["unit"] += 1
                pe.wait_ge(lo_sb, k + 1)
                w = [split_pieces(k, part)[0] for part in range(2)]
                if g in TOKEN_MAJOR:
                    if q == 0 and g > min(TOKEN_MAJOR):
                        pe.wait_ge(proj_sb, 2)
                    for tt in range(TT):
                        for c in range(2):
                            f = 2 * q + c
                            last = product(bank[6 + tt][:, :], [x[:, f, tt * P:(tt + 1) * P] for x in (x_hi, x_lo)],
                                           [p[:, c, :] for p in w], f == 0, f == KC - 1)
                else:
                    n = BLOCK_UNIT.index(k)
                    before = [m for m in range(n) if BLOCK_BANK[m] == BLOCK_BANK[n]]
                    if before and before[-1] < 8:
                        pe.wait_ge(u_sb, before[-1] + 1)
                    elif before:
                        pe.wait_ge(proj_sb, before[-1] - 7)
                    for c in range(KC):
                        if k == 0 and c % 2 == 0:
                            pe.wait_ge(x_lo_sb, c // 2 + 1)
                        last = product(bank[BLOCK_BANK[n]][:, 0:T], [p[:, c, :] for p in w],
                                       (x_hi[:, c, :], x_lo[:, c, :]), c == 0, c == KC - 1)
                last.then_inc(unit_used, 1)

            for _ in range(6):
                pe.matmul(bank[3][:, 0:P], ident[:, :], ident[:, :], start=True, stop=True)
            project(0, 0)
            pe.wait_ge(par_in, 16 * 7)
            pe.transpose(bank[3][:, 0:N_PARAM], param_raw, ident[0:N_PARAM, 0:N_PARAM]).then_inc(par_ps, 1)
            project(0, 1)
            pe.wait_ge(wg_in, 48)
            pe.wait_ge(xT_a, 4)
            for c in range(KC):
                last = pe.matmul(bank[2][0:96, 0:T], wg[:, c, :], hT[:, c, :], start=(c == 0), stop=(c == KC - 1))
            last.then_inc(gate_ps, 1)
            for k in range(2, 24):
                project(k // 4, k % 4)
                if k == 18:
                    pe.wait_ge(rows_sb, 1)
                    pe.wait_ge(par_sb, 1)
                    for tt in range(TT):
                        last = pe.transpose(bank[3][:, tt * P:(tt + 1) * P], rowpack[:, tt * P:(tt + 1) * P], ident[:, :])
                    last.then_inc(col_ps, 1)

            def scores(u):
                tt, heads = UNITS[u]
                if u == 0:
                    pe.wait_ge(proj_sb, 10)
                    pe.wait_ge(row3_sb, 1)
                    pe.wait_ge(consts, 2)
                    pe.wait_ge(col_sb, 1)
                if u >= 2:
                    pe.wait_ge(exp_sb, u - 1)
                n = (tt + 1) * P
                for j, hd in enumerate(heads):
                    o = bank[2 + u % 2][:, j * n:(j + 1) * n]
                    pe.matmul(o, fqT[:, hd // 2, tt * P:(tt + 1) * P], fkz[:, hd, 0:n], start=True, stop=False)
                    pe.matmul(o, sel[:, hd, :], row3F[:, 0:n], start=False, stop=False)
                    last = pe.matmul(o[:, n - P:n], identb[:, :], maskS[:, :], start=False, stop=True)
                last.then_inc(S_ps, 1)

            def turn(u):
                pe.wait_ge(prob_sb, u + 1)
                if u >= 2:
                    pe.wait_ge(PT_sb, u - 1)
                for j in range(4):
                    last = pe.transpose(bank[4 + u % 2][:, j * P:(j + 1) * P], pr[:, u % 2, j * P:(j + 1) * P], ident[:, :])
                last.then_inc(T_ps, 1)

            def values(pair):
                pe.wait_ge(PT_sb, 6)
                if pair >= 2:
                    pe.wait_ge(hf_sb, pair - 1)
                for j in range(2):
                    hd = 2 * pair + j
                    o = bank[6 + pair % 2][64 * j:64 * j + 64, :]
                    pe.matmul(o[:, 0:P], fv[:, 0, hd * F_D:(hd + 1) * F_D],
                              PT[:, 4 + pair // 2, (hd % 4) * P:(hd % 4 + 1) * P], start=True, stop=True)
                    for s in range(2):
                        last = pe.matmul(o[:, P:T], fv[:, s, hd * F_D:(hd + 1) * F_D],
                                         PT[:, pair, (2 * j + s) * P:(2 * j + s + 1) * P],
                                         start=(s == 0), stop=(s == 1))
                last.then_inc(V_ps, 1)

            def decay(hd):
                if hd == 0:
                    pe.wait_ge(exp_sb, 6)
                    pe.wait_ge(qk_sb, 8)
                else:
                    pe.wait_ge(dec_sb, 2 * hd)
                    pe.wait_ge(ptm_sb, hd)
                pe.matmul(bank[2][:, 0:T], sel[:, hd, :], row3M, start=True, stop=False)
                pe.matmul(bank[2][:, 0:P], identb[:, :], maskT[:, :], start=False, stop=True)
                pe.matmul(bank[2][:, T:T + P], sel[:, hd, :], row3M[:, P:T], start=True, stop=False)
                pe.matmul(bank[2][:, T:T + P], identb[:, :], maskT[:, :], start=False, stop=True)
                pe.matmul(bank[3][:, 0:T], qk[:, 4 + hd, 0:P], qk[:, hd, :], start=True, stop=True)
                pe.matmul(bank[3][:, T:T + P], qk[:, 4 + hd, P:T], qk[:, hd, P:T], start=True, stop=True).then_inc(B_ps, 1)

            def numerators(hd):
                pe.wait_ge(ptm_sb, hd + 1)
                if hd < 2:
                    pe.wait_ge(PT_sb, 5 + hd)
                if hd >= 2:
                    pe.wait_ge(num_sb, hd - 1)
                o = bank[4 + hd % 2]
                w = ptm[:, hd % 2, :]
                pe.matmul(o[:, 0:M_D + 1], w[:, 0:P], vm[:, 0, hd, :], start=True, stop=True)
                pe.matmul(o[:, T:T + M_D + 1], w[:, P:T], vm[:, 0, hd, :], start=True, stop=False)
                pe.matmul(o[:, T:T + M_D + 1], w[:, T:T + P], vm[:, 1, hd, :], start=False, stop=True).then_inc(N_ps, 1)

            kinds = {"S": scores, "T": turn, "V": values, "B": decay, "N": numerators}
            for k, steps in enumerate(STEPS):
                for s in steps:
                    kinds[s[0]](int(s[1]))
                if k == 16:
                    pe.wait_ge(hn_sb, 1)
                    for b in range(2):
                        for j in range(2):
                            for tt in range(TT):
                                last = pe.transpose(bank[2 + b][:, (j * TT + tt) * P:(j * TT + tt + 1) * P],
                                                    hml[:, tt, 2 * b + j, :], ident[:, :])
                        last.then_inc(hm_ps, 1)
                project(6 + k // 4, k % 4)

            def branches(f):
                k = tail_unit(f"Y{f}")
                if f == 0:
                    pe.wait_ge(hm_lo_sb, 2)
                    pe.wait_ge(hf_lo_sb, 1)
                    pe.wait_ge(num_sb, 4)
                if f >= 2:
                    pe.wait_ge(y_sb, f - 1)
                pe.wait_ge(lo_sb, k + 1)
                for b, (hi, lo) in enumerate(((hm_hi, hm_lo), (hf_hi, hf_lo))):
                    w = [split_pieces(k, part)[0][:, 4 * b:4 * b + 4, :] for part in range(2)]
                    for c in range(4):
                        last = product(bank[4 + 2 * b + f % 2][:, 0:T], [p[:, c, :] for p in w], (hi[:, c, :], lo[:, c, :]),
                                       c == 0, c == 3)
                last.then_inc(unit_used, 1)

            def mix(c, tt, j):
                w = [split_pieces(tail_unit(f"O{c}"), part)[0][:, j * 512:(j + 1) * 512] for part in range(2)]
                return product(bank[2 * tt + j][:, :], [y[:, c, tt * P:(tt + 1) * P] for y in (y_hi, y_lo)], w,
                               c == 0, c == KC - 1)

            def mix_both(c):
                if c == 0:
                    pe.wait_ge(proj_sb, 32)
                    pe.wait_ge(hm_sb, 2)
                pe.wait_ge(lo_sb, tail_unit(f"O{c}") + 1)
                pe.wait_ge(y_sb, c + 1)
                for tt in range(TT):
                    for j in range(2):
                        last = mix(c, tt, j)
                last.then_inc(unit_used, 1)

            for name in TAIL[:-SPLITS]:
                (branches if name[0] == "Y" else mix_both)(int(name[1]))
            for c in range(KC - SPLITS, KC):
                pe.wait_ge(lo_sb, tail_unit(f"O{c}") + 1)
                pe.wait_ge(y_sb, c + 1)
                for j in range(2):
                    last = mix(c, 0, j)
                    if c == KC - 1:
                        last.then_inc(mix_ps, 1)
            for j in range(2):
                for c in range(KC - SPLITS, KC):
                    last = mix(c, 1, j)
                last.then_inc(mix_ps, 1)

            pe.wait_ge(wr_in, 16)
            for tt in range(TT):
                for g in range(2):
                    pe.wait_ge(h1_sb, 2 * tt + g + 1)
                    for c in range(4):
                        f = 4 * g + c
                        last = pe.transpose(bank[4 + 2 * tt + g][:, c * P:(c + 1) * P], h[:, tt, f * P:(f + 1) * P], ident[:, :])
                    last.then_inc(hT_ps, 1)
                if tt == 1:
                    keep_busy(12, 3)
                for c in range(KC):
                    if c % 4 == 0:
                        pe.wait_ge(hT_a, 2 * tt + c // 4 + 1)
                    last = pe.matmul(bank[tt][:, 0:E], hT[:, c, tt * P:(tt + 1) * P], wr[:, c, :],
                                     start=(c == 0), stop=(c == KC - 1))
                last.then_inc(lg_ps, 1)
                if tt == 0:
                    keep_busy(60, 7)

            def open_sums(tt):
                for j in range(2):
                    pe.matmul(bank[4 + 2 * tt + j][:, :], aident[:, :], h[:, tt, j * 512:(j + 1) * 512],
                              start=True, stop=False, skip_group_check=True)

            open_sums(0)
            keep_busy(10, 2)
            for tt in range(TT):
                pe.wait_ge(mask_sb, tt + 1)
                pe.matmul(bank[3][0:96, 0:1], mask3[:, tt, :, :].rearrange("p g e -> p (g e)"), ones_b[:, 0:1],
                          start=(tt == 0), stop=(tt == TT - 1)).then_inc(cnt_ps, 1)
            pe.matmul(bank[2][:, 0:E], below[:, :], mask3[:, 0, 0, :], start=True, stop=True)
            pe.matmul(bank[2][:, E:2 * E], ones_b[:, :], mask3[:, 0, 0, :], start=True, stop=False)
            pe.matmul(bank[2][:, E:2 * E], below[:, :], mask3[:, 1, 0, :], start=False, stop=True).then_inc(cnt_ps, 1)
            open_sums(1)
            keep_busy(6, 0)
            pe.wait_ge(nb_sb, 1)
            pe.matmul(bank[1][0:96, 1:2], upto3[:, :, :].rearrange("p g e -> p (g e)"), nbb[0:32, :], start=True, stop=True)
            pe.matmul(bank[3][0:1, 0:E], nbb[0:32, :], upto3[:, 0, :], start=True, stop=True)
            pe.matmul(bank[0][:, 0:E], nbB[:, :], start64[:, :], start=True, stop=True).then_inc(end_ps, 1)
            keep_busy(6, 2)
            pe.wait_ge(gpg_sb, 1)
            for tt in range(TT):
                last = pe.transpose(bank[0][0:64, 64 + tt * P:64 + (tt + 1) * P], gpg[:, tt, :], ident[:, :])
            last.then_inc(gpgT_ps, 1)
            keep_busy(6, 2)
            pe.wait_ge(gpgT_sb, 1)
            pe.wait_ge(own_sb, 1)
            for tt in range(TT):
                pe.matmul(bank[1][:, tt * ITEMS:(tt + 1) * ITEMS], gpgT[0:32, tt, :], own[0:32, :], start=True, stop=True)
                last = pe.matmul(bank[2][:, tt * ITEMS:(tt + 1) * ITEMS], gpgT[32:64, tt, :], own[32:64, :],
                                 start=True, stop=True)
            last.then_inc(item_ps, 1)

            def gather(chunks=range(KC)):
                for c in chunks:
                    for tt in range(TT):
                        last = pe.matmul(bank[3][:, c * SLOTS:(c + 1) * SLOTS], h[:, tt, c * P:(c + 1) * P],
                                         pick[:, tt, :], start=(tt == 0), stop=(tt == TT - 1))
                if chunks[-1] == KC - 1:
                    last.then_inc(xg_ps, 1)

            def scatter(tile_done=None):
                for tt in range(TT):
                    for j in range(2):
                        last = pe.matmul(bank[4 + 2 * tt + j][:, :], gatedT[64 * j:64 * j + 64, tt, :],
                                         ydn[64 * j:64 * j + 64, :], start=False, stop=False, skip_group_check=True)
                    if tile_done is not None:
                        last.then_inc(tile_done, 1)

            pe.wait_ge(tables, 1)
            n = pe.value_load(items_end[0:1, E:E + 1], min_val=E, max_val=MAX_ITEMS)
            keep_busy(20, 3)
            pe.wait_ge(pick_sb, 1)
            gather()
            pe.wait_ge(xg_ps, 1)
            keep_busy(12, 0)

            def expert(e, third):
                begin, end = (pe.value_load(items_end[0:1, bass.ds(e + k, 1)], min_val=k, max_val=MAX_ITEMS) for k in range(2))
                with pe.Fori(begin, end) as i:
                    pe.wait_ge(xg_sb, i + 1)
                    pe.wait_ge(actT_sb, i + 1)
                    pe.wait_ge(gatedT_sb, i + 1)
                    for k in range(GU_SLOTS):
                        if k == GU_SLOTS // 2:
                            pe.wait_ge(ydn_sb, i + 1)
                            scatter()
                        pe.wait_ge(slot_in[k], e * 16 + 16)
                        for b in range(2):
                            for j in range(2):
                                o = D_FF * b + 512 * j
                                last = pe.matmul(bank[b][64 * j:64 * j + 64, :], xgT[:, k, :], slot(2 * third + k // HALF, k)[:, o:o + 512],
                                                 start=(k == 0), stop=(k == GU_SLOTS - 1))
                        last.then_inc(released, 1)
                        if k == GU_SLOTS - 2:
                            pe.wait_ge(selb_sb, i + 1)
                            for b in range(2):
                                for j in range(2):
                                    o = D_FF * b + 512 * j
                                    pe.matmul(bank[b][64 * j:64 * j + 64, :], selb, bias3[:, o:o + 512],
                                              start=False, stop=False)
                    pe.wait_ge(pick_sb, i + 2)
                    gather(range(GATHER_FIRST))
                    pe.wait_ge(act_sb, i + 1)
                    for q in range(4):
                        last = pe.transpose(bank[0][:, q * P:(q + 1) * P], act[:, q * P:(q + 1) * P], ident[:, :])
                    last.then_inc(tr_ps, 1)
                    gather(range(GATHER_FIRST, KC))
                    pe.wait_ge(gated_sb, i + 1)
                    for tt in range(TT):
                        last = pe.transpose(bank[1][:, tt * P:(tt + 1) * P], gated[:, tt, :], ident[:, :])
                    last.then_inc(gates_ps, 1)
                    for j in range(2):
                        o = 2 * D + 512 * j
                        pe.matmul(bank[2][64 * j:64 * j + 64, :], selb, bias3[:, o:o + 512], start=True, stop=False)
                    pe.wait_ge(actT_sb, i + 2)
                    for k in range(GU_SLOTS, SLOTS_E):
                        pe.wait_ge(slot_in[k], e * 16 + 16)
                        for c in range(2):
                            f = 2 * (k - GU_SLOTS) + c
                            for j in range(2):
                                last = pe.matmul(bank[2][64 * j:64 * j + 64, :],
                                                 actT[:, f % 4, 64 * (f // 4):64 * (f // 4) + 64],
                                                 slot(2 * third + k // HALF, k)[:, c * D + 512 * j:c * D + 512 * j + 512],
                                                 start=False, stop=(f == KC - 1))
                        last.then_inc(released, 1)

            with pe.Fori(0, E // 3) as t:
                for step in range(3):
                    expert(t * 3 + step, step)
            for e in range(E - E % 3, E):
                expert(e, e % 3)
            pe.wait_ge(ydn_sb, n + 1)
            scatter(final_ps)

        @block.scalar
        def _(sc):
            count = [0]

            def link(ins):
                count[0] += 1
                ins.then_inc(a_chain, 1)
                sc.wait_ge(a_chain, count[0])

            def split_high(k):
                n, pieces = raw_pieces(k)
                if n == 0:
                    sc.wait_ge(half_in[k // 2], 16)
                elif k == TAIL_AT or raw_pieces(k - 1)[0] != n:
                    sc.wait_ge(blk_in[n], 32 if n in (W_B0, W_B1) else 16)
                if k >= SPLITS:
                    sc.wait_ge(unit_used, k - SPLITS + 1)
                for src, dst in zip(pieces, split_pieces(k, 0)):
                    last = sc.copy(dst, src)
                last.then_inc(hi_sb, 1)

            for g in range(4):
                sc.wait_ge(xT_ps, g + 1)
                sc.copy(x_hi[:, 2 * g:2 * g + 2, :], bank[4 + g][:, :].rearrange("p (c t) -> p c t", t=T)).then_inc(x_hi_sb, 1)
                if g % 2:
                    split_high(g // 2)
            for g in range(4):
                sc.wait_ge(x_lo_sb, g + 1)
                sc.copy(hT[:, 2 * g:2 * g + 2, :], bank[4 + g][:, :].rearrange("p (c t) -> p c t", t=T)).then_inc(xT_a, 1)
            for k in range(2, SPLITS):
                split_high(k)

            def conv_sigmoid(b):
                sc.wait_ge(conv_sb, b + 1)
                if b >= 2:
                    sc.wait_ge(qk_sb, b - 1)
                sc.activation(sg_c[:, b % 2, :], cv[:, b % 2, :], ACT.Sigmoid).then_inc(csig, 1)

            for b in range(8):
                sc.wait_ge(unit_used, b + 1)
                if b == 0:
                    sc.wait_ge(par_sb, 1)
                    sc.wait_ge(consts, 2)
                if b >= 2:
                    sc.wait_ge(conv_sb, b - 1)
                sc.activation(upad[:, b % 2, 3:3 + T], bank[b % 2][:, 0:T], ACT.Identity,
                              bias=param[:, b:b + 1]).then_inc(u_sb, 1)
                if b >= 2:
                    sc.wait_ge(qk_sb, b - 1)
                cw, cb = PARAM_ROWS["cw"] + b, PARAM_ROWS["cb"] + b
                sc.wait_ge(u_sb, b + 1)
                sc.activation(cv[:, b % 2, :], upad[:, b % 2, 0:T], ACT.Identity, scale=param[:, cw:cw + 1],
                              bias=param[:, cb:cb + 1]).then_inc(tap_sb, 1)
                if b >= 1:
                    conv_sigmoid(b - 1)
                split_high(b + SPLITS)
            conv_sigmoid(7)
            for k in range(8, 24):
                split_high(k + SPLITS)
                if k == 9:
                    sc.wait_ge(z_sb, 1)
                    link(sc.activation(tmp_rows[:, 2, :], tmp_rows[:, 1, :], ACT.Exp))
                    sc.activation(tmp_rows[:, 1, :], tmp_rows[:, 2, :], ACT.Ln, bias=1.0).then_inc(logexp, 1)
                if k == 20:
                    sc.wait_ge(col_sb, 1)
                    sc.activation(em, colT[:, :, 32:36], ACT.Exp).then_inc(em_sb, 1)

            def softmax_exp(u):
                tt, heads = UNITS[u]
                n = (tt + 1) * P
                sc.wait_ge(max_sb, u + 1)
                if u >= 2:
                    sc.wait_ge(T_ps, u - 1)
                for j in range(len(heads)):
                    last = sc.activation(pr[:, u % 2, j * n:(j + 1) * n], bank[2 + u % 2][:, j * n:(j + 1) * n], ACT.Exp,
                                         bias=negmax[:, 4 * u + j:4 * u + j + 1],
                                         accum_out=rsum[:, 4 * u + j:4 * u + j + 1])
                last.then_inc(exp_sb, 1)

            def decay_exp(hd):
                sc.wait_ge(B_ps, hd + 1)
                if hd >= 2:
                    sc.wait_ge(ptm_sb, hd - 1)
                for s, (o, n) in enumerate(((0, T), (T, P))):
                    sc.activation(dec[:, hd % 2, o:o + n], bank[2][:, o:o + n], ACT.Exp,
                                  bias=colT[:, s, hd:hd + 1]).then_inc(dec_sb, 1)

            def open_gate(g, blocks):
                sc.wait_ge(proj_sb, blocks)
                sc.activation(g, g, ACT.Sigmoid).then_inc(gates_sig, 1)

            for k, steps in enumerate(STEPS):
                for s in steps:
                    if s[0] == "S":
                        softmax_exp(int(s[1]))
                    if s[0] == "B":
                        decay_exp(int(s[1]))
                if k == 12:
                    sc.wait_ge(hvar, 1)
                    sc.activation(hrstd, hrstd, ACT.Sqrt).then_inc(hstd, 1)
                if k == 17:
                    for b in range(2):
                        sc.wait_ge(hm_sb, b + 1)
                        sc.copy(hm_hi[:, 2 * b:2 * b + 2, :], hmT[:, 2 * b:2 * b + 2, :]).then_inc(hm_hi_sb, 1)
                split_high(24 + k + SPLITS)
                if k == 13:
                    sc.wait_ge(hf_sb, 4)
                    sc.copy(hf_hi, hfT).then_inc(hf_hi_sb, 1)
                    open_gate(mo, 16)
                if k == 14:
                    open_gate(gm[:, 0:4, :], 24)
                if k == 15:
                    open_gate(gm[:, 4:8, :], 24)
                if k == 17:
                    open_gate(gf[:, 0:4, :], 28)
            open_gate(gf[:, 4:8, :], 32)
            for t, name in enumerate(TAIL):
                if t + SPLITS < len(TAIL):
                    split_high(TAIL_AT + t + SPLITS)
                if name[0] == "Y":
                    f = int(name[1])
                    sc.wait_ge(y_sum, f + 1)
                    sc.copy(y_hi[:, f, :], gm[:, f, :]).then_inc(y_hi_sb, 1)
            def first_std(tt):
                sc.wait_ge(var1, tt + 1)
                sc.activation(lrstd[:, tt:tt + 1], lrstd[:, tt:tt + 1], ACT.Sqrt).then_inc(std1, 1)

            first_std(0)
            for tt in range(TT):
                for g in range(2):
                    sc.wait_ge(hT_ps, 2 * tt + g + 1)
                    sc.copy(hT[:, 4 * g:4 * g + 4, tt * P:(tt + 1) * P],
                            bank[4 + 2 * tt + g][:, :].rearrange("p (c t) -> p c t", t=P)).then_inc(hT_a, 1)
                if tt == 0:
                    first_std(1)
            for tt in range(TT):
                sc.wait_ge(lgmax, tt + 1)
                sc.activation(gexp[:, tt, :], lg[:, tt, :], ACT.Exp, bias=ntop[:, tt:tt + 1]).then_inc(gexp_sb, 1)

            sc.wait_ge(tables, 1)
            n = sc.value_load(items_end[0:1, E:E + 1], min_val=E, max_val=MAX_ITEMS)

            def take_tokens():
                sc.copy(xgT, bank[3][:, :].rearrange("p (c s) -> p c s", s=SLOTS)).then_inc(xg_sb, 1)

            sc.wait_ge(xg_ps, 1)
            take_tokens()
            with sc.Fori(0, n) as i:
                sc.wait_ge(glu_sb, i + 1)
                sc.activation(sig, glu, ACT.Sigmoid, scale=SW_ALPHA).then_inc(sig_sb, 1)
                sc.wait_ge(xg_ps, i + 2)
                take_tokens()
                sc.wait_ge(gates_ps, i + 1)
                sc.copy(gatedT, bank[1][:, 0:T].rearrange("p (a t) -> p a t", a=TT)).then_inc(gatedT_sb, 1)
                sc.wait_ge(released, i * SLOTS_E + SLOTS_E)
                sc.copy(ydn, bank[2][:, :]).then_inc(ydn_sb, 1)
            for tt in range(TT):
                sc.wait_ge(var2, tt + 1)
                sc.activation(lrstd[:, tt:tt + 1], lrstd[:, tt:tt + 1], ACT.Sqrt).then_inc(std2, 1)

        @block.vector
        def _(v):
            count = [0]

            def link(ins):
                count[0] += 1
                ins.then_inc(v_chain, 1)
                v.wait_ge(v_chain, count[0])

            def split_low(k):
                v.wait_ge(hi_sb, k + 1)
                for src, hi, lo in zip(raw_pieces(k)[1], split_pieces(k, 0), split_pieces(k, 1)):
                    last = v.tensor_tensor(lo, src, hi.bitcast(F32), ALU.subtract)
                last.then_inc(lo_sb, 1)

            for g in range(4):
                v.wait_ge(x_hi_sb, g + 1)
                v.tensor_tensor(x_lo[:, 2 * g:2 * g + 2, :], bank[4 + g][:, :].rearrange("p (c t) -> p c t", t=T),
                                x_hi[:, 2 * g:2 * g + 2, :].bitcast(F32), ALU.subtract).then_inc(x_lo_sb, 1)
                if g % 2:
                    split_low(g // 2)
            for k in range(2, SPLITS):
                split_low(k)
                if k == 2:
                    v.wait_ge(par_ps, 1)
                    v.tensor_copy(param[:, :], bank[3][:, 0:N_PARAM]).then_inc(par_sb, 1)

            z, ln1p, logf, gate_in = (tmp_rows[:, k, :] for k in range(4))

            def gate_inputs():
                v.wait_ge(gate_ps, 1)
                v.wait_ge(gb_in, 48)
                link(v.tensor_scalar(z, bank[2][0:64, 0:T], gbias[0:64, :], None, ALU.add))
                v.scalar_tensor_tensor(out=ln1p, in0=z, scalar=-1.0, in1=z, op0=ALU.mult, op1=ALU.min).then_inc(z_sb, 1)
                v.tensor_scalar(gate_in[0:4, :], bank[2][64:68, 0:T], gbias[64:68, :], None, ALU.add)

            def gate_rows(step):
                if step == 0:
                    v.wait_ge(logexp, 1)
                    link(v.scalar_tensor_tensor(out=logf, in0=z, scalar=0.0, in1=ln1p, op0=ALU.min, op1=ALU.subtract))
                    v.wait_ge(consts, 2)
                    link(v.tensor_tensor_scan(z, ones256, logf, 0.0, ALU.mult, ALU.add))
                else:
                    link(v.tensor_tensor(rowpack[0:4, :], gate_in[0:4, :], z[0:4, :], ALU.subtract))
                    link(v.tensor_tensor_scan(ln1p[0:4, :], rowpack[0:4, :], rowpack[0:4, :], 0.0, ALU.max, ALU.max))
                    v.tensor_scalar(rowM[0:4, :], ln1p[0:4, :], -1.0, None, ALU.mult)
                    v.scalar_tensor_tensor(out=rowpack[32:36, :], in0=z[0:4, :], scalar=-1.0, in1=ln1p[0:4, :],
                                           op0=ALU.mult, op1=ALU.subtract)
                    v.tensor_scalar(rowF[0:8, :], z[32:40, :], -1.0, None, ALU.mult).then_inc(rows_sb, 1)

            def row_parts(step):
                if step == 0:
                    v.wait_ge(rows_sb, 1)
                    link(v.tensor_copy(row3[0:8, :], rows_MF[0:8, :]))
                    link(v.tensor_tensor(rows_MF[0:8, :], rows_MF[0:8, :], row3[0:8, :], ALU.subtract))
                    link(v.tensor_copy(row_mid[0:8, :], rows_MF[0:8, :]))
                else:
                    v.tensor_copy(row3[32:40, :], row_mid[0:8, :])
                    link(v.tensor_tensor(rows_MF[0:8, :], rows_MF[0:8, :], row_mid[0:8, :], ALU.subtract))
                    v.tensor_copy(row3[64:72, :], rows_MF[0:8, :]).then_inc(row3_sb, 1)

            def conv(b):
                v.wait_ge(tap_sb, b + 1)
                cw = PARAM_ROWS["cw"]
                u, o = upad[:, b % 2, :], cv[:, b % 2, :]
                for j in range(1, CONV_W):
                    w = param[:, cw + 8 * j + b:cw + 8 * j + b + 1]
                    last = v.scalar_tensor_tensor(out=o, in0=u[:, j:j + T], scalar=w, in1=o, op0=ALU.mult, op1=ALU.add)
                    if j < CONV_W - 1:
                        link(last)
                last.then_inc(conv_sb, 1)

            def silu(b):
                v.wait_ge(csig, b + 1)
                v.scalar_tensor_tensor(out=qk[:, b, :], in0=cv[:, b % 2, :], scalar=1.0 if b < 4 else M_D ** -0.5,
                                       in1=sg_c[:, b % 2, :], op0=ALU.mult, op1=ALU.mult).then_inc(qk_sb, 1)

            for b in range(8):
                conv(b)
                if b >= 1:
                    silu(b - 1)
                split_low(b + SPLITS)
            silu(7)

            for k in range(8, 24):
                v.wait_ge(unit_used, k + 1)
                b = k % 4
                if k == 11:
                    v.wait_ge(vb_in, 64)
                    for tt in range(TT):
                        v.tensor_tensor(vm[:, tt, :, 0:M_D], bank[6 + tt][:, :].rearrange("p (h d) -> p h d", h=M_HEADS),
                                        vm[:, tt, :, 0:M_D], ALU.add).then_inc(proj_sb, 1)
                elif 12 <= k < 16:
                    v.tensor_scalar(fqT[:, b, :], bank[b % 2][:, 0:T], param[:, 12 + b:13 + b], F_D ** -0.5,
                                    ALU.add, ALU.mult).then_inc(proj_sb, 1)
                elif 16 <= k < 20:
                    for j in range(2):
                        r = slice(64 * j, 64 * j + 64)
                        last = v.tensor_scalar(fkz[r, 2 * b + j, :], bank[b % 2][r, 0:T], param[r, 16 + b:17 + b], None, ALU.add)
                    last.then_inc(proj_sb, 1)
                elif k == 23:
                    for tt in range(TT):
                        v.tensor_tensor(fv[:, tt, :], bank[6 + tt][:, :], fv[:, tt, :], ALU.add).then_inc(proj_sb, 1)
                split_low(k + SPLITS)
                if k == 8:
                    gate_inputs()
                if k in (10, 13):
                    gate_rows(k // 13)
                if k in (14, 15):
                    row_parts(k - 14)
                if k == 19:
                    v.wait_ge(col_ps, 1)
                    v.tensor_copy(colT, bank[3][:, 0:TT * P].rearrange("p (a r) -> p a r", a=TT)[:, :, 0:64]).then_inc(col_sb, 1)

            def row_max(u):
                tt, heads = UNITS[u]
                k = len(heads)
                v.wait_ge(S_ps, u + 1)
                link(v.tensor_reduce(negmax[:, 4 * u:4 * u + k],
                                     bank[2 + u % 2][:, :].rearrange("p (k n) -> p k n", k=k), AX.X, ALU.max))
                v.tensor_scalar(negmax[:, 4 * u:4 * u + k], negmax[:, 4 * u:4 * u + k], -1.0, None, ALU.mult).then_inc(max_sb, 1)

            def normalise(u):
                tt, heads = UNITS[u]
                k = len(heads)
                v.wait_ge(exp_sb, u + 1)
                r = rrec[:, 4 * u:4 * u + k]
                link(v.reciprocal(r, rsum[:, 4 * u:4 * u + k]))
                pp = pr[:, u % 2, :].rearrange("p (k n) -> p k n", k=k)
                v.tensor_tensor(pp, pp, r.unsqueeze(2).to_broadcast([P, k, 512 // k]), ALU.mult).then_inc(prob_sb, 1)

            def take_turned(u):
                v.wait_ge(T_ps, u + 1)
                if u == 0:
                    v.wait_ge(bias3_done, 1)
                v.tensor_copy(PT[:, u, :], bank[4 + u % 2][:, :]).then_inc(PT_sb, 1)

            def take_values(pair):
                v.wait_ge(V_ps, pair + 1)
                v.tensor_copy(hfT[:, pair, :], bank[6 + pair % 2][:, 0:T]).then_inc(hf_sb, 1)

            def weigh(hd):
                v.wait_ge(dec_sb, 2 * hd + 2)
                if hd >= 2:
                    v.wait_ge(N_ps, hd - 1)
                v.tensor_tensor(ptm[:, hd % 2, :], bank[3][:, 0:384], dec[:, hd % 2, :], ALU.mult).then_inc(ptm_sb, 1)

            def divide(hd):
                v.wait_ge(N_ps, hd + 1)
                if hd == 0:
                    v.wait_ge(em_sb, 1)
                o = bank[4 + hd % 2][:, :].rearrange("p (a n) -> p a n", a=TT)
                den = msum[:, 2 * hd:2 * hd + 2].unsqueeze(2)
                total = o[:, :, M_D:M_D + 1]
                link(v.scalar_tensor_tensor(out=den, in0=total, scalar=-1.0, in1=em[:, :, hd:hd + 1],
                                            op0=ALU.mult, op1=ALU.max))
                link(v.tensor_tensor(den, total, den, ALU.max))
                r = rden[:, 2 * hd:2 * hd + 2]
                link(v.reciprocal(r, msum[:, 2 * hd:2 * hd + 2]))
                for tt in range(TT):
                    last = v.tensor_scalar(hml[:, tt, hd, :], o[:, tt, 0:M_D], r[:, tt:tt + 1], None, ALU.mult)
                last.then_inc(num_sb, 1)
                v.wait_ge(num_sb, hd + 1)
                for tt in range(TT):
                    link(v.bn_stats(bn6[:, 6 * tt:6 * tt + 6], hml[:, tt, hd, :]))
                    k = 2 * (tt * M_HEADS + hd)
                    last = v.bn_aggr(hstat[:, k:k + 2], bn6[:, 6 * tt:6 * tt + 6])
                last.then_inc(heads_stat, 1)

            kinds = {"S": row_max, "T": take_turned, "V": take_values, "N": divide, "w": weigh}
            dest = [mo[:, b, :] for b in range(4)] + [gm[:, b, :] for b in range(8)] + [gf[:, b, :] for b in range(8)]
            pcol = [8 + b for b in range(4)] + [20 + b for b in range(8)] + [28 + b for b in range(8)]
            for k, steps in enumerate(V_STEPS):
                for s in steps:
                    kinds[s[0]](int(s[1]))
                if k == 11:
                    v.wait_ge(heads_stat, M_HEADS)
                    v.tensor_scalar(hrstd, hstat.rearrange("p (k s) -> p k s", s=2)[:, :, 1], LN_EPS, None, ALU.add).then_inc(hvar, 1)
                if k == 16:
                    v.wait_ge(gates_sig, 1)
                    for b in range(2):
                        v.wait_ge(hm_ps, b + 1)
                        for hd in (2 * b, 2 * b + 1):
                            ng = PARAM_ROWS["ng"] + hd
                            last = v.scalar_tensor_tensor(out=hmT[:, hd, :], in0=bank[2 + b][:, (hd % 2) * T:(hd % 2 + 1) * T],
                                                          scalar=param[:, ng:ng + 1], in1=mo[:, hd, :],
                                                          op0=ALU.mult, op1=ALU.mult)
                        last.then_inc(hm_sb, 1)
                if k == 18:
                    for b in range(2):
                        v.wait_ge(hm_hi_sb, b + 1)
                        v.tensor_tensor(hm_lo[:, 2 * b:2 * b + 2, :], hmT[:, 2 * b:2 * b + 2, :],
                                        hm_hi[:, 2 * b:2 * b + 2, :].bitcast(F32), ALU.subtract).then_inc(hm_lo_sb, 1)
                v.wait_ge(unit_used, 24 + k + 1)
                v.tensor_scalar(dest[k], bank[k % 2][:, 0:T], param[:, pcol[k]:pcol[k] + 1], None, ALU.add).then_inc(proj_sb, 1)
                if k < len(UNITS):
                    normalise(k)
                split_low(24 + k + SPLITS)
                if k == 13:
                    v.wait_ge(hstd, 1)
                    link(v.reciprocal(hrstd, hrstd))
                    for tt in range(TT):
                        for hd in range(M_HEADS):
                            j = tt * M_HEADS + hd
                            last = v.tensor_scalar(hml[:, tt, hd, :], hml[:, tt, hd, :], hstat[:, 2 * j:2 * j + 1],
                                                   hrstd[:, j:j + 1], ALU.subtract, ALU.mult)
                    last.then_inc(hn_sb, 1)
                if k == 15:
                    v.wait_ge(hf_hi_sb, 1)
                    v.tensor_tensor(hf_lo, hfT, hf_hi.bitcast(F32), ALU.subtract).then_inc(hf_lo_sb, 1)

            def merge(f):
                v.wait_ge(unit_used, tail_unit(f"Y{f}") + 1)
                v.wait_ge(gates_sig, 5 if f >= 4 else 4)
                v.tensor_tensor(gm[:, f, :], bank[4 + f % 2][:, 0:T], gm[:, f, :], ALU.mult)
                link(v.tensor_tensor(gf[:, f, :], bank[6 + f % 2][:, 0:T], gf[:, f, :], ALU.mult))
                v.tensor_tensor(gm[:, f, :], gm[:, f, :], gf[:, f, :], ALU.add).then_inc(y_sum, 1)

            def merge_low(f):
                v.wait_ge(y_hi_sb, f + 1)
                v.tensor_tensor(y_lo[:, f, :], gm[:, f, :], y_hi[:, f, :].bitcast(F32), ALU.subtract).then_inc(y_sb, 1)

            for t, name in enumerate(TAIL):
                if name[0] == "Y":
                    merge(int(name[1]))
                if t + SPLITS < len(TAIL):
                    split_low(TAIL_AT + t + SPLITS)
                if name[0] == "Y":
                    merge_low(int(name[1]))

            for tt in range(TT):
                for j in range(2):
                    v.wait_ge(mix_ps, 2 * tt + j + 1)
                    hs = h[:, tt, j * 512:(j + 1) * 512]
                    link(v.scalar_tensor_tensor(out=hs, in0=hs, scalar=ALPHA, in1=bank[2 * tt + j][:, :],
                                                op0=ALU.mult, op1=ALU.add))
                    link(v.bn_stats(bn6[:, 12 * tt + 6 * j:12 * tt + 6 * j + 6], hs))
                link(v.bn_aggr(lstat[:, 2 * tt:2 * tt + 2], bn6[:, 12 * tt:12 * tt + 12]))
                v.tensor_scalar(lrstd[:, tt:tt + 1], lstat[:, 2 * tt + 1:2 * tt + 2], LN_EPS, None, ALU.add).then_inc(var1, 1)
                if tt == 0:
                    v.wait_ge(ln1_in, 32)
                link(v.scalar_tensor_tensor(out=h[:, tt, :], in0=h[:, tt, :], scalar=lstat[:, 2 * tt:2 * tt + 1], in1=ln_g,
                                            op0=ALU.subtract, op1=ALU.mult))
                v.wait_ge(std1, tt + 1)
                link(v.reciprocal(lrstd[:, tt:tt + 1], lrstd[:, tt:tt + 1]))
                for j in range(2):
                    cols = slice(j * 512, (j + 1) * 512)
                    v.scalar_tensor_tensor(out=h[:, tt, cols], in0=h[:, tt, cols], scalar=lrstd[:, tt:tt + 1],
                                           in1=ln_b[:, cols], op0=ALU.mult, op1=ALU.add).then_inc(h1_sb, 1)

            v.wait_ge(br_in, 16)
            v.wait_ge(iotas, 1)
            for tt in range(TT):
                v.wait_ge(lg_ps, tt + 1)
                link(v.tensor_tensor(lg[:, tt, :], bank[tt][:, 0:E], br, ALU.add))
                link(v.max(top8[:, tt, :], lg[:, tt, :]))
                v.tensor_scalar(ntop[:, tt:tt + 1], top8[:, tt, 0:1], -1.0, None, ALU.mult).then_inc(lgmax, 1)
                link(v.max_index(idx8[:, tt, :].bitcast(U32), top8[:, tt, :], lg[:, tt, :]))
                link(v.tensor_copy(idxf[:, tt, :], idx8[:, tt, :].bitcast(U32)))
                link(v.tensor_scalar(mask[:, tt, :], iota_e, idxf[:, tt, 0:1], None, ALU.is_equal))
                for k in range(1, TOP_K):
                    link(v.scalar_tensor_tensor(out=mask[:, tt, :], in0=iota_e, scalar=idxf[:, tt, k:k + 1],
                                                in1=mask[:, tt, :], op0=ALU.is_equal, op1=ALU.add))
                v.tensor_copy(mask3[:, tt, :, :], mask[:, tt, :].unsqueeze(1).to_broadcast([P, 3, E])).then_inc(mask_sb, 1)
            v.wait_ge(gexp_sb, 2)
            link(v.tensor_tensor(gexp, gexp, mask, ALU.mult))
            link(v.tensor_reduce(gsum, gexp, AX.X, ALU.add))
            link(v.reciprocal(gsum, gsum))
            v.tensor_tensor(gpg[:, :, E:2 * E], gexp, gsum.unsqueeze(2).to_broadcast([P, TT, E]), ALU.mult)
            v.wait_ge(cnt_ps, 3)
            v.tensor_scalar(slot1, bank[2][:, 0:TT * E].rearrange("p (a e) -> p a e", a=TT), 1.0, None, ALU.add)
            tokens = bank[3][0:96, 0:1]
            link(v.tensor_scalar(nb[0:96, :], tokens, float(SLOTS), 1.0, ALU.is_gt, ALU.add))
            for k in range(2, T // SLOTS):
                link(v.scalar_tensor_tensor(out=nb[0:96, :], in0=tokens, scalar=float(k * SLOTS), in1=nb[0:96, :],
                                            op0=ALU.is_gt, op1=ALU.add))
            v.tensor_copy(nbb[:, :], nb[0:96, :])
            v.tensor_copy(nbB[:, :], nb[0:32, :].to_broadcast([32, P])).then_inc(nb_sb, 1)
            v.wait_ge(end_ps, 1)
            link(v.tensor_copy(start_sb, bank[0][:, 0:E]))
            link(v.tensor_tensor(slot1, slot1, start_sb.unsqueeze(1).to_broadcast([P, TT, E]), ALU.add))
            v.tensor_tensor(gpg[:, :, 0:E], slot1, mask, ALU.mult).then_inc(gpg_sb, 1)
            link(v.tensor_copy(cnt[0:96, :], bank[1][0:96, 1:2]))
            link(v.tensor_tensor(st_col[0:96, :], cnt[0:96, :], nb[0:96, :], ALU.subtract))
            link(v.tensor_scalar(ownT[0:96, :], iota_item[0:96, :], cnt[0:96, :], None, ALU.is_lt))
            v.scalar_tensor_tensor(out=own[0:96, :], in0=iota_item[0:96, :], scalar=st_col[0:96, :],
                                   in1=ownT[0:96, :], op0=ALU.is_ge, op1=ALU.mult).then_inc(own_sb, 1)
            v.memset(items_end[:, 0:1], 0)
            v.tensor_copy(items_end[:, 1:E + 1], bank[3][0:1, 0:E])
            v.tensor_scalar(last_item[:, :], bank[3][0:1, 0:E], -1.0, None, ALU.add).then_inc(tables, 1)
            v.wait_ge(gpgT_ps, 1)
            v.tensor_copy(gpgT, bank[0][0:64, 64:64 + T].rearrange("p (a t) -> p a t", a=TT)).then_inc(gpgT_sb, 1)
            v.wait_ge(item_ps, 1)
            link(v.tensor_tensor(local, bank[1][:, 0:TT * ITEMS].rearrange("p (a i) -> p a i", a=TT),
                                 item_off.unsqueeze(1).to_broadcast([P, TT, ITEMS]), ALU.subtract))

            def pick_tokens(i):
                for tt in range(TT):
                    last = v.tensor_scalar(pick[:, tt, :], iota_slot, local[:, tt, bass.ds(i, 1)], None, ALU.is_equal)
                last.then_inc(pick_sb, 1)

            def gate_tokens(i):
                for tt in range(TT):
                    for j in range(2):
                        last = v.tensor_scalar(gated[:, tt, 64 * j:64 * j + 64], iota_slot, local[:, tt, bass.ds(i, 1)],
                                               igate[:, tt, bass.ds(i, 1)], ALU.is_equal, ALU.mult)
                last.then_inc(gated_sb, 1)

            def select_bias(i):
                v.tensor_scalar(selb, ones_b[0:96, 0:SLOTS], own[0:96, bass.ds(i, 1)], None, ALU.mult).then_inc(selb_sb, 1)

            v.wait_ge(own_sb, 1)
            v.wait_ge(tables, 1)
            n = v.value_load(items_end[0:1, E:E + 1], min_val=E, max_val=MAX_ITEMS)
            pick_tokens(0)
            link(v.tensor_copy(igate, bank[2][:, 0:TT * ITEMS].rearrange("p (a i) -> p a i", a=TT)))
            gate_tokens(0)
            select_bias(0)
            v.memset(ydn, 0.0).then_inc(ydn_sb, 1)
            v.memset(gatedT, 0.0).then_inc(gatedT_sb, 1)
            v.memset(actT, 0.0).then_inc(actT_sb, 1)
            with v.Fori(0, n) as i:
                v.wait_ge(xg_ps, i + 1)
                pick_tokens(i + 1)
                v.wait_ge(released, i * SLOTS_E + GU_SLOTS)
                v.tensor_scalar(glu, bank[0][:, :], SW_LIMIT, None, ALU.min).then_inc(glu_sb, 1)
                v.tensor_scalar(lin, bank[1][:, :], SW_LIMIT, -SW_LIMIT, ALU.min, ALU.max).then_inc(moe_v, 1)
                v.wait_ge(moe_v, i * 2 + 1)
                v.scalar_tensor_tensor(out=half_act, in0=lin, scalar=1.0, in1=glu, op0=ALU.add, op1=ALU.mult).then_inc(moe_v, 1)
                v.wait_ge(moe_v, i * 2 + 2)
                v.wait_ge(sig_sb, i + 1)
                v.tensor_tensor(act, half_act, sig, ALU.mult).then_inc(act_sb, 1)
                v.wait_ge(tr_ps, i + 1)
                v.tensor_copy(actT, bank[0][:, :].rearrange("p (c s) -> p c s", s=P)).then_inc(actT_sb, 1)
                v.wait_ge(gates_ps, i + 1)
                gate_tokens(i + 1)
                v.wait_ge(released, i * SLOTS_E + SLOTS_E)
                select_bias(i + 1)

            def second_statistics(tt):
                v.wait_ge(final_ps, tt + 1)
                for j in range(2):
                    last = v.bn_stats(bn6[:, 12 * tt + 6 * j:12 * tt + 6 * j + 6], bank[4 + 2 * tt + j][:, :])
                link(last)
                link(v.bn_aggr(lstat[:, 2 * tt:2 * tt + 2], bn6[:, 12 * tt:12 * tt + 12]))
                v.tensor_scalar(lrstd[:, tt:tt + 1], lstat[:, 2 * tt + 1:2 * tt + 2], LN_EPS, None, ALU.add).then_inc(var2, 1)

            def second_norm(tt):
                for j in range(2):
                    cols = slice(j * 512, (j + 1) * 512)
                    last = v.scalar_tensor_tensor(out=h[:, tt, cols], in0=bank[4 + 2 * tt + j][:, :],
                                                  scalar=lstat[:, 2 * tt:2 * tt + 1], in1=ln_g[:, cols],
                                                  op0=ALU.subtract, op1=ALU.mult)
                link(last)
                v.wait_ge(std2, tt + 1)
                link(v.reciprocal(lrstd[:, tt:tt + 1], lrstd[:, tt:tt + 1]))
                for j in range(2):
                    cols = slice(j * 512, (j + 1) * 512)
                    v.scalar_tensor_tensor(out=h[:, tt, cols], in0=h[:, tt, cols], scalar=lrstd[:, tt:tt + 1],
                                           in1=ln_b[:, cols], op0=ALU.mult, op1=ALU.add).then_inc(fin_sb, 1)

            v.wait_ge(ln2_in, 32)
            for tt in range(TT):
                second_statistics(tt)
                second_norm(tt)


NAMES = ["x", "w_in", "b_in", "m_conv_w", "m_conv_b", "m_norm_g", "w_bm", "w_bf", "w_o", "ln1_g", "ln1_b",
         "w_router", "b_router", "w_gu", "b_gu", "w_dn", "b_dn", "ln2_g", "ln2_b"]


def kernel(**inputs):
    import concourse.bacc as bacc
    import numpy as np
    from concourse.bass_utils import run_bass_kernel_spmd

    nc = bacc.Bacc("TRN2", target_bir_lowering=False, num_devices=1)
    arrays, args = {}, {}
    for name in NAMES:
        a = np.ascontiguousarray(inputs[name])
        arrays[f"in_{name}"] = a
        args[name] = nc.dram_tensor(f"in_{name}", a.shape, mybir.dt.from_np(a.dtype), kind="ExternalInput").ap()
    out = nc.dram_tensor("out_h", (1, T, D), F32, kind="ExternalOutput").ap()
    build(nc, out=out, **args)
    r = run_bass_kernel_spmd(nc, [arrays], core_ids=[0])
    return r.results[0]["out_h"]
```
